# Optimizing a Trainium2 kernel written in Bass

```python
import jax, jax.numpy as jnp
from jax import lax
import numpy as np

D_MODEL = 1024
BATCH = 1
SEQ = 1024
DEPTH = 1
DEC_BATCH = 8
DEC_SEQ = 4
PAST_LEN = 2048
PAGE_SIZE = 128

D_MIX = D_MODEL
D_RNN = D_MIX // 2
D_ATTN = D_MIX - D_RNN
N_RNN_BLOCKS = 8
RNN_BLOCK = D_RNN // N_RNN_BLOCKS
CONV_WIDTH = 4
LRU_C = 8.0
N_HEADS = 8
HEAD_DIM = D_ATTN // N_HEADS
DILATED_PATTERNS = ((128, 1), (512, 4), (2048, 16))
CLASS_BLOCK = 128
MAX_WINDOW = max(w for w, _ in DILATED_PATTERNS)
D_IN = 2 * D_RNN + 3 * D_ATTN
N_KEYS = 128
N_EXPERTS = N_KEYS * N_KEYS
PEER_HEADS = 8
PEER_QDIM = 256
PEER_HALF = PEER_QDIM // 2
PEER_TOPK = 16
PEER_TOKEN_BLOCK = 256
EPS = 1e-6

kernel_name = 'hymba_rglru_dilated_peer_step'

def rmsnorm(x, g):
    xf = x.astype(jnp.float32)
    y = xf * lax.rsqrt(jnp.mean(xf * xf, axis=-1, keepdims=True) + EPS)
    return (y * g.astype(jnp.float32)).astype(x.dtype)

def causal_conv(xp, w, b):
    y = lax.conv_general_dilated(xp, w[:, None, :], window_strides=(1,), padding='VALID',
                                 dimension_numbers=('NWC', 'WIO', 'NWC'),
                                 feature_group_count=xp.shape[-1])
    return y + b

def rg_lru(x, w_a, b_a, w_x, b_x, lam, h0):
    B, T, _ = x.shape
    xb = x.reshape(B, T, N_RNN_BLOCKS, RNN_BLOCK)
    r = jax.nn.sigmoid((jnp.einsum('btnc,ncd->btnd', xb, w_a).reshape(B, T, D_RNN) + b_a).astype(jnp.float32))
    i = jax.nn.sigmoid((jnp.einsum('btnc,ncd->btnd', xb, w_x).reshape(B, T, D_RNN) + b_x).astype(jnp.float32))
    log_a = -LRU_C * r * jax.nn.softplus(-lam.astype(jnp.float32))
    a = jnp.exp(log_a)
    u = jnp.sqrt(-jnp.expm1(2.0 * log_a)) * (i * x.astype(jnp.float32))

    def step(h, au):
        h = au[0] * h + au[1]
        return h, h

    h_last, hs = lax.scan(step, h0.astype(jnp.float32), (jnp.swapaxes(a, 0, 1), jnp.swapaxes(u, 0, 1)))
    return jnp.swapaxes(hs, 0, 1).astype(x.dtype), h_last.astype(x.dtype)

def to_classes(t, dilation, s_pad):
    B, S, H, E = t.shape
    t = jnp.pad(t, ((0, 0), (0, s_pad - S), (0, 0), (0, 0)))
    t = jnp.swapaxes(t.reshape(B, s_pad // dilation, dilation, H, E), 1, 2)
    return t.reshape(B, dilation, s_pad // (dilation * CLASS_BLOCK), CLASS_BLOCK, H, E)

def from_classes(t, S):
    B, r, nb, qb = t.shape[:4]
    rest = t.shape[4:]
    t = jnp.swapaxes(t.reshape((B, r, nb * qb) + rest), 1, 2)
    return t.reshape((B, r * nb * qb) + rest)[:, :S]

def dilated_pattern_prompt(q, k, v, window, dilation):
    B, S, H, E = q.shape
    span = dilation * CLASS_BLOCK
    s_pad = -(-S // span) * span
    qc = to_classes(q, dilation, s_pad)
    kc = to_classes(k, dilation, s_pad)
    vc = to_classes(v, dilation, s_pad)
    nb = qc.shape[2]

    def with_prev(t):
        prev = jnp.pad(t, ((0, 0), (0, 0), (1, 0), (0, 0), (0, 0), (0, 0)))[:, :, :-1]
        return jnp.concatenate([prev, t], axis=3)

    kk, vv = with_prev(kc), with_prev(vc)
    logits = jnp.einsum('brnqhe,brnkhe->brnhqk', qc, kk) * (HEAD_DIM ** -0.5)
    qi = jnp.arange(CLASS_BLOCK)[:, None]
    ki = jnp.arange(2 * CLASS_BLOCK)[None, :]
    dist = qi + CLASS_BLOCK - ki
    blk = jnp.arange(nb)[:, None, None]
    valid = (dist >= 0) & (dist <= window // dilation) & ((ki >= CLASS_BLOCK) | (blk > 0))
    logits = jnp.where(valid[:, None], logits, -jnp.inf)
    m = jnp.max(logits, axis=-1)
    p = jnp.exp(logits - m[..., None])
    den = jnp.sum(p, axis=-1)
    num = jnp.einsum('brnhqk,brnkhe->brnqhe', p, vv)
    return (from_classes(jnp.swapaxes(m, 3, 4), S), from_classes(jnp.swapaxes(den, 3, 4), S),
            from_classes(num, S))

def dilated_pattern_sample(q, k_all, v_all, window, dilation, n_past):
    T = q.shape[1]
    idx = n_past + jnp.arange(T)[:, None] - dilation * jnp.arange(window // dilation + 1)[None, :]
    valid = idx >= 0
    idx = jnp.maximum(idx, 0)
    kg = jnp.take(k_all, idx, axis=1)
    vg = jnp.take(v_all, idx, axis=1)
    logits = jnp.einsum('bjhe,bjkhe->bjhk', q, kg) * (HEAD_DIM ** -0.5)
    logits = jnp.where(valid[None, :, None, :], logits, -jnp.inf)
    m = jnp.max(logits, axis=-1)
    p = jnp.exp(logits - m[..., None])
    den = jnp.sum(p, axis=-1)
    num = jnp.einsum('bjhk,bjkhe->bjhe', p, vg)
    return m, den, num

def mix_patterns(stats):
    m_all = stats[0][0]
    for s in stats[1:]:
        m_all = jnp.maximum(m_all, s[0])
    c0 = jnp.exp(stats[0][0] - m_all)
    den = c0 * stats[0][1]
    num = c0[..., None] * stats[0][2]
    for m, d, n in stats[1:]:
        c = jnp.exp(m - m_all)
        den = den + c * d
        num = num + c[..., None] * n
    return num / den[..., None]

def peer_block(xc, w_query, sub_keys, expert_u, expert_v):
    C = xc.shape[0]
    qh = (xc @ w_query).reshape(C, PEER_HEADS, 2, PEER_HALF)
    scores = jnp.einsum('chpe,hpne->chpn', qh, sub_keys).astype(jnp.float32)
    s, ix = lax.top_k(scores, PEER_TOPK)
    cand = (s[:, :, 0, :, None] + s[:, :, 1, None, :]).reshape(C, PEER_HEADS, PEER_TOPK * PEER_TOPK)
    cid = (ix[:, :, 0, :, None] * N_KEYS + ix[:, :, 1, None, :]).reshape(C, PEER_HEADS, PEER_TOPK * PEER_TOPK)
    top_s, pos = lax.top_k(cand, PEER_TOPK)
    eid = jnp.take_along_axis(cid, pos, axis=-1).reshape(C, PEER_HEADS * PEER_TOPK)
    g = jax.nn.softmax(top_s, axis=-1).reshape(C, PEER_HEADS * PEER_TOPK)
    u = expert_u[eid]
    act = jax.nn.gelu(jnp.einsum('cd,ced->ce', xc, u).astype(jnp.float32))
    return jnp.einsum('ce,ced->cd', (g * act).astype(xc.dtype), expert_v[eid])

def peer(x, w_query, sub_keys, expert_u, expert_v):
    B, T, D = x.shape
    flat = x.reshape(B * T, D)
    n = B * T
    n_pad = -(-n // PEER_TOKEN_BLOCK) * PEER_TOKEN_BLOCK
    flat = jnp.pad(flat, ((0, n_pad - n), (0, 0))).reshape(n_pad // PEER_TOKEN_BLOCK, PEER_TOKEN_BLOCK, D)
    out = lax.map(lambda xc: peer_block(xc, w_query, sub_keys, expert_u, expert_v), flat)
    return out.reshape(n_pad, D)[:n].reshape(B, T, D)

def layer(x, conv_prev, h_prev, k_past, v_past, g_mix, w_in, conv_w, conv_b, w_a, b_a, w_x, b_x,
          lru_lambda, g_rnn_out, g_attn_out, w_out, g_ffn, w_query, sub_keys, expert_u, expert_v):
    B, T, _ = x.shape
    xn = rmsnorm(x, g_mix)
    z = xn @ w_in
    xr, gate, q, k, v = jnp.split(z, [D_RNN, 2 * D_RNN, 2 * D_RNN + D_ATTN, 2 * D_RNN + 2 * D_ATTN], axis=-1)
    conv_in = jnp.concatenate([conv_prev, xr], axis=1)
    xc = causal_conv(conv_in, conv_w, conv_b)
    hs, h_last = rg_lru(xc, w_a, b_a, w_x, b_x, lru_lambda, h_prev)
    y_rnn = hs * jax.nn.gelu(gate)
    k_rows = k.reshape(B, T, N_HEADS, HEAD_DIM)
    v_rows = v.reshape(B, T, N_HEADS, HEAD_DIM)
    qf = q.reshape(B, T, N_HEADS, HEAD_DIM).astype(jnp.float32)
    kf = k_rows.astype(jnp.float32)
    vf = v_rows.astype(jnp.float32)
    if k_past is None:
        stats = [dilated_pattern_prompt(qf, kf, vf, w, d) for w, d in DILATED_PATTERNS]
        keep = min(MAX_WINDOW, T)
        k_rows, v_rows = k_rows[:, T - keep:], v_rows[:, T - keep:]
    else:
        k_all = jnp.concatenate([k_past.astype(jnp.float32), kf], axis=1)
        v_all = jnp.concatenate([v_past.astype(jnp.float32), vf], axis=1)
        stats = [dilated_pattern_sample(qf, k_all, v_all, w, d, k_past.shape[1]) for w, d in DILATED_PATTERNS]
    y_attn = mix_patterns(stats).reshape(B, T, D_ATTN).astype(x.dtype)
    merged = jnp.concatenate([rmsnorm(y_rnn, g_rnn_out), rmsnorm(y_attn, g_attn_out)], axis=-1) @ w_out
    x = x + merged
    x = x + peer(rmsnorm(x, g_ffn), w_query, sub_keys, expert_u, expert_v)
    return x, k_rows, v_rows, conv_in[:, -(CONV_WIDTH - 1):], h_last

def setup_inputs(seed: int = 0) -> dict:
    key = jax.random.key(seed)
    ks = jax.random.split(key, 24)
    f32 = jnp.float32

    def nrm(k, shape, scale):
        return jax.random.normal(k, shape, f32) * scale

    win_buf = min(MAX_WINDOW, PAST_LEN)
    a0 = jax.random.uniform(ks[10], (DEPTH, D_RNN), f32, 0.9, 0.999)
    return {
        'x_prompt': nrm(ks[0], (BATCH, SEQ, D_MODEL), 1.0),
        'x_sample': nrm(ks[1], (DEC_BATCH, DEC_SEQ, D_MODEL), 1.0),
        'cache_k': nrm(ks[2], (DEPTH, DEC_BATCH, win_buf, N_HEADS, HEAD_DIM), 1.0),
        'cache_v': nrm(ks[3], (DEPTH, DEC_BATCH, win_buf, N_HEADS, HEAD_DIM), 1.0),
        'state_conv': nrm(ks[4], (DEPTH, DEC_BATCH, CONV_WIDTH - 1, D_RNN), 1.0),
        'state_h': nrm(ks[5], (DEPTH, DEC_BATCH, D_RNN), 0.5),
        'g_mix': 1.0 + nrm(ks[6], (DEPTH, D_MODEL), 0.05),
        'w_in': nrm(ks[7], (DEPTH, D_MODEL, D_IN), D_MODEL ** -0.5),
        'conv_w': nrm(ks[8], (DEPTH, CONV_WIDTH, D_RNN), CONV_WIDTH ** -0.5),
        'conv_b': nrm(ks[9], (DEPTH, D_RNN), 0.02),
        'w_a': nrm(ks[11], (DEPTH, N_RNN_BLOCKS, RNN_BLOCK, RNN_BLOCK), RNN_BLOCK ** -0.5),
        'b_a': nrm(ks[12], (DEPTH, D_RNN), 0.02),
        'w_x': nrm(ks[13], (DEPTH, N_RNN_BLOCKS, RNN_BLOCK, RNN_BLOCK), RNN_BLOCK ** -0.5),
        'b_x': nrm(ks[14], (DEPTH, D_RNN), 0.02),
        'lru_lambda': jnp.log(a0) - jnp.log1p(-a0),
        'g_rnn_out': 1.0 + nrm(ks[15], (DEPTH, D_RNN), 0.05),
        'g_attn_out': 1.0 + nrm(ks[16], (DEPTH, D_ATTN), 0.05),
        'w_out': nrm(ks[17], (DEPTH, D_MIX, D_MODEL), D_MIX ** -0.5),
        'g_ffn': 1.0 + nrm(ks[18], (DEPTH, D_MODEL), 0.05),
        'w_query': nrm(ks[19], (DEPTH, D_MODEL, PEER_HEADS * PEER_QDIM), D_MODEL ** -0.5),
        'sub_keys': nrm(ks[20], (DEPTH, PEER_HEADS, 2, N_KEYS, PEER_HALF), PEER_HALF ** -0.5),
        'expert_u': nrm(ks[21], (DEPTH, N_EXPERTS, D_MODEL), D_MODEL ** -0.5),
        'expert_v': nrm(ks[22], (DEPTH, N_EXPERTS, D_MODEL), PEER_HEADS ** -0.5),
        'g_final': 1.0 + nrm(ks[23], (D_MODEL,), 0.05),
    }

def reference(x_prompt, x_sample, cache_k, cache_v, state_conv, state_h, g_mix, w_in, conv_w, conv_b,
              w_a, b_a, w_x, b_x, lru_lambda, g_rnn_out, g_attn_out, w_out, g_ffn, w_query, sub_keys,
              expert_u, expert_v, g_final):
    xp, xs = x_prompt, x_sample
    kp_l, vp_l, ks_l, vs_l, cp_l, cs_l, hp_l, hs_l = [], [], [], [], [], [], [], []
    for l in range(DEPTH):
        w = (g_mix[l], w_in[l], conv_w[l], conv_b[l], w_a[l], b_a[l], w_x[l], b_x[l], lru_lambda[l],
             g_rnn_out[l], g_attn_out[l], w_out[l], g_ffn[l], w_query[l], sub_keys[l], expert_u[l], expert_v[l])
        conv0 = jnp.zeros((xp.shape[0], CONV_WIDTH - 1, D_RNN), xp.dtype)
        h0 = jnp.zeros((xp.shape[0], D_RNN), xp.dtype)
        xp, kp, vp, cp, hp = layer(xp, conv0, h0, None, None, *w)
        xs, ksm, vsm, csm, hsm = layer(xs, state_conv[l], state_h[l], cache_k[l], cache_v[l], *w)
        kp_l.append(kp); vp_l.append(vp); cp_l.append(cp); hp_l.append(hp)
        ks_l.append(ksm); vs_l.append(vsm); cs_l.append(csm); hs_l.append(hsm)
    y_prompt = rmsnorm(xp, g_final)
    y_sample = rmsnorm(xs, g_final)
    return (y_prompt, y_sample, jnp.stack(kp_l), jnp.stack(vp_l), jnp.stack(ks_l), jnp.stack(vs_l),
            jnp.stack(cp_l), jnp.stack(cs_l), jnp.stack(hp_l), jnp.stack(hs_l))


_drawn_inputs = setup_inputs


def setup_inputs(seed=0):
    import zlib

    import numpy as np

    out = dict(_drawn_inputs(seed))
    spreads = {}
    factors = {'b_a': 6.64, 'b_x': 6.214}
    for name, (base, spread) in spreads.items():
        noise = np.random.default_rng([zlib.crc32(name.encode()), seed]).standard_normal(out[name].shape)
        drawn = base * np.exp(spread * noise) if base else spread * noise
        out[name] = __import__('jax').numpy.asarray(drawn.astype(out[name].dtype))
    for name, factor in factors.items():
        out[name] = (out[name] * factor).astype(out[name].dtype)
    return out
```

```python
from contextlib import ExitStack

import concourse.bass as bass
from concourse import mybir

F32, BF16, I32, U32 = mybir.dt.float32, mybir.dt.bfloat16, mybir.dt.int32, mybir.dt.uint32
ALU, ACT, AX = mybir.AluOpType, mybir.ActivationFunctionType, mybir.AxisListType
EPS = 1e-6
P = 128
HALF = 512
D = 1024
KC = D // P
DR = 512
CC = DR // P
SEQ, DB, DT = 1024, 8, 4
NS = DB * DT
NTOK = SEQ + NS
PT = SEQ // P
PAST = 2048
HEADS, HD = 8, 64
LRU_C = 8.0
CW = 4
NEG = -1e30
SCALE = HD ** -0.5
NARROW = [(0, HALF), (HALF, 2 * HALF)]
TILES = [(t, P) for t in range(PT)] + [(PT, NS)]

R_CONVW, R_CONVB, R_BA, R_BX, R_LAM, R_GRNN, R_GATT, R_GMIX, R_GFFN, R_SCONV = 0, 4, 5, 6, 7, 8, 9, 10, 12, 14
R_SH = R_SCONV + DB * (CW - 1)
N_ROWS = R_SH + DB


class Shop:

    def __init__(self, nc, ctx, stage):
        self.nc, self.ctx, self.stage, self.sems = nc, ctx, stage, []
        ctx.callback(self.close)

    def close(self):
        for held, sem in self.sems:
            self.nc.sync.sem_clear(sem)
        if self.sems:
            self.nc.all_engine_barrier()
        for held, sem in self.sems:
            held.__exit__(None, None, None)

    def sb(self, name, shape, dt=F32):
        return self.ctx.enter_context(self.nc.sbuf_tensor(name, shape, dt))

    def ps(self, name, shape):
        return self.ctx.enter_context(self.nc.psum_tensor(name, shape, F32))

    def sem(self, name):
        held = self.nc.semaphore(f"{self.stage}_{name}")
        self.sems.append((held, held.__enter__()))
        return self.sems[-1][1]


def cols(tile, rows=P):
    return bass.ds(tile * P, rows)


def constants(nc, a, c):
    with ExitStack() as ctx:
        s = Shop(nc, ctx, "constants")
        table = s.sb("table", [N_ROWS, DR])
        turned = s.ps("turned", [P, CC, 64])
        delta = s.sb("delta", [P, SEQ], I32)
        bits = s.sb("bits", [P, SEQ], I32)
        deltaf = s.sb("deltaf", [P, SEQ])
        term = s.sb("term", [P, SEQ])
        w1, w2, w3 = s.sb("w1", [P, CC]), s.sb("w2", [P, CC]), s.sb("w3", [P, CC])
        rows_landed, blocks_landed = s.sem("rows_landed"), s.sem("blocks_landed")
        zeroed, pool_step, turned_ready, params_ready = (
            s.sem("zeroed"), s.sem("pool_step"), s.sem("turned_ready"), s.sem("params_ready"))
        exp_done, step = s.sem("exp_done"), s.sem("step")
        iota_ready = s.sem("iota_ready")
        jrow = s.sb("jrow", [NS, 2], I32)
        jf = s.sb("jf", [NS, 1])
        sdel = s.sb("sdel", [NS, c.SK], I32)
        sbit = s.sb("sbit", [NS, c.SK], I32)
        sdelf = s.sb("sdelf", [NS, c.SK])
        sterm = s.sb("sterm", [NS, c.SK])
        ndel = s.sb("ndel", [NS, DB, NS], I32)
        nbit = s.sb("nbit", [NS, DB, NS], I32)
        ndelf = s.sb("ndelf", [NS, DB, NS])
        nterm = s.sb("nterm", [NS, DB, NS])
        block = ctx.enter_context(nc.Block())

        @block.sync
        def _(sp):
            rows = [(R_CONVW, a["conv_w"][0]), (R_CONVB, a["conv_b"]), (R_BA, a["b_a"]), (R_BX, a["b_x"]),
                    (R_LAM, a["lru_lambda"]), (R_GRNN, a["g_rnn_out"]), (R_GATT, a["g_attn_out"]),
                    (R_GMIX, a["g_mix"][0].rearrange("(r e) -> r e", e=DR)),
                    (R_GFFN, a["g_ffn"][0].rearrange("(r e) -> r e", e=DR)),
                    (R_SCONV, a["state_conv"][0].rearrange("b w e -> (b w) e")), (R_SH, a["state_h"][0])]
            for r, src in rows:
                sp.dma_start(table[r:r + src.shape[0], :], src).then_inc(rows_landed, 16)
            sp.wait_ge(zeroed, 1)
            for g, w in enumerate(("w_a", "w_x")):
                for half in range(2):
                    sp.dma_start(c.wgate[64 * half:64 * half + 64, g, :, 64 * half:64 * half + 64],
                                 a[w][0].rearrange("(t two) i o -> two i t o", two=2)[half]).then_inc(blocks_landed, 16)
            sp.wait_ge(blocks_landed, 64)

        @block.gpsimd
        def _(pool):
            nc.gpsimd.memset(c.wgate[:], 0.0).then_inc(zeroed, 1)
            nc.gpsimd.memset(c.ident[:], 0.0).then_inc(pool_step, 1)
            nc.gpsimd.memset(c.ones[:], 1.0).then_inc(pool_step, 1)
            pool.wait_ge(pool_step, 2)
            nc.gpsimd.affine_select(out=c.ident[:], in_=c.ident[:], compare_op=ALU.not_equal, fill=1.0, base=0,
                                    pattern=[[-1, P]], channel_multiplier=1).then_inc(pool_step, 1)
            nc.gpsimd.iota(delta[:], pattern=[[-1, SEQ]], base=SEQ - P, channel_multiplier=1).then_inc(iota_ready, 1)
            nc.gpsimd.iota(jrow[:, 0:1], pattern=[[0, 1]], base=0, channel_multiplier=1).then_inc(iota_ready, 1)
            nc.gpsimd.iota(sdel[:, 0:HALF], pattern=[[-1, 4], [-4, P]], base=HALF,
                           channel_multiplier=0).then_inc(iota_ready, 1)
            nc.gpsimd.iota(sdel[:, HALF:c.SK], pattern=[[-1, 4], [-16, c.OLD]], base=PAST,
                           channel_multiplier=0).then_inc(iota_ready, 1)
            nc.gpsimd.iota(ndel[:], pattern=[[4, DB], [-1, NS]], base=0, channel_multiplier=0).then_inc(iota_ready, 1)

        @block.tensor
        def _(pe):
            pe.wait_ge(rows_landed, 16 * 11)
            pe.wait_ge(pool_step, 3)
            for t in range(CC):
                last = nc.tensor.transpose(turned[:, t, 0:N_ROWS], table[:, t * P:(t + 1) * P], c.ident[0:N_ROWS, 0:N_ROWS])
            last.then_inc(turned_ready, 1)

        @block.scalar
        def _(act):
            act.wait_ge(params_ready, 1)
            act.wait_ge(step, 1)
            nc.scalar.activation(w2[:], w1[:], ACT.Exp, scale=-1.0).then_inc(exp_done, 1)

        @block.vector
        def _(dve):
            n = [0]

            def then(ins):
                n[0] += 1
                ins.then_inc(step, 1)
                dve.wait_ge(step, n[0])

            dve.wait_ge(turned_ready, 1)
            nc.vector.tensor_copy(c.par[:, :, 0:N_ROWS], turned[:, :, 0:N_ROWS]).then_inc(params_ready, 1)
            dve.wait_ge(params_ready, 1)
            lam = c.par[:, :, R_LAM]
            then(nc.vector.scalar_tensor_tensor(out=w1[:], in0=lam, scalar=-1.0, in1=lam, op0=ALU.mult, op1=ALU.max))
            dve.wait_ge(exp_done, 1)
            then(nc.vector.tensor_scalar(w3[:], w2[:], 2.0, None, ALU.add))
            then(nc.vector.reciprocal(w1[:], w3[:]))
            then(nc.vector.tensor_tensor(w2[:], w2[:], w1[:], ALU.mult))
            then(nc.vector.tensor_tensor(w3[:], w2[:], w2[:], ALU.mult))
            then(nc.vector.tensor_scalar(w1[:], w3[:], 1.0 / 17, 1.0 / 15, ALU.mult, ALU.add))
            for k in (13, 11, 9, 7, 5, 3, 1):
                then(nc.vector.tensor_tensor(w1[:], w1[:], w3[:], ALU.mult))
                then(nc.vector.tensor_scalar(w1[:], w1[:], 1.0 / k, None, ALU.add))
            then(nc.vector.tensor_tensor(w1[:], w1[:], w2[:], ALU.mult))
            then(nc.vector.tensor_scalar(w3[:], lam, -1.0, 0.0, ALU.mult, ALU.max))
            then(nc.vector.scalar_tensor_tensor(out=w3[:], in0=w1[:], scalar=2.0, in1=w3[:], op0=ALU.mult, op1=ALU.add))
            then(nc.vector.tensor_scalar(c.coef[:, 0, :], w3[:], -LRU_C, None, ALU.mult))
            then(nc.vector.tensor_scalar(c.coef[:, 1, :], w3[:], LRU_C, None, ALU.mult))
            for g, r in ((c.g_mix, R_GMIX), (c.g_ffn, R_GFFN)):
                then(nc.vector.tensor_copy(g[:].rearrange("p (r t) -> p r t", t=CC),
                                           c.par[:, :, r:r + 2].rearrange("p t r -> p r t")))

            dve.wait_ge(iota_ready, 5)

            def multiplicity(di, df, bi, tm, out):
                then(nc.vector.tensor_copy(df, di))
                then(nc.vector.tensor_scalar(out, df, 128.0, None, ALU.is_le))
                for dil, win in ((4, 512.0), (16, 2048.0)):
                    then(nc.vector.tensor_single_scalar(bi, di, dil - 1, ALU.bitwise_and))
                    then(nc.vector.tensor_copy(tm, bi))
                    then(nc.vector.tensor_single_scalar(tm, tm, 0.0, ALU.is_equal))
                    then(nc.vector.scalar_tensor_tensor(out=tm, in0=df, scalar=win, in1=tm, op0=ALU.is_le, op1=ALU.mult))
                    then(nc.vector.tensor_tensor(out, out, tm, ALU.add))
                then(nc.vector.scalar_tensor_tensor(out=out, in0=df, scalar=0.0, in1=out, op0=ALU.is_ge, op1=ALU.mult))

            def bias_of(bias, mult):
                then(nc.vector.tensor_scalar(bias, mult, 0.0, NEG, ALU.is_equal, ALU.mult))

            multiplicity(delta[:], deltaf[:], bits[:], term[:], c.mult[:])
            bias_of(c.bias[:], c.mult[:])
            then(nc.vector.tensor_single_scalar(jrow[:, 1:2], jrow[:, 0:1], DT - 1, ALU.bitwise_and))
            then(nc.vector.tensor_copy(jf[:], jrow[:, 1:2]))
            for di, df, bi, tm, out in ((sdel[:], sdelf[:], sbit[:], sterm[:], c.s_mult[:, 0, 0:c.SK]),
                                        (ndel[:], ndelf[:], nbit[:], nterm[:], c.n_mult[:])):
                then(nc.vector.tensor_copy(df, di))
                then(nc.vector.tensor_scalar(df, df, jf[:, 0:1], None, ALU.add))
                then(nc.vector.tensor_copy(di, df))
                multiplicity(di, df, bi, tm, out)
            then(nc.vector.tensor_scalar(nterm[:], ndelf[:], jf[:, 0:1], None, ALU.is_le))
            then(nc.vector.tensor_tensor(c.n_mult[:], c.n_mult[:], nterm[:], ALU.mult))
            bias_of(c.s_bias[:, 0, 0:c.SK], c.s_mult[:, 0, 0:c.SK])
            for x in (c.s_bias, c.s_mult):
                then(nc.vector.tensor_copy(x[:, 1, 0:c.SK], x[:, 0, 0:c.SK]))
            bias_of(c.n_bias[:], c.n_mult[:])


def normed_T(nc, a, c, xnT):
    with ExitStack() as ctx:
        s = Shop(nc, ctx, "normed_T")
        x_in = s.sb("x_in", [P, 2, D])
        xn = s.sb("xn", [P, 2, D])
        squares = s.sb("squares", [P, D])
        stat = s.sb("stat", [P, 2, 4])
        tp = [s.ps(f"tp{i}", [P, KC, P]) for i in range(2)]
        x_landed = [s.sem(f"x_landed{i}") for i in range(2)]
        x_used, xn_used, tp_used = s.sem("x_used"), s.sem("xn_used"), s.sem("tp_used")
        sq_done, ms_ready, rt_done, rinv_ready = s.sem("sq_done"), s.sem("ms_ready"), s.sem("rt_done"), s.sem("rinv_ready")
        block = ctx.enter_context(nc.Block())
        LOOPS = PT // 2

        @block.sync
        def _(sp):
            sp.sem_inc(x_used, 2)

            def load(t, par, src, rows=P):
                sp.wait_ge(x_used, t + 1)
                sp.dma_start(x_in[0:rows, par, :], src).then_inc(x_landed[par], 16)

            with sp.Fori(0, LOOPS) as i:
                for par in range(2):
                    load(2 * i + par, par, a["x_prompt"][0, cols(2 * i + par), :])
            load(PT, 0, a["x_sample"].rearrange("b t d -> (b t) d"), NS)

        @block.scalar
        def _(act):
            def norm(t, par, loads, rows=P):
                act.wait_ge(x_landed[par], 16 * loads)
                nc.scalar.activation(squares[0:rows, :], x_in[0:rows, par, :], ACT.Square,
                                     accum_out=stat[0:rows, par, 0:1]).then_inc(sq_done, 1)
                act.wait_ge(ms_ready, t + 1)
                nc.scalar.activation(stat[0:rows, par, 2:3], stat[0:rows, par, 1:2], ACT.Sqrt).then_inc(rt_done, 1)
                act.wait_ge(rinv_ready, t + 1)
                act.wait_ge(xn_used, t + 1)
                nc.scalar.activation(xn[0:rows, par, :], x_in[0:rows, par, :], ACT.Copy,
                                     scale=stat[0:rows, par, 3:4]).then_inc(x_used, 1)
                act.wait_ge(x_used, t + 3)

            with act.Fori(0, LOOPS) as i:
                for par in range(2):
                    norm(2 * i + par, par, i + 1)
            norm(PT, 0, LOOPS + 1, NS)

        @block.tensor
        def _(pe):
            pe.sem_inc(xn_used, 2)

            def turn(t, par, rows=P):
                pe.wait_ge(x_used, t + 3)
                pe.wait_ge(tp_used, t + 1)
                for k in range(KC):
                    last = nc.tensor.transpose(tp[par][:, k, 0:rows], xn[0:rows, par, k * P:(k + 1) * P],
                                               c.ident[0:rows, 0:rows])
                last.then_inc(xn_used, 1)

            with pe.Fori(0, LOOPS) as i:
                for par in range(2):
                    turn(2 * i + par, par)
            turn(PT, 0, NS)

        @block.vector
        def _(dve):
            dve.sem_inc(tp_used, 2)

            def serve(t, par, rows=P):
                dve.wait_ge(sq_done, t + 1)
                nc.vector.tensor_scalar(stat[0:rows, par, 1:2], stat[0:rows, par, 0:1], 1.0 / D, EPS,
                                        ALU.mult, ALU.add).then_inc(ms_ready, 1)
                dve.wait_ge(rt_done, t + 1)
                nc.vector.reciprocal(stat[0:rows, par, 3:4], stat[0:rows, par, 2:3]).then_inc(rinv_ready, 1)
                dve.wait_ge(xn_used, t + 3)
                nc.vector.tensor_tensor(xnT[:, :, cols(t, rows)], tp[par][:, :, 0:rows],
                                        c.g_mix[:].unsqueeze(2).to_broadcast((P, KC, rows)),
                                        ALU.mult).then_inc(tp_used, 1)

            with dve.Fori(0, LOOPS) as i:
                for par in range(2):
                    serve(2 * i + par, par)
            serve(PT, 0, NS)


def project(nc, a, c, xnT, zT, v_tok):
    w_view = a["w_in"][0].rearrange("(k p) n -> p k n", p=P)
    with ExitStack() as ctx:
        s = Shop(nc, ctx, "project")
        w = s.sb("w", [P, 2, KC, P])
        wv = s.sb("wv", [P, KC, DR])
        k_tok = s.sb("k_tok", [P, 2, DR])
        xc, gr, gi, th = s.sb("xc", [P, NTOK]), s.sb("gr", [P, NTOK]), s.sb("gi", [P, NTOK]), s.sb("th", [P, NTOK])
        hist = s.sb("hist", [P, DB, CW - 1 + DT])
        last_in = s.sb("last_in", [P, CC, 36])
        last_rows = s.sb("last_rows", [36, DR])
        zp = [s.ps(f"zp{i}", [P, SEQ]) for i in range(2)]
        zs = [s.ps(f"zs{i}", [P, HALF]) for i in range(2)]
        gp = [s.ps(f"gp{i}", [P, HALF]) for i in range(2)]
        lp = gp[0][0:36, :]
        w_landed = [s.sem(f"w_landed{i}") for i in range(2)]
        wv_landed = s.sem("wv_landed")
        w_used, z_free, z_ready = s.sem("w_used"), s.sem("z_free"), s.sem("z_ready")
        tok_ready, v_done, k_done, v_landed = s.sem("tok_ready"), s.sem("v_done"), s.sem("k_done"), s.sem("v_landed")
        k_landed = [s.sem(f"k_landed{i}") for i in range(2)]
        xc_ready, gates_done, gp_free = s.sem("xc_ready"), s.sem("gates_done"), s.sem("gp_free")
        a_done, gx_ready, sq_done, gelu_done, c_done = (
            s.sem("a_done"), s.sem("gx_ready"), s.sem("sq_done"), s.sem("gelu_done"), s.sem("c_done"))
        step, lp_ready, last_ready, last_landed = s.sem("step"), s.sem("lp_ready"), s.sem("last_ready"), s.sem("last_landed")
        NZ = 4 * CC
        block = ctx.enter_context(nc.Block())

        @block.sync
        def _(sp):
            sp.sem_inc(w_used, 2)
            with sp.Fori(0, NZ // 2) as i:
                for par in range(2):
                    sp.wait_ge(w_used, 2 * i + par + 1)
                    sp.dma_start(w[:, par], w_view[:, :, bass.ds((2 * i + par) * P, P)]).then_inc(w_landed[par], 16)
            sp.dma_start(wv[:], w_view[:, :, NZ * P:]).then_inc(wv_landed, 16)
            for t, rows in TILES:
                sp.wait_ge(k_done, t + 3)
                dst = a["k_prompt"][t * P:(t + 1) * P, :] if t < PT else a["k_sample"]
                sp.dma_start(dst, k_tok[0:rows, t % 2, :]).then_inc(k_landed[t % 2], 16)
            sp.wait_ge(v_done, len(TILES) + 2)
            sp.dma_start(a["v_prompt"].rearrange("(t p) e -> p t e", p=P), v_tok[:, 0:PT, :]).then_inc(v_landed, 16)
            sp.dma_start(a["v_sample"], v_tok[0:NS, PT, :]).then_inc(v_landed, 16)
            sp.wait_ge(last_ready, 1)
            n = DB * (CW - 1)
            sp.dma_start(a["conv_sample"], last_rows[0:n, :]).then_inc(last_landed, 16)
            sp.dma_start(a["conv_prompt"], last_rows[n:n + 3, :]).then_inc(last_landed, 16)
            sp.dma_start(a["h_prompt"], last_rows[n + 3:n + 4, :]).then_inc(last_landed, 16)
            sp.dma_start(a["h_sample"], last_rows[n + 4:n + 12, :]).then_inc(last_landed, 16)
            sp.wait_ge(last_landed, 64)
            sp.wait_ge(v_landed, 32)
            for par in range(2):
                sp.wait_ge(k_landed[par], 16 * len(TILES[par::2]))

        @block.tensor
        def _(pe):
            pe.sem_inc(gp_free, 2)

            def tile(n, par, loads):
                pe.wait_ge(w_landed[par], 16 * loads)
                pe.wait_ge(z_free, n + 1)
                for k in range(KC):
                    for lo, hi in NARROW:
                        nc.tensor.matmul(zp[par][:, lo:hi], w[:, par, k, :], xnT[:, k, lo:hi],
                                         start=(k == 0), stop=(k == KC - 1))
                    last = nc.tensor.matmul(zs[par][:, 0:NS], w[:, par, k, :], xnT[:, k, SEQ:NTOK],
                                            start=(k == 0), stop=(k == KC - 1))
                last.then_inc(w_used, 1)

            def gates(t):
                pe.wait_ge(xc_ready, t + 1)
                n = 0
                for g in range(2):
                    for lo, hi in NARROW + [(SEQ, NTOK)]:
                        pe.wait_ge(gp_free, 6 * t + n + 1)
                        nc.tensor.matmul(gp[n % 2][:, 0:hi - lo], c.wgate[:, g, t, :], xc[:, lo:hi],
                                         start=True, stop=True).then_inc(z_ready, 1)
                        n += 1

            with pe.Fori(0, CC // 2) as i:
                for par in range(2):
                    tile(2 * i + par, par, i + 1)
            for t in range(CC):
                tile(CC + t, t % 2, CC // 2 + t // 2 + 1)
                gates(t)
            with pe.Fori(CC, NZ // 2) as i:
                for par in range(2):
                    tile(2 * i + par, par, i + 1)
            pe.wait_ge(wv_landed, 16)
            pe.wait_ge(z_free, NZ + 2)
            for t, rows in TILES:
                pe.wait_ge(v_done, t + 1)
                pe.wait_ge(k_done, t + 1)
                for k in range(KC):
                    last = nc.tensor.matmul(zp[t % 2][0:rows, 0:DR], xnT[:, k, t * P:t * P + rows], wv[:, k, :],
                                            start=(k == 0), stop=(k == KC - 1))
                for j in range(CC):
                    last = nc.tensor.transpose(zp[t % 2][0:rows, DR + j * P:DR + (j + 1) * P],
                                               zT[:, 3 * CC + j, t * P:t * P + rows], c.ident[:])
                last.then_inc(tok_ready, 1)
            pe.wait_ge(c_done, CC)
            for j in range(CC):
                last = nc.tensor.transpose(lp[:, j * P:(j + 1) * P], last_in[:, j, :], c.ident[:])
            last.then_inc(lp_ready, 1)

        @block.scalar
        def _(act):
            act.sem_inc(z_free, 2)
            act.sem_inc(v_done, 2)

            def keep(n, par):
                act.wait_ge(w_used, n + 3)
                nc.scalar.activation(zT[:, n, 0:SEQ], zp[par][:], ACT.Copy)
                nc.scalar.activation(zT[:, n, SEQ:NTOK], zs[par][:, 0:NS], ACT.Copy).then_inc(z_free, 1)

            def keep_at(i, par):
                n = 2 * i + par
                act.wait_ge(w_used, n + 3)
                nc.scalar.activation(zT[:, bass.ds(n, 1), 0:SEQ].rearrange("p a n -> p (a n)"), zp[par][:],
                                     ACT.Copy)
                nc.scalar.activation(zT[:, bass.ds(n, 1), SEQ:NTOK].rearrange("p a n -> p (a n)"), zs[par][:, 0:NS],
                                     ACT.Copy).then_inc(z_free, 1)

            with act.Fori(0, CC // 2) as i:
                for par in range(2):
                    keep_at(i, par)
            for t in range(CC):
                keep(CC + t, t % 2)
                n = 0
                for g, (buf, row) in enumerate(((gr, R_BA), (gi, R_BX))):
                    for lo, hi in NARROW + [(SEQ, NTOK)]:
                        act.wait_ge(z_ready, 6 * t + n + 1)
                        if t > 0 and n == 0:
                            act.wait_ge(c_done, t)
                        nc.scalar.activation(buf[:, lo:hi], gp[n % 2][:, 0:hi - lo], ACT.Sigmoid,
                                             bias=c.par[:, t, row:row + 1]).then_inc(gp_free, 1)
                        n += 1
                act.wait_ge(gp_free, 6 * t + 8)
                nc.scalar.activation(th[:], gr[:], ACT.Tanh, scale=c.coef[:, 1, t:t + 1]).then_inc(a_done, 1)
                act.wait_ge(a_done, 2 * t + 1)
                nc.scalar.activation(gr[:], gr[:], ACT.Exp, scale=c.coef[:, 0, t:t + 1]).then_inc(a_done, 1)
                act.wait_ge(gx_ready, t + 1)
                nc.scalar.activation(th[:], th[:], ACT.Sqrt).then_inc(sq_done, 1)
                gate = zT[:, CC + t, :]
                act.wait_ge(z_free, CC + t + 3)
                nc.scalar.activation(gate, gate, ACT.Gelu_apprx_tanh).then_inc(gelu_done, 1)
            with act.Fori(CC, NZ // 2) as i:
                for par in range(2):
                    keep_at(i, par)
            for t, rows in TILES:
                act.wait_ge(tok_ready, t + 1)
                nc.scalar.activation(v_tok[0:rows, t, :], zp[t % 2][0:rows, 0:DR], ACT.Copy).then_inc(v_done, 1)

        @block.vector
        def _(dve):
            n = [0]

            def then(ins):
                n[0] += 1
                ins.then_inc(step, 1)
                dve.wait_ge(step, n[0])

            dve.sem_inc(k_done, 2)
            wts = lambda t, j: c.par[:, t, R_CONVW + j:R_CONVW + j + 1]
            for t in range(CC):
                dve.wait_ge(z_free, t + 3)
                xr = zT[:, t, :]
                then(nc.vector.tensor_scalar(xc[:, 0:SEQ], xr[:, 0:SEQ], wts(t, CW - 1), c.par[:, t, R_CONVB:R_CONVB + 1],
                                             ALU.mult, ALU.add))
                for j in range(CW - 2, -1, -1):
                    d = CW - 1 - j
                    then(nc.vector.scalar_tensor_tensor(out=xc[:, d:SEQ], in0=xr[:, 0:SEQ - d], scalar=wts(t, j),
                                                        in1=xc[:, d:SEQ], op0=ALU.mult, op1=ALU.add))
                old = c.par[:, t, R_SCONV:R_SCONV + DB * (CW - 1)].rearrange("p (b w) -> p b w", b=DB)
                new = xr[:, SEQ:NTOK].rearrange("p (b w) -> p b w", b=DB)
                nc.vector.tensor_copy(hist[:, :, 0:CW - 1], old).then_inc(step, 1)
                n[0] += 1
                then(nc.vector.tensor_copy(hist[:, :, CW - 1:], new))
                xs = xc[:, SEQ:NTOK].rearrange("p (b w) -> p b w", b=DB)
                then(nc.vector.tensor_scalar(xs, hist[:, :, CW - 1:CW - 1 + DT], wts(t, CW - 1),
                                             c.par[:, t, R_CONVB:R_CONVB + 1], ALU.mult, ALU.add))
                for j in range(CW - 2, -1, -1):
                    ins = nc.vector.scalar_tensor_tensor(out=xs, in0=hist[:, :, j:j + DT], scalar=wts(t, j), in1=xs,
                                                         op0=ALU.mult, op1=ALU.add)
                    if j:
                        then(ins)
                ins.then_inc(xc_ready, 1)
                nc.vector.tensor_copy(last_in[:, t, 0:24].rearrange("p (b w) -> p b w", b=DB),
                                      new[:, :, DT - (CW - 1):]).then_inc(step, 1)
                nc.vector.tensor_copy(last_in[:, t, 24:27], xr[:, SEQ - 3:SEQ]).then_inc(step, 1)
                n[0] += 2
                dve.wait_ge(a_done, 2 * t + 2)
                sq = zT[:, t, :]
                dve.wait_ge(step, n[0])
                then(nc.vector.tensor_tensor(sq, gr[:], gr[:], ALU.mult))
                nc.vector.scalar_tensor_tensor(out=th[:], in0=sq, scalar=1.0, in1=th[:], op0=ALU.add,
                                               op1=ALU.mult).then_inc(gx_ready, 1)
                then(nc.vector.tensor_tensor(gi[:], gi[:], xc[:], ALU.mult))
                dve.wait_ge(sq_done, t + 1)
                then(nc.vector.tensor_tensor(gi[:], gi[:], th[:], ALU.mult))
                then(nc.vector.tensor_tensor_scan(th[:, 0:SEQ], gr[:, 0:SEQ], gi[:, 0:SEQ], 0.0, ALU.mult, ALU.add))
                v = lambda x: x[:, SEQ:NTOK].rearrange("p (b w) -> p b w", b=DB)
                prev = c.par[:, t, R_SH:R_SH + DB]
                for j in range(DT):
                    then(nc.vector.tensor_tensor(v(th)[:, :, j], v(gr)[:, :, j], prev, ALU.mult))
                    then(nc.vector.tensor_tensor(v(th)[:, :, j], v(th)[:, :, j], v(gi)[:, :, j], ALU.add))
                    prev = v(th)[:, :, j]
                nc.vector.tensor_copy(last_in[:, t, 27:28], th[:, SEQ - 1:SEQ]).then_inc(step, 1)
                nc.vector.tensor_copy(last_in[:, t, 28:36], prev).then_inc(step, 1)
                n[0] += 2
                dve.wait_ge(gelu_done, t + 1)
                then(nc.vector.tensor_tensor(sq, th[:], zT[:, CC + t, :], ALU.mult))
                dve.sem_inc(c_done, 1)
            for t, rows in TILES:
                dve.wait_ge(tok_ready, t + 1)
                if t >= 2:
                    dve.wait_ge(k_landed[t % 2], 16 * (t // 2))
                nc.vector.tensor_copy(k_tok[0:rows, t % 2, :], zp[t % 2][0:rows, DR:2 * DR]).then_inc(k_done, 1)
            dve.wait_ge(lp_ready, 1)
            nc.vector.tensor_copy(last_rows[:], lp).then_inc(last_ready, 1)


def attend_prompt(nc, a, c, zT, v_tok, y_tok):
    PAIRS = HEADS // 2
    UNITS = 2 * PT
    unit = [(n // PT, n % PT) for n in range(UNITS)]
    groups = []
    first_group = []
    for n, (h, i) in enumerate(unit):
        first_group.append(len(groups))
        groups += [(n, lo, min(lo + 4, i + 1)) for lo in range(0, i + 1, 4)]
    GROUPS = len(groups)
    first_group.append(GROUPS)
    of_unit = lambda n: range(first_group[n], first_group[n + 1])
    assert GROUPS % 4 == 0 and UNITS % 4 == 0
    with ExitStack() as ctx:
        s = Shop(nc, ctx, "attend_prompt")
        passed = s.sem("passed")
        qT, kT = s.sb("qT", [P, SEQ]), s.sb("kT", [P, SEQ])
        logits, prob = s.sb("logits", [P, 2, SEQ]), s.sb("prob", [P, 2, SEQ])
        probT = s.sb("probT", [P, 4, HALF])
        top, neg_top, den, rden = (s.sb(x, [P, 4]) for x in ("top", "neg_top", "den", "rden"))
        sp_ = [s.ps(f"s{i}", [P, SEQ]) for i in range(2)]
        pt = [s.ps(f"pt{i}", [P, HALF]) for i in range(2)]
        o = [s.ps(f"o{i}", [P, HALF]) for i in range(2)]
        q_ready, k_ready, s_ready, s_free = s.sem("q_ready"), s.sem("k_ready"), s.sem("s_ready"), s.sem("s_free")
        top_ready, exp_done, p_ready, rden_ready = s.sem("top_ready"), s.sem("exp_done"), s.sem("p_ready"), s.sem("rden_ready")
        pt_ready, pt_free, pv_done, o_free = s.sem("pt_ready"), s.sem("pt_free"), s.sem("pv_done"), s.sem("o_free")
        probT_free = s.sem("probT_free")
        block = ctx.enter_context(nc.Block())

        @block.gpsimd
        def _(pool):
            with pool.Fori(0, PAIRS) as i:
                pool.wait_ge(s_ready, UNITS * i + 1)
                nc.gpsimd.tensor_copy(qT[:], zT[:, bass.ds(i + 2 * CC, 1), 0:SEQ].rearrange("p a n -> p (a n)")).then_inc(q_ready, 1)
                nc.gpsimd.tensor_copy(kT[:], zT[:, bass.ds(i + 3 * CC, 1), 0:SEQ].rearrange("p a n -> p (a n)")).then_inc(k_ready, 1)

        @block.tensor
        def _(pe):
            pe.sem_inc(s_ready, 1)
            pe.sem_inc(probT_free, 4)

            def scores(it, n):
                h, i = unit[n]
                rows, L = slice(HD * h, HD * h + HD), (i + 1) * P
                if n == 0:
                    pe.wait_ge(q_ready, it + 1)
                    pe.wait_ge(k_ready, it + 1)
                pe.wait_ge(s_free, UNITS * it + n + 1)
                for lo in range(0, L, HALF):
                    hi = min(lo + HALF, L)
                    last = nc.tensor.matmul(sp_[n % 2][:, lo:hi], qT[rows, i * P:(i + 1) * P], kT[rows, lo:hi],
                                            start=True, stop=True)
                last.then_inc(s_ready, 1)

            def turn(it, n):
                pe.wait_ge(p_ready, UNITS * it + n + 1)
                for g in of_unit(n):
                    _, lo, hi = groups[g]
                    pe.wait_ge(pt_free, GROUPS * it + g + 1)
                    for b in range(lo, hi):
                        last = nc.tensor.transpose(pt[g % 2][:, (b - lo) * P:(b - lo + 1) * P],
                                                   prob[:, n % 2, b * P:(b + 1) * P], c.ident[:])
                    last.then_inc(pt_ready, 1)

            def values(it, n):
                h, i = unit[n]
                pe.wait_ge(o_free, UNITS * it + n + 1)
                for g in of_unit(n):
                    _, lo, hi = groups[g]
                    pe.wait_ge(pt_free, GROUPS * it + g + 3)
                    for b in range(lo, hi):
                        last = nc.tensor.matmul(o[n % 2][:, 0:HD], probT[:, g % 4, (b - lo) * P:(b - lo + 1) * P],
                                                v_tok[:, b, bass.ds(it * 2 * HD + h * HD, HD)],
                                                start=(b == 0), stop=(b == i))
                    last.then_inc(probT_free, 1)
                pe.wait_ge(probT_free, GROUPS * it + first_group[n + 1] + 4)
                pe.sem_inc(pv_done, 1)

            with pe.Fori(0, PAIRS) as it:
                for k in range(UNITS + 2):
                    if k < UNITS:
                        scores(it, k)
                    if k >= 2:
                        values(it, k - 2)
                    if 1 <= k <= UNITS:
                        turn(it, k - 1)

        @block.scalar
        def _(act):
            act.sem_inc(pt_free, 2)

            def exps(it, n):
                L = (unit[n][1] + 1) * P
                act.wait_ge(top_ready, UNITS * it + n + 1)
                nc.scalar.activation(prob[:, n % 2, 0:L], logits[:, n % 2, 0:L], ACT.Exp, scale=SCALE,
                                     bias=neg_top[:, n % 4:n % 4 + 1]).then_inc(exp_done, 1)

            def keep(it, n):
                for g in of_unit(n):
                    _, lo, hi = groups[g]
                    act.wait_ge(pt_ready, GROUPS * it + g + 1)
                    act.wait_ge(probT_free, GROUPS * it + g + 1)
                    nc.scalar.activation(probT[:, g % 4, 0:(hi - lo) * P], pt[g % 2][:, 0:(hi - lo) * P],
                                         ACT.Copy).then_inc(pt_free, 1)

            with act.Fori(0, PAIRS) as it:
                for k in range(UNITS + 1):
                    if k < UNITS:
                        exps(it, k)
                    if k >= 1:
                        keep(it, k - 1)

        @block.vector
        def _(dve):
            dve.sem_inc(s_free, 2)
            dve.sem_inc(o_free, 2)

            def tops(it, n):
                L = (unit[n][1] + 1) * P
                dve.wait_ge(s_ready, UNITS * it + n + 2)
                dve.sem_inc(passed, 1)
                nc.vector.tensor_tensor_reduce(out=logits[:, n % 2, 0:L], in0=sp_[n % 2][:, 0:L],
                                               in1=c.bias[:, SEQ - L:SEQ], scale=1.0, scalar=-3e38, op0=ALU.add,
                                               op1=ALU.max, accum_out=top[:, n % 4:n % 4 + 1]).then_inc(s_free, 1)
                dve.wait_ge(s_free, UNITS * it + n + 3)
                nc.vector.tensor_scalar(neg_top[:, n % 4:n % 4 + 1], top[:, n % 4:n % 4 + 1], -SCALE, None,
                                        ALU.mult).then_inc(top_ready, 1)

            def weigh(it, n):
                L = (unit[n][1] + 1) * P
                dve.wait_ge(exp_done, UNITS * it + n + 1)
                nc.vector.tensor_tensor_reduce(out=prob[:, n % 2, 0:L], in0=prob[:, n % 2, 0:L],
                                               in1=c.mult[:, SEQ - L:SEQ], scale=1.0, scalar=0.0, op0=ALU.mult,
                                               op1=ALU.add, accum_out=den[:, n % 4:n % 4 + 1]).then_inc(p_ready, 1)
                dve.wait_ge(p_ready, UNITS * it + n + 1)
                nc.vector.reciprocal(rden[:, n % 4:n % 4 + 1], den[:, n % 4:n % 4 + 1]).then_inc(rden_ready, 1)

            def divide(it, n):
                h, i = unit[n]
                dve.wait_ge(pv_done, UNITS * it + n + 1)
                dve.wait_ge(rden_ready, UNITS * it + n + 1)
                nc.vector.tensor_scalar(y_tok[:, i, bass.ds(it * 2 * HD + h * HD, HD)], o[n % 2][:, 0:HD],
                                        rden[:, n % 4:n % 4 + 1], None, ALU.mult).then_inc(o_free, 1)

            with dve.Fori(0, PAIRS) as it:
                for k in range(UNITS + 3):
                    if k < UNITS:
                        tops(it, k)
                    if 1 <= k <= UNITS:
                        weigh(it, k - 1)
                    if k >= 3:
                        divide(it, k - 3)


def attend_sample(nc, a, c, zT, v_tok, ysT, xT):
    OLD, SK = c.OLD, c.SK
    NW = SK + NS
    with ExitStack() as ctx:
        s = Shop(nc, ctx, "attend_sample")
        passed = s.sem("passed")
        spent = xT[:].rearrange("p k n -> p (k n)")
        kn, vn = (spent[:, i * 8 * DR:(i + 1) * 8 * DR].rearrange("p (a t e) -> p a t e", a=2, t=4) for i in range(2))
        ko, vo = s.sb("ko", [OLD, 2, DT, DR]), s.sb("vo", [OLD, 2, DT, DR])
        q_all = s.sb("q_all", [P, DB, CC, NS])
        q_one = s.sb("q_one", [P, 2, CC, NS])
        ktn, kto = s.sb("ktn", [P, 2, HALF]), s.sb("kto", [P, 2, DT * OLD])
        bias, mult = c.s_bias, c.s_mult
        gate = zT[0:NS, CC:2 * CC, :].rearrange("p a n -> p (a n)")
        logits = gate[:, 0:2 * NW].rearrange("p (a n) -> p a n", a=2)
        prob = gate[:, 2 * NW:4 * NW].rearrange("p (a n) -> p a n", a=2)
        probT = s.sb("probT_s", [P, 9, NS])
        top, den = s.sb("top_s", [NS, 2, 4]), s.sb("den_s", [NS, 2, 2])
        pn, po = s.ps("pn", [P, HALF]), s.ps("po", [P, HALF])
        sn = [s.ps(f"sn{i}", [NS, HALF]) for i in range(2)]
        so = [s.ps(f"so{i}", [NS, HALF]) for i in range(2)]
        pt, ot = s.ps("pt_s", [P, HALF]), s.ps("ot", [P, HALF])
        k_landed = [s.sem(f"ks_landed{i}") for i in range(2)]
        v_landed = [s.sem(f"vs_landed{i}") for i in range(2)]
        names = ("q_zero", "q_all_ready", "q_ready", "masks_ready", "pn_ready", "po_ready", "pn_free", "po_free",
                 "kt_used", "s_ready", "step", "top_ready", "exp_done", "den_ready", "p_ready", "pt_ready",
                 "pt_free", "pv_done", "out_done")
        m = {x: s.sem(x) for x in names}
        block = ctx.enter_context(nc.Block())
        LOOPS = DB // 2

        @block.sync
        def _(sp):
            with sp.Fori(0, LOOPS) as i:
                for par in range(2):
                    b = 2 * i + par
                    sp.wait_ge(m["out_done"], b + 1)
                    for x, new, old, sem in (("cache_k", kn, ko, k_landed), ("cache_v", vn, vo, v_landed)):
                        cache = a[x][0].rearrange("b t h e -> b (t h e)")
                        row = HEADS * HD
                        sp.dma_start(new[:, par].rearrange("p i e -> p (i e)"),
                                     cache[bass.ds(b, 1), (PAST - HALF) * row:PAST * row].rearrange(
                                         "a (p f) -> (a p) f", p=P)).then_inc(sem[par], 16)
                        sp.dma_start(old[:, par].rearrange("p i e -> p (i e)"),
                                     cache[bass.ds(b, 1), 0:(PAST - HALF) * row].rearrange(
                                         "a (p f) -> (a p) f", p=OLD)[:, 0:DT * row]).then_inc(sem[par], 16)

        @block.gpsimd
        def _(pool):
            nc.gpsimd.memset(q_all[:], 0.0).then_inc(m["q_zero"], 1)
            pool.wait_ge(m["q_zero"], 1)
            n = 0
            for j in range(CC):
                for half in range(2):
                    rows, col = slice(HD * half, HD * half + HD), DT * (2 * j + half)
                    nc.gpsimd.tensor_copy(q_all[rows, :, j, col:col + DT],
                                          zT[rows, 2 * CC + j, SEQ:NTOK].rearrange("p (b w) -> p b w", b=DB)
                                          ).then_inc(m["q_all_ready"], 1)
                    n += 1
            pool.wait_ge(m["q_all_ready"], n)
            with pool.Fori(0, LOOPS) as i:
                for par in range(2):
                    b = 2 * i + par
                    pool.wait_ge(m["out_done"], b + 1)
                    nc.gpsimd.tensor_copy(q_one[:, par], q_all[:, bass.ds(b, 1)].rearrange("p a j r -> p (a j) r")
                                          ).then_inc(m["q_ready"], 1)
                    nc.gpsimd.tensor_copy(bias[:, par, SK:NW], c.n_bias[:, bass.ds(b, 1), :].rearrange("p a r -> p (a r)")
                                          ).then_inc(m["masks_ready"], 1)
                    nc.gpsimd.tensor_copy(mult[:, par, SK:NW], c.n_mult[:, bass.ds(b, 1), :].rearrange("p a r -> p (a r)")
                                          ).then_inc(m["masks_ready"], 1)

        @block.tensor
        def _(pe):
            pe.sem_inc(m["kt_used"], 2)

            def scores(b, i, par):
                pe.wait_ge(k_landed[par], 32 * (i + 1))
                pe.wait_ge(m["q_ready"], b + 1)

                def product(j):
                    pe.wait_ge(m["pn_free"], CC * b + j + 2)
                    pe.wait_ge(m["po_free"], CC * b + j + 2)
                    q = q_one[:, par, j, :]
                    nc.tensor.matmul(sn[par][:], q, ktn[:, j % 2, :], start=(j == 0), stop=(j == CC - 1))
                    nc.tensor.matmul(so[par][:, 0:DT * OLD], q, kto[:, j % 2, :], start=(j == 0), stop=(j == CC - 1),
                                     skip_group_check=True)
                    nc.tensor.matmul(so[par][:, DT * OLD:DT * OLD + NS], q, zT[:, 3 * CC + j, SEQ:NTOK],
                                     start=False, stop=(j == CC - 1),
                                     skip_group_check=True).then_inc(m["kt_used"], 1)

                for j in range(CC):
                    pe.wait_ge(m["pn_free"], CC * b + j + 1)
                    for t in range(4):
                        last = nc.tensor.transpose(pn[:, t * P:(t + 1) * P], kn[:, par, t, j * P:(j + 1) * P], c.ident[:])
                    last.then_inc(m["pn_ready"], 1)
                    pe.wait_ge(m["po_free"], CC * b + j + 1)
                    for t in range(DT):
                        last = nc.tensor.transpose(po[:, t * OLD:(t + 1) * OLD], ko[:, par, t, j * P:(j + 1) * P],
                                                   c.ident[0:OLD, 0:OLD])
                    last.then_inc(m["po_ready"], 1)
                    if j:
                        product(j - 1)
                product(CC - 1)
                pe.wait_ge(m["kt_used"], CC * (b + 1) + 2)
                pe.sem_inc(m["s_ready"], 1)

            def values(b, i, par):
                pe.wait_ge(m["p_ready"], b + 1)
                pe.sem_inc(passed, 1)
                for t in range(4):
                    nc.tensor.transpose(pt[:, t * NS:(t + 1) * NS], prob[:, par, t * P:(t + 1) * P], c.ident[0:NS, 0:NS])
                for t in range(DT):
                    nc.tensor.transpose(pt[0:OLD, (4 + t) * NS:(5 + t) * NS],
                                        prob[:, par, HALF + t * OLD:HALF + (t + 1) * OLD], c.ident[0:NS, 0:NS])
                nc.tensor.transpose(pt[0:NS, 8 * NS:9 * NS], prob[:, par, SK:NW], c.ident[0:NS, 0:NS]).then_inc(m["pt_ready"], 1)
                pe.wait_ge(v_landed[par], 32 * (i + 1))
                pe.wait_ge(m["pt_free"], b + 1)
                pe.wait_ge(m["out_done"], b + 2)
                for j in range(CC):
                    r = slice(2 * DT * j, 2 * DT * (j + 1))
                    e = slice(j * P, (j + 1) * P)
                    for t in range(4):
                        nc.tensor.matmul(ot[:, 8 * j:8 * j + 8], vn[:, par, t, e], probT[:, t, r],
                                         start=(t == 0), stop=False)
                    for t in range(DT):
                        nc.tensor.matmul(ot[:, 8 * j:8 * j + 8], vo[:, par, t, e], probT[0:OLD, 4 + t, r],
                                         start=False, stop=False)
                    last = nc.tensor.matmul(ot[:, 8 * j:8 * j + 8], v_tok[0:NS, PT, e], probT[0:NS, 8, r],
                                            start=False, stop=True)
                last.then_inc(m["pv_done"], 1)

            with pe.Fori(0, LOOPS) as i:
                for par in range(2):
                    scores(2 * i + par, i, par)
                for par in range(2):
                    values(2 * i + par, i, par)

        @block.scalar
        def _(act):
            act.sem_inc(m["pn_free"], 1)

            def keys(b):
                for j in range(CC):
                    act.wait_ge(m["pn_ready"], CC * b + j + 1)
                    act.wait_ge(m["kt_used"], CC * b + j + 1)
                    nc.scalar.activation(ktn[:, j % 2, :], pn[:], ACT.Copy).then_inc(m["pn_free"], 1)

            def exps(b, par):
                act.wait_ge(m["top_ready"], b + 1)
                nc.scalar.activation(prob[:, par], logits[:, par], ACT.Exp, scale=SCALE,
                                     bias=top[:, par, 2:3]).then_inc(m["exp_done"], 1)

            def norm(b, par):
                act.wait_ge(m["den_ready"], b + 1)
                nc.scalar.activation(prob[:, par], prob[:, par], ACT.Copy, scale=den[:, par, 1:2]).then_inc(m["p_ready"], 1)

            def turned(b):
                act.wait_ge(m["pt_ready"], b + 1)
                act.wait_ge(m["pv_done"], b + 1)
                nc.scalar.activation(probT[:, 0:4], pt[:, 0:4 * NS].rearrange("p (t r) -> p t r", r=NS), ACT.Copy)
                nc.scalar.activation(probT[0:OLD, 4:8], pt[0:OLD, 4 * NS:8 * NS].rearrange("p (t r) -> p t r", r=NS), ACT.Copy)
                nc.scalar.activation(probT[0:NS, 8], pt[0:NS, 8 * NS:9 * NS], ACT.Copy).then_inc(m["pt_free"], 1)

            act.sem_inc(m["pv_done"], 1)
            with act.Fori(0, LOOPS) as i:
                for par in range(2):
                    keys(2 * i + par)
                for par in range(2):
                    exps(2 * i + par, par)
                for par in range(2):
                    norm(2 * i + par, par)
                for par in range(2):
                    turned(2 * i + par)

        @block.vector
        def _(dve):
            dve.sem_inc(m["po_free"], 1)
            dve.sem_inc(m["out_done"], 2)

            def keys(b):
                for j in range(CC):
                    dve.wait_ge(m["po_ready"], CC * b + j + 1)
                    dve.wait_ge(m["kt_used"], CC * b + j + 1)
                    nc.vector.tensor_copy(kto[:, j % 2, :], po[:, 0:DT * OLD]).then_inc(m["po_free"], 1)

            def tops(b, par):
                dve.wait_ge(m["s_ready"], b + 1)
                dve.wait_ge(m["masks_ready"], 2 * b + 2)
                dve.sem_inc(passed, 1)
                nc.vector.tensor_tensor_reduce(out=logits[:, par, 0:HALF], in0=sn[par][:], in1=bias[:, par, 0:HALF],
                                               scale=1.0, scalar=-3e38, op0=ALU.add, op1=ALU.max,
                                               accum_out=top[:, par, 0:1]).then_inc(m["step"], 1)
                dve.wait_ge(m["step"], 2 * b + 1)
                dve.sem_inc(passed, 1)
                nc.vector.tensor_tensor_reduce(out=logits[:, par, HALF:NW], in0=so[par][:, 0:NW - HALF],
                                               in1=bias[:, par, HALF:NW], scale=1.0, scalar=top[:, par, 0:1],
                                               op0=ALU.add, op1=ALU.max, accum_out=top[:, par, 1:2]).then_inc(m["step"], 1)
                dve.wait_ge(m["step"], 2 * b + 2)
                nc.vector.tensor_scalar(top[:, par, 2:3], top[:, par, 1:2], -SCALE, None, ALU.mult).then_inc(m["top_ready"], 1)

            def sums(b, par):
                dve.wait_ge(m["exp_done"], b + 1)
                nc.vector.tensor_tensor_reduce(out=prob[:, par], in0=prob[:, par], in1=mult[:, par], scale=1.0, scalar=0.0,
                                               op0=ALU.mult, op1=ALU.add, accum_out=den[:, par, 0:1]).then_inc(m["q_zero"], 1)
                dve.wait_ge(m["q_zero"], b + 2)
                nc.vector.reciprocal(den[:, par, 1:2], den[:, par, 0:1]).then_inc(m["den_ready"], 1)

            def keep(b, par):
                dve.wait_ge(m["pv_done"], b + 2)
                for half in range(2):
                    rows = slice(HD * half, HD * half + HD)
                    last = nc.vector.tensor_copy(
                        ysT[rows, :, bass.ds(b * DT, DT)],
                        ot[rows, 0:8 * CC].rearrange("p (j h w) -> p j h w", j=CC, h=2)[:, :, half, :])
                last.then_inc(m["out_done"], 1)

            with dve.Fori(0, LOOPS) as i:
                for par in range(2):
                    keys(2 * i + par)
                for par in range(2):
                    tops(2 * i + par, par)
                for par in range(2):
                    sums(2 * i + par, par)
                for par in range(2):
                    keep(2 * i + par, par)


def merge(nc, a, c, zT, y_tok, ysT, xT, x_res, x_parts):
    with ExitStack() as ctx:
        s = Shop(nc, ctx, "merge")
        passed = s.sem("passed")
        spent = zT[:, CC:4 * CC, :].rearrange("p a n -> p (a n)")
        w_out = spent[:, 0:KC * D].rearrange("p (k n) -> p k n", k=KC)
        x_in = spent[:, KC * D:(KC + 2) * D].rearrange("p (k n) -> p k n", k=2)
        x2 = spent[:, (KC + 2) * D:(KC + 4) * D].rearrange("p (k n) -> p k n", k=2)
        g_row = s.sb("g_row", [P, D])
        sq, sg, ya = s.sb("sq", [P, CC, P]), s.sb("sg", [P, 2, CC, P]), s.sb("ya", [P, 2, CC, P])
        rr = s.sb("rr", [P, 3, P])
        yn = s.sb("yn", [P, DR])
        xn, xf = s.sb("xn2", [P, D]), s.sb("xf", [P, D])
        squares = s.sb("squares2", [P, D])
        pieces = s.sb("pieces", [P, 3, D], BF16)
        stat = s.sb("stat2", [P, 2, 8])
        acc = [s.ps(f"acc{i}", [P, D]) for i in range(2)]
        ssb, yp, tp = s.ps("ssb", [P, HALF]), s.ps("yp", [P, HALF]), s.ps("tp2", [P, KC, P])
        x_landed = [s.sem(f"mx_landed{i}") for i in range(2)]
        x2_stored = [s.sem(f"x2_stored{i}") for i in range(2)]
        w_landed = s.sem("w_out_landed")
        m = {x: s.sem(x) for x in (
            "sq_ready ssb_ready msr_ready rtr_done rr_ready sg_ready sga_done msa_ready rta_done ra_ready yn_ready "
            "yp_ready ya_ready summed x2_half x2_ready sqb_done msb_ready rtb_done rb_ready xn_ready xt_ready xt_done "
            "xf_ready hi_ready r1_ready mid_ready lo_ready stored sqa_ready").split()}
        block = ctx.enter_context(nc.Block())

        def run(eng, step):
            step(0, 0)
            step(1, 1)
            with eng.Fori(1, PT // 2) as i:
                step(2 * i, 0)
                step(2 * i + 1, 1)
            step(PT, 0)
            step(PT + 1, 1)
            step(PT + 2, 0)

        def has(k, back):
            if not isinstance(k, int):
                return P
            t = k - back
            return 0 if t < 0 or t > PT else (NS if t == PT else P)

        @block.sync
        def _(sp):
            sp.dma_start(w_out, a["w_out"][0].rearrange("(k p) n -> p k n", p=P)).then_inc(w_landed, 16)
            sp.dma_start(g_row[:], a["g_ffn"].to_broadcast((P, D))).then_inc(w_landed, 16)

            def step(k, par):
                rows = has(k, 0)
                if rows:
                    if not (isinstance(k, int) and k < 2):
                        sp.wait_ge(m["x2_ready"], k - 1)
                        sp.sem_inc(passed, 1)
                    src = a["x_prompt"][0, cols(k), :] if rows == P else a["x_sample"].rearrange("b t d -> (b t) d")
                    sp.dma_start(x_in[0:rows, par, :], src).then_inc(x_landed[par], 16)
                rows = has(k, 2)
                if rows:
                    t = k - 2
                    sp.dma_start(x_res[bass.ds(t * P, rows), :], x2[0:rows, par, :]).then_inc(x2_stored[par], 16)
                    sp.wait_ge(m["lo_ready"], t + 1)
                    sp.sem_inc(passed, 1)
                    for part in range(3):
                        sp.dma_start(x_parts[part, bass.ds(t * P, rows), :], pieces[0:rows, part, :]).then_inc(m["stored"], 16)

            def step2(k, par):
                if has(k, 2):
                    sp.wait_ge(m["x2_ready"], k - 1)
                step(k, par)

            run(sp, step2)
            sp.wait_ge(m["stored"], 48 * (PT + 1))
            sp.wait_ge(x2_stored[0], 16 * (PT // 2 + 1))
            sp.wait_ge(x2_stored[1], 16 * (PT // 2))

        @block.tensor
        def _(pe):
            def groups(k, par, rows):
                pe.wait_ge(m["sq_ready"], k + 1)
                if not (isinstance(k, int) and k == 0):
                    pe.wait_ge(m["msr_ready"], k)
                for j in range(CC):
                    last = nc.tensor.matmul(ssb[:, 0:rows], c.ones[:], sq[:, j, 0:rows], start=(j == 0), stop=(j == CC - 1))
                last.then_inc(m["ssb_ready"], 1)
                if rows == P:
                    pe.wait_ge(m["yn_ready"], k + 1)
                    if not (isinstance(k, int) and k == 0):
                        pe.wait_ge(m["ya_ready"], k)
                    for j in range(CC):
                        last = nc.tensor.transpose(yp[:, j * P:(j + 1) * P], yn[:, j * P:(j + 1) * P], c.ident[:])
                    last.then_inc(m["yp_ready"], 1)
                else:
                    pe.wait_ge(m["sqa_ready"], 1)
                    for j in range(CC):
                        last = nc.tensor.matmul(yp[:, 0:rows], c.ones[:], sq[:, j, P - NS:P], start=(j == 0), stop=(j == CC - 1))
                    last.then_inc(m["yp_ready"], 1)

            def product(t, par, rows):
                pe.wait_ge(m["sg_ready"], t + 1)
                pe.wait_ge(m["ya_ready"], t + 1)
                if not (isinstance(t, int) and t < 2):
                    pe.wait_ge(m["x2_ready"], t - 1)
                for n, y in enumerate((sg, ya)):
                    for j in range(CC):
                        for lo, hi in NARROW:
                            last = nc.tensor.matmul(acc[par][0:rows, lo:hi], y[:, par, j, 0:rows], w_out[:, CC * n + j, lo:hi],
                                                    start=(n + j == 0), stop=(n == 1 and j == CC - 1))
                last.then_inc(m["summed"], 1)

            def second_norm(t, rows):
                pe.wait_ge(m["xn_ready"], t + 1)
                if not (isinstance(t, int) and t == 0):
                    pe.wait_ge(m["xt_done"], t)
                for j in range(KC):
                    last = nc.tensor.transpose(tp[:, j, 0:rows], xn[0:rows, j * P:(j + 1) * P], c.ident[0:rows, 0:rows])
                last.then_inc(m["xt_ready"], 1)

            def step(k, par):
                if has(k, 0):
                    groups(k, par, has(k, 0))
                if has(k, 1):
                    product(k - 1, 1 - par, has(k, 1))
                if has(k, 2):
                    second_norm(k - 2, has(k, 2))

            pe.wait_ge(w_landed, 32)
            run(pe, step)

        @block.scalar
        def _(act):
            def groups(k, par, rows):
                if rows == P:
                    if not (isinstance(k, int) and k == 0):
                        act.wait_ge(m["yn_ready"], k)
                        act.sem_inc(passed, 1)
                    nc.scalar.activation(squares[:, 0:DR], y_tok[:, bass.ds(k, 1), :].rearrange("p a e -> p (a e)"),
                                         ACT.Square, accum_out=stat[:, par, 0:1]).then_inc(m["sga_done"], 1)
                act.wait_ge(m["msr_ready"], k + 1)
                nc.scalar.activation(rr[:, 1, 0:rows], rr[:, 0, 0:rows], ACT.Sqrt).then_inc(m["rtr_done"], 1)
                act.wait_ge(m["msa_ready"], k + 1)
                if rows == P:
                    nc.scalar.activation(stat[:, par, 2:3], stat[:, par, 1:2], ACT.Sqrt).then_inc(m["rta_done"], 1)
                    act.wait_ge(m["ra_ready"], k + 1)
                    if not (isinstance(k, int) and k == 0):
                        act.wait_ge(m["yp_ready"], k)
                        act.sem_inc(passed, 1)
                    nc.scalar.activation(yn[:], y_tok[:, bass.ds(k, 1), :].rearrange("p a e -> p (a e)"), ACT.Copy,
                                         scale=stat[:, par, 3:4]).then_inc(m["yn_ready"], 1)
                else:
                    nc.scalar.activation(rr[:, 1, P - NS:P], rr[:, 0, P - NS:P], ACT.Sqrt).then_inc(m["rta_done"], 1)

            def second_norm(t, par, rows):
                act.wait_ge(m["x2_ready"], t + 1)
                nc.scalar.activation(squares[0:rows, :], x2[0:rows, par, :], ACT.Square,
                                     accum_out=stat[0:rows, par, 4:5]).then_inc(m["sqb_done"], 1)
                act.wait_ge(m["msb_ready"], t + 1)
                nc.scalar.activation(stat[0:rows, par, 6:7], stat[0:rows, par, 5:6], ACT.Sqrt).then_inc(m["rtb_done"], 1)
                act.wait_ge(m["rb_ready"], t + 1)
                if not (isinstance(t, int) and t == 0):
                    act.wait_ge(m["xt_ready"], t)
                    act.wait_ge(m["xf_ready"], t)
                nc.scalar.activation(xn[0:rows, :], x2[0:rows, par, :], ACT.Copy,
                                     scale=stat[0:rows, par, 7:8]).then_inc(m["xn_ready"], 1)
                act.wait_ge(m["xf_ready"], t + 1)
                if not (isinstance(t, int) and t == 0):
                    act.wait_ge(m["stored"], 48 * t)
                nc.scalar.activation(pieces[0:rows, 0, :], xf[0:rows, :], ACT.Copy).then_inc(m["hi_ready"], 1)
                act.wait_ge(m["r1_ready"], t + 1)
                nc.scalar.activation(pieces[0:rows, 1, :], xf[0:rows, :], ACT.Copy).then_inc(m["mid_ready"], 1)

            def step(k, par):
                if has(k, 0):
                    groups(k, par, has(k, 0))
                if has(k, 2):
                    second_norm(k - 2, par, has(k, 2))

            run(act, step)

        @block.gpsimd
        def _(pool):
            def step(k, par):
                rows = has(k, 2)
                if rows:
                    t = k - 2
                    pool.wait_ge(m["xn_ready"], t + 1)
                    if not (isinstance(t, int) and t == 0):
                        pool.wait_ge(m["lo_ready"], t)
                    nc.gpsimd.tensor_tensor(xf[0:rows, :], xn[0:rows, :], g_row[0:rows, :], ALU.mult).then_inc(m["xf_ready"], 1)
                    pool.wait_ge(m["hi_ready"], t + 1)
                    nc.gpsimd.tensor_tensor(xf[0:rows, :], xf[0:rows, :], pieces[0:rows, 0, :], ALU.subtract).then_inc(m["r1_ready"], 1)
                    pool.wait_ge(m["mid_ready"], t + 1)
                    nc.gpsimd.tensor_tensor(pieces[0:rows, 2, :], xf[0:rows, :], pieces[0:rows, 1, :],
                                            ALU.subtract).then_inc(m["lo_ready"], 1)

            pool.wait_ge(w_landed, 32)
            run(pool, step)

        @block.vector
        def _(dve):
            wide = lambda x, rows: x.unsqueeze(2).to_broadcast((P, CC, rows))

            def groups(k, par, rows):
                y = zT[:, 0:CC, cols(k, rows)]
                if not (isinstance(k, int) and k == 0):
                    dve.wait_ge(m["ssb_ready"], k)
                nc.vector.tensor_tensor(sq[:, :, 0:rows], y, y, ALU.mult).then_inc(m["sq_ready"], 1)
                if not (isinstance(k, int) and k < 2):
                    dve.wait_ge(m["summed"], k - 1)
                nc.vector.tensor_tensor(sg[:, par, :, 0:rows], y, wide(c.par[:, :, R_GRNN], rows), ALU.mult)
                if rows != P:
                    nc.vector.tensor_tensor(sq[:, :, P - NS:P], ysT[:], ysT[:], ALU.mult).then_inc(m["sqa_ready"], 1)
                dve.wait_ge(m["ssb_ready"], k + 1)
                nc.vector.tensor_scalar(rr[:, 0, 0:rows], ssb[:, 0:rows], 1.0 / DR, EPS, ALU.mult, ALU.add).then_inc(m["msr_ready"], 1)
                if rows == P:
                    dve.wait_ge(m["sga_done"], k + 1)
                    nc.vector.tensor_scalar(stat[:, par, 1:2], stat[:, par, 0:1], 1.0 / DR, EPS, ALU.mult, ALU.add).then_inc(m["msa_ready"], 1)
                else:
                    dve.wait_ge(m["yp_ready"], k + 1)
                    nc.vector.tensor_scalar(rr[:, 0, P - NS:P], yp[:, 0:rows], 1.0 / DR, EPS, ALU.mult, ALU.add).then_inc(m["msa_ready"], 1)
                dve.wait_ge(m["rtr_done"], k + 1)
                nc.vector.reciprocal(rr[:, 2, 0:rows], rr[:, 1, 0:rows]).then_inc(m["rr_ready"], 1)
                dve.wait_ge(m["rr_ready"], k + 1)
                nc.vector.tensor_tensor(sg[:, par, :, 0:rows], sg[:, par, :, 0:rows],
                                        rr[:, 2:3, 0:rows].to_broadcast((P, CC, rows)), ALU.mult).then_inc(m["sg_ready"], 1)
                dve.wait_ge(m["rta_done"], k + 1)
                if rows == P:
                    nc.vector.reciprocal(stat[:, par, 3:4], stat[:, par, 2:3]).then_inc(m["ra_ready"], 1)
                    dve.wait_ge(m["yp_ready"], k + 1)
                    nc.vector.tensor_tensor(ya[:, par], yp[:].rearrange("p (j n) -> p j n", j=CC),
                                            wide(c.par[:, :, R_GATT], rows), ALU.mult).then_inc(m["ya_ready"], 1)
                else:
                    nc.vector.reciprocal(rr[:, 2, P - NS:P], rr[:, 1, P - NS:P]).then_inc(m["ra_ready"], 1)
                    dve.wait_ge(m["ra_ready"], k + 1)
                    nc.vector.tensor_tensor(ya[:, par, :, 0:rows], ysT[:], wide(c.par[:, :, R_GATT], rows), ALU.mult).then_inc(m["ra_ready"], 1)
                    dve.wait_ge(m["ra_ready"], k + 2)
                    nc.vector.tensor_tensor(ya[:, par, :, 0:rows], ya[:, par, :, 0:rows],
                                            rr[:, 2:3, P - NS:P].to_broadcast((P, CC, rows)), ALU.mult).then_inc(m["ya_ready"], 1)

            def product(t, par, rows):
                dve.wait_ge(m["summed"], t + 1)
                dve.wait_ge(x_landed[par], x_count(t))
                if not (isinstance(t, int) and t < 2):
                    dve.wait_ge(x2_stored[par], x_count(t) - 16)
                    dve.wait_ge(m["xn_ready"], t - 1)
                nc.vector.tensor_tensor(x2[0:rows, par, :], acc[par][0:rows, :], x_in[0:rows, par, :], ALU.add).then_inc(m["x2_ready"], 1)

            def x_count(t):
                return 16 * (t // 2 + 1) if isinstance(t, int) else count[0]

            count = [0]

            def second_norm(t, par, rows):
                dve.wait_ge(m["sqb_done"], t + 1)
                nc.vector.tensor_scalar(stat[0:rows, par, 5:6], stat[0:rows, par, 4:5], 1.0 / D, EPS, ALU.mult, ALU.add).then_inc(m["msb_ready"], 1)
                dve.wait_ge(m["rtb_done"], t + 1)
                nc.vector.reciprocal(stat[0:rows, par, 7:8], stat[0:rows, par, 6:7]).then_inc(m["rb_ready"], 1)
                dve.wait_ge(m["xt_ready"], t + 1)
                nc.vector.tensor_tensor(xT[:, :, cols(t, rows)], tp[:, :, 0:rows],
                                        c.g_ffn[:].unsqueeze(2).to_broadcast((P, KC, rows)), ALU.mult).then_inc(m["xt_done"], 1)

            def step(k, par):
                if has(k, 0):
                    groups(k, par, has(k, 0))
                if has(k, 1):
                    product(k - 1, 1 - par, has(k, 1))
                if has(k, 2):
                    second_norm(k - 2, par, has(k, 2))

            step(0, 0)
            step(1, 1)
            with dve.Fori(1, PT // 2) as i:
                count[0] = 16 * i
                step(2 * i, 0)
                count[0] = 16 * (i + 1)
                step(2 * i + 1, 1)
            step(PT, 0)
            step(PT + 1, 1)
            step(PT + 2, 0)


def route(nc, a, c, xT, best, best_at):
    NQ = 16
    w_view = a["w_query"][0].rearrange("(k p) n -> p k n", p=P)
    keys_view = a["sub_keys"][0].rearrange("h s n e -> (h s) n e")
    NT = PT + 1
    with ExitStack() as ctx:
        s = Shop(nc, ctx, "route")
        passed = s.sem("passed")
        w = s.sb("wq", [P, 2, KC, P])
        keys = s.sb("keys", [P, 2, P])
        keyT = s.sb("keyT", [P, 2, P])
        qT = s.sb("qT_r", [P, 2, NTOK])
        rest = s.sb("rest", [P, NT, P])
        top, top_at = s.sb("top16", [P, NT, 16]), s.sb("top16_at", [P, NT, 16], U32)
        qp, qs, kp = s.ps("qp", [P, SEQ]), s.ps("qs", [P, HALF]), s.ps("kp", [P, HALF])
        sc = [s.ps(f"sc{i}", [P, 4, P]) for i in range(3)]
        w_landed = [s.sem(f"wq_landed{i}") for i in range(2)]
        m = {x: s.sem(x) for x in (
            "w_used k_turned k_kept q_kept scored sc_free max1 rest1 max2 done moved").split()}
        block = ctx.enter_context(nc.Block())
        TT = [(t, P if t < PT else NS) for t in range(NT)]
        place = lambda t: sc[t // 4][:, t % 4, :]

        @block.sync
        def _(sp):
            with sp.Fori(0, NQ // 2) as i:
                for par in range(2):
                    n = 2 * i + par
                    sp.wait_ge(m["w_used"], n + 1)
                    sp.dma_start(w[:, par], w_view[:, :, bass.ds(n * P, P)]).then_inc(w_landed[par], 16)
                    sp.dma_start(keys[:, par], keys_view[bass.ds(n, 1)].rearrange("a n e -> (a n) e")).then_inc(w_landed[par], 16)

        @block.gpsimd
        def _(pool):
            with pool.Fori(0, NQ) as n:
                pool.wait_ge(m["done"], NT * (n + 1))
                for src, dst in ((top, best), (top_at, best_at)):
                    nc.gpsimd.tensor_copy(dst[:, 0:PT, bass.ds(n * 16, 16)], src[:, 0:PT, :]).then_inc(m["moved"], 1)
                    nc.gpsimd.tensor_copy(dst[0:NS, PT, bass.ds(n * 16, 16)], src[0:NS, PT, :]).then_inc(m["moved"], 1)

        @block.tensor
        def _(pe):
            pe.sem_inc(m["w_used"], 2)

            def project(n, par, loads):
                pe.wait_ge(w_landed[par], 32 * loads)
                if not (isinstance(n, int) and n == 0):
                    pe.wait_ge(m["k_kept"], n)
                    pe.wait_ge(m["q_kept"], n)
                nc.tensor.transpose(kp[:, 0:P], keys[:, par], c.ident[:]).then_inc(m["k_turned"], 1)
                for k in range(KC):
                    for lo, hi in NARROW:
                        nc.tensor.matmul(qp[:, lo:hi], w[:, par, k, :], xT[:, k, lo:hi], start=(k == 0), stop=(k == KC - 1))
                    last = nc.tensor.matmul(qs[:, 0:NS], w[:, par, k, :], xT[:, k, SEQ:NTOK], start=(k == 0), stop=(k == KC - 1))
                last.then_inc(m["w_used"], 1)

            def score(n, par):
                pe.wait_ge(m["q_kept"], n + 1)
                pe.wait_ge(m["k_kept"], n + 1)
                pe.wait_ge(m["sc_free"], n + 1)
                for t, rows in TT:
                    last = nc.tensor.matmul(place(t)[0:rows, :], qT[:, par, t * P:t * P + rows], keyT[:, par, :],
                                            start=True, stop=True)
                last.then_inc(m["scored"], 1)

            project(0, 0, 1)
            with pe.Fori(0, NQ // 2 - 1) as i:
                project(2 * i + 1, 1, i + 1)
                score(2 * i, 0)
                project(2 * i + 2, 0, i + 2)
                score(2 * i + 1, 1)
            project(NQ - 1, 1, NQ // 2)
            score(NQ - 2, 0)
            score(NQ - 1, 1)

        @block.scalar
        def _(act):
            with act.Fori(0, NQ // 2) as i:
                for par in range(2):
                    n = 2 * i + par
                    act.wait_ge(m["k_turned"], n + 1)
                    act.wait_ge(m["scored"], n + 1)
                    nc.scalar.activation(keyT[:, par], kp[:, 0:P], ACT.Copy).then_inc(m["k_kept"], 1)
                    act.wait_ge(m["w_used"], n + 3)
                    nc.scalar.activation(qT[:, par, 0:SEQ], qp[:], ACT.Copy)
                    nc.scalar.activation(qT[:, par, SEQ:NTOK], qs[:, 0:NS], ACT.Copy).then_inc(m["q_kept"], 1)

        @block.vector
        def _(dve):
            dve.sem_inc(m["sc_free"], 1)
            dve.sem_inc(m["scored"], 2)

            dve.sem_inc(m["moved"], 2)
            eight = lambda x, lo, rows, t: x[0:rows, t, lo:lo + 8]

            with dve.Fori(0, NQ) as n:
                dve.wait_ge(m["scored"], n + 3)
                dve.wait_ge(m["moved"], 4 * n + 2)
                dve.sem_inc(passed, 1)
                for t, rows in TT:
                    nc.vector.max(eight(top, 0, rows, t), place(t)[0:rows, :]).then_inc(m["max1"], 1)
                dve.wait_ge(m["max1"], NT * (n + 1))
                dve.sem_inc(passed, 1)
                for t, rows in TT:
                    nc.vector.max_index(eight(top_at, 0, rows, t), eight(top, 0, rows, t), place(t)[0:rows, :])
                    nc.vector.match_replace(rest[0:rows, t, :], eight(top, 0, rows, t), place(t)[0:rows, :], NEG).then_inc(m["rest1"], 1)
                dve.wait_ge(m["rest1"], NT * (n + 1))
                dve.sem_inc(m["sc_free"], 1)
                for t, rows in TT:
                    nc.vector.max(eight(top, 8, rows, t), rest[0:rows, t, :]).then_inc(m["max2"], 1)
                dve.wait_ge(m["max2"], NT * (n + 1))
                dve.sem_inc(passed, 1)
                for t, rows in TT:
                    nc.vector.max_index(eight(top_at, 8, rows, t), eight(top, 8, rows, t), rest[0:rows, t, :]).then_inc(m["done"], 1)
                dve.wait_ge(m["done"], NT * (n + 1))


def choose(nc, a, c, best, best_at, idxT, gateT):
    PH, K = HEADS, 16
    with ExitStack() as ctx:
        s = Shop(nc, ctx, "choose")
        passed = s.sem("passed")
        cand, left = s.sb("cand", [P, PH, K * K]), s.sb("left", [P, PH, K * K])
        at = s.sb("at", [P, PH * 2 * K])
        score, pos = s.sb("score", [P, PH * K]), s.sb("pos", [P, PH * K], U32)
        digit, dig = s.sb("digit", [P, 2, PH * K], U32), s.sb("dig", [P, 2, PH * K])
        opt = s.sb("opt", [P, K])
        opt_i = s.sb("opt_i", [P, K], I32)
        hit = s.sb("hit", [P, PH * K, K])
        number = s.sb("number", [P, 3, PH * K])
        gate, total, share = s.sb("gate", [P, PH * K]), s.sb("total", [P, 2, PH]), s.sb("share", [P, PH * K])
        gt, nt = s.ps("gt", [P, HALF]), s.ps("nt", [P, HALF])
        m = {x: s.sem(x) for x in "iota step exp_in exp_done turn turned kept".split()}
        block = ctx.enter_context(nc.Block())
        NT = PT + 1

        @block.gpsimd
        def _(pool):
            nc.gpsimd.iota(opt_i[:], pattern=[[1, K]], base=0, channel_multiplier=0).then_inc(m["iota"], 1)

        @block.tensor
        def _(pe):
            def turn(t, rows):
                pe.wait_ge(m["turn"], t + 1)
                nc.tensor.transpose(gt[:, 0:rows], share[0:rows, :], c.ident[0:rows, 0:rows])
                nc.tensor.transpose(nt[:, 0:rows], number[0:rows, 2, :], c.ident[0:rows, 0:rows]).then_inc(m["turned"], 1)

            with pe.Fori(0, PT) as t:
                turn(t, P)
            turn(PT, NS)

        @block.scalar
        def _(act):
            def go(t, rows):
                act.wait_ge(m["exp_in"], t + 1)
                nc.scalar.activation(gate[0:rows, :], gate[0:rows, :], ACT.Exp).then_inc(m["exp_done"], 1)
                act.wait_ge(m["turned"], t + 1)
                nc.scalar.activation(gateT[:, cols(t, rows)], gt[:, 0:rows], ACT.Copy)
                nc.scalar.activation(idxT[:, cols(t, rows)], nt[:, 0:rows], ACT.Copy).then_inc(m["kept"], 1)

            with act.Fori(0, PT) as t:
                go(t, P)
            go(PT, NS)

        @block.vector
        def _(dve):
            base, n = [0], [0]

            def then(*ins):
                for x in ins:
                    x.then_inc(m["step"], 1)
                    n[0] += 1
                dve.wait_ge(m["step"], base[0] + n[0])
                dve.sem_inc(passed, 1)

            def choose_tile(t, rows):
                r = slice(0, rows)
                b = best[r, bass.ds(t, 1), :].rearrange("p a (h s k) -> p (a h) s k", s=2, k=K)
                then(nc.vector.tensor_copy(at[r, :], best_at[r, bass.ds(t, 1), :].rearrange("p a n -> p (a n)")))
                cv = cand[r].rearrange("p h (i j) -> p h i j", i=K)
                then(nc.vector.tensor_tensor(cv, b[:, :, 0, :].unsqueeze(3).to_broadcast((rows, PH, K, K)),
                                             b[:, :, 1, :].unsqueeze(2).to_broadcast((rows, PH, K, K)), ALU.add))
                v8 = lambda x, h, lo: x[r, h * K + lo:h * K + lo + 8]
                then(*[nc.vector.max(v8(score, h, 0), cand[r, h]) for h in range(PH)])
                for h in range(PH):
                    nc.vector.max_index(v8(pos, h, 0), v8(score, h, 0), cand[r, h])
                then(*[nc.vector.match_replace(left[r, h], v8(score, h, 0), cand[r, h], NEG) for h in range(PH)])
                then(*[nc.vector.max(v8(score, h, 8), left[r, h]) for h in range(PH)])
                then(*[nc.vector.max_index(v8(pos, h, 8), v8(score, h, 8), left[r, h]) for h in range(PH)])
                sv = score[r].rearrange("p (h k) -> p h k", k=K)
                gv = gate[r].rearrange("p (h k) -> p h k", k=K)
                nc.vector.tensor_tensor(gv, sv, sv[:, :, 0:1].to_broadcast((rows, PH, K)), ALU.subtract).then_inc(m["exp_in"], 1)
                then(nc.vector.tensor_single_scalar(digit[r, 0], pos[r], 4, ALU.logical_shift_right),
                     nc.vector.tensor_single_scalar(digit[r, 1], pos[r], K - 1, ALU.bitwise_and))
                then(nc.vector.tensor_copy(dig[r], digit[r]))
                av = at[r].rearrange("p (h s k) -> p h s k", s=2, k=K)
                for side in range(2):
                    h4 = hit[r].rearrange("p (h q) k -> p h q k", q=K)
                    then(nc.vector.tensor_tensor(hit[r], dig[r, side].unsqueeze(2).to_broadcast((rows, PH * K, K)),
                                                 opt[r].unsqueeze(1).to_broadcast((rows, PH * K, K)), ALU.is_equal))
                    then(nc.vector.tensor_tensor(h4, h4, av[:, :, side, :].unsqueeze(2).to_broadcast((rows, PH, K, K)), ALU.mult))
                    then(nc.vector.tensor_reduce(number[r, side], hit[r], AX.X, ALU.add))
                nc.vector.scalar_tensor_tensor(out=number[r, 2], in0=number[r, 0], scalar=float(P), in1=number[r, 1],
                                               op0=ALU.mult, op1=ALU.add)
                dve.wait_ge(m["exp_done"], t + 1)
                then(nc.vector.tensor_reduce(total[r, 0], gv, AX.X, ALU.add))
                then(nc.vector.reciprocal(total[r, 1], total[r, 0]))
                shv = share[r].rearrange("p (h k) -> p h k", k=K)
                nc.vector.tensor_tensor(shv, gv, total[r, 1].unsqueeze(2).to_broadcast((rows, PH, K)), ALU.mult).then_inc(m["turn"], 1)
                dve.wait_ge(m["turned"], t + 1)
                return n[0]

            dve.wait_ge(m["iota"], 1)
            nc.vector.memset(idxT[:, NTOK:], 0)
            then(nc.vector.tensor_copy(opt[:], opt_i[:]))
            per = PH * 4 + 13
            with dve.Fori(0, PT) as t:
                base[0], n[0] = t * per + 1, 0
                done = choose_tile(t, P)
                assert done == per, (done, per)
            base[0], n[0] = PT * per + 1, 0
            choose_tile(PT, NS)


TB = 32
U_SLOTS = 8
V_SLOTS = 8
XB_SLOTS = 2


def expert_stage(nc, idxT, gateT, x_parts, x_res, expert_u, expert_v, g_final, y_prompt, y_sample):
    N_TOK, D = x_res.shape
    NB = N_TOK // TB
    LOOPS = (NB - 1) // 2
    assert NB % 2 == 1 and y_prompt.shape[0] == (NB - 1) * TB and y_sample.shape[0] == TB
    U_USES, V_USES = TB // U_SLOTS, TB // V_SLOTS
    HALVES = [slice(h, h + HALF) for h in range(0, D, HALF)]
    with ExitStack() as ctx:
        shop = Shop(nc, ctx, "expert_stage")
        passed = shop.sem("passed")
        sb, sem = shop.sb, shop.sem
        ps = shop.ps
        u_rows = sb("u_rows", [P, U_SLOTS, D], F32)
        v_rows = sb("v_rows", [P, V_SLOTS, D], F32)
        idx_u = [sb(f"idx_u{i}", [P, TB], I32) for i in range(2)]
        idx_v = [sb(f"idx_v{i}", [P, TB], I32) for i in range(2)]
        parts = sb("parts", [3 * TB, 2, D], BF16)
        resid = sb("resid", [TB, 2, D], F32)
        pick = sb("pick", [3 * TB, TB, P], BF16)
        eye = sb("eye", [P, TB, TB], F32)
        dots = sb("dots", [P, TB], F32)
        acts = sb("acts", [P, TB], F32)
        wts = sb("wts", [P, TB], F32)
        w_diag = sb("w_diag", [P, 2, TB, TB], F32)
        x_out = sb("x_out", [TB, D], F32)
        squares = sb("y_squares", [TB, D], F32)
        y_out = sb("y_out", [TB, D], F32)
        stat = sb("y_stat", [TB, 4], F32)
        gfin = sb("gfin", [TB, D], F32)
        xb = ps("xb", [P, XB_SLOTS, D])
        acc = ps("y_acc", [TB, 2, D])

        u_landed = [sem(f"u_landed{i}") for i in range(U_SLOTS)]
        v_landed = [sem(f"v_landed{i}") for i in range(V_SLOTS)]
        parts_landed = [sem(f"parts_landed{i}") for i in range(2)]
        resid_landed = [sem(f"resid_landed{i}") for i in range(2)]
        gfin_landed, out_landed = sem("gfin_landed"), sem("out_landed")
        const_ready = sem("const_ready")
        idx_u_ready, idx_v_ready = sem("idx_u_ready"), sem("idx_v_ready")
        xb_ready, dot_done, v_free = sem("xb_ready"), sem("dot_done"), sem("v_free")
        gelu_done, w_ready, acc_read = sem("gelu_done"), sem("w_ready"), sem("acc_read")
        wts_ready, sq_done, ms_done, rt_done, rinv_ready = (
            sem("wts_ready"), sem("sq_done"), sem("ms_done"), sem("rt_done"), sem("rinv_ready"))
        y_ready, y_free = sem("y_ready"), sem("y_free")

        block = ctx.enter_context(nc.Block())

        @block.gpsimd
        def _(pool):
            nc.gpsimd.memset(pick[:], 0.0).then_inc(const_ready, 1)
            nc.gpsimd.memset(eye[:], 0.0).then_inc(const_ready, 1)
            pool.wait_ge(const_ready, 2)
            for part in range(3):
                nc.gpsimd.affine_select(out=pick[:], in_=pick[:], compare_op=ALU.not_equal, fill=1.0,
                                        base=-TB * part, pattern=[[-1, TB], [0, P]],
                                        channel_multiplier=1).then_inc(const_ready, 1)
                pool.wait_ge(const_ready, 3 + part)
            nc.gpsimd.affine_select(out=eye[:], in_=eye[:], compare_op=ALU.not_equal, fill=1.0, base=0,
                                    pattern=[[1, TB], [-1, TB]], channel_multiplier=0).then_inc(const_ready, 1)
            pool.sem_inc(v_free, V_SLOTS)

            def gather_u(b, t, par):
                if t == 0:
                    pool.wait_ge(idx_u_ready, b + 1)
                if not isinstance(b, int) or TB * b + t >= U_SLOTS:
                    pool.wait_ge(dot_done, TB * b + t - U_SLOTS + 1)
                pool.sem_inc(passed, 1)
                nc.gpsimd.indirect_dma_start(
                    u_rows[:, t % U_SLOTS, :], None, expert_u,
                    bass.IndirectOffsetOnAxis(ap=idx_u[par][:, t:t + 1], axis=0)).then_inc(u_landed[t % U_SLOTS], 16)

            def gather_v(b, t, par):
                if t == 0:
                    pool.wait_ge(idx_v_ready, b + 1)
                pool.wait_ge(v_free, TB * b + t + 1)
                pool.sem_inc(passed, 1)
                nc.gpsimd.indirect_dma_start(
                    v_rows[:, t % V_SLOTS, :], None, expert_v,
                    bass.IndirectOffsetOnAxis(ap=idx_v[par][:, t:t + 1], axis=0)).then_inc(v_landed[t % V_SLOTS], 16)

            for t in range(TB):
                gather_u(0, t, 0)
            with pool.Fori(0, LOOPS) as i:
                for odd in range(2):
                    for t in range(TB):
                        gather_u(2 * i + 1 + odd, t, 1 - odd)
                        gather_v(2 * i + odd, t, odd)
            for t in range(TB):
                gather_v(NB - 1, t, 0)

        @block.sync
        def _(sp):
            sp.sem_inc(y_free, 1)
            sp.dma_start(gfin[:], g_final.unsqueeze(0).to_broadcast((TB, D))).then_inc(gfin_landed, 16)

            def load_parts(b, par):
                for part in range(3):
                    sp.dma_start(parts[part * TB:(part + 1) * TB, par, :],
                                 x_parts[part, bass.ds(b * TB, TB), :]).then_inc(parts_landed[par], 16)

            def load_resid(b, par):
                sp.dma_start(resid[:, par, :], x_res[bass.ds(b * TB, TB), :]).then_inc(resid_landed[par], 16)

            def store(b, rows):
                sp.wait_ge(y_ready, b + 1)
                sp.dma_start(rows, y_out[:]).then_inc(out_landed, 16)
                sp.wait_ge(out_landed, 16 * b + 16)
                sp.sem_inc(y_free, 1)

            load_parts(0, 0)
            load_resid(0, 0)
            load_parts(1, 1)
            load_resid(1, 1)
            with sp.Fori(0, LOOPS - 1) as i:
                for odd in range(2):
                    sp.wait_ge(dot_done, TB * (2 * i + 1 + odd))
                    load_parts(2 * i + 2 + odd, odd)
                    store(2 * i + odd, y_prompt[bass.ds((2 * i + odd) * TB, TB), :])
                    load_resid(2 * i + 2 + odd, odd)
            b = NB - 3
            sp.wait_ge(dot_done, TB * (b + 1))
            load_parts(b + 2, 0)
            store(b, y_prompt[b * TB:(b + 1) * TB, :])
            load_resid(b + 2, 0)
            store(b + 1, y_prompt[(b + 1) * TB:(b + 2) * TB, :])
            store(b + 2, y_sample)

        @block.tensor
        def _(pe):
            def broadcast(b, t, par, loads):
                if t == 0:
                    pe.wait_ge(parts_landed[par], 48 * loads)
                if not isinstance(b, int) or TB * b + t >= XB_SLOTS:
                    pe.wait_ge(dot_done, TB * b + t - XB_SLOTS + 1)
                for half in HALVES:
                    last = nc.tensor.matmul(xb[:, t % XB_SLOTS, half], pick[:, t, :], parts[:, par, half],
                                            start=True, stop=True)
                last.then_inc(xb_ready, 1)

            def combine(b, t, par):
                if t == 0:
                    pe.wait_ge(w_ready, b + 1)
                    pe.wait_ge(acc_read, b + 1)
                pe.wait_ge(v_landed[t % V_SLOTS], 16 * (V_USES * b + t // V_SLOTS + 1))
                for half in HALVES:
                    last = nc.tensor.matmul(acc[:, par, half], w_diag[:, par, t, :], v_rows[:, t % V_SLOTS, half],
                                            start=(t == 0), stop=(t == TB - 1))
                last.then_inc(v_free, 1)

            pe.wait_ge(const_ready, 6)
            for t in range(TB):
                broadcast(0, t, 0, 1)
            with pe.Fori(0, LOOPS) as i:
                for odd in range(2):
                    for t in range(TB):
                        broadcast(2 * i + 1 + odd, t, 1 - odd, i + 1 + odd)
                        combine(2 * i + odd, t, odd)
            for t in range(TB):
                combine(NB - 1, t, 0)

        @block.scalar
        def _(act):
            def gelu(b):
                act.wait_ge(dot_done, TB * b + TB)
                nc.scalar.activation(acts[:], dots[:], ACT.Gelu_apprx_tanh).then_inc(gelu_done, 1)

            def norm(b):
                act.wait_ge(acc_read, b + 3)
                nc.scalar.activation(squares[:], x_out[:], ACT.Square, accum_out=stat[:, 0:1]).then_inc(sq_done, 1)
                act.wait_ge(ms_done, b + 1)
                nc.scalar.activation(stat[:, 2:3], stat[:, 1:2], ACT.Sqrt).then_inc(rt_done, 1)

            gelu(0)
            with act.Fori(0, LOOPS) as i:
                for odd in range(2):
                    gelu(2 * i + 1 + odd)
                    norm(2 * i + odd)
            norm(NB - 1)

        @block.vector
        def _(dve):
            def indices_u(b, par):
                nc.vector.tensor_copy(idx_u[par][:], idxT[:, bass.ds(b * TB, TB)]).then_inc(idx_u_ready, 1)

            def indices_v(b, par):
                nc.vector.tensor_copy(idx_v[par][:], idxT[:, bass.ds(b * TB, TB)]).then_inc(idx_v_ready, 1)

            def dot(b, t):
                dve.wait_ge(u_landed[t % U_SLOTS], 16 * (U_USES * b + t // U_SLOTS + 1))
                dve.wait_ge(xb_ready, TB * b + t + 1)
                nc.vector.tensor_tensor_reduce(
                    out=u_rows[:, t % U_SLOTS, :], in0=u_rows[:, t % U_SLOTS, :], in1=xb[:, t % XB_SLOTS, :],
                    scale=1.0, scalar=0.0, op0=ALU.mult, op1=ALU.add, accum_out=dots[:, t:t + 1]).then_inc(dot_done, 1)

            def weigh(b, par):
                dve.wait_ge(gelu_done, b + 1)
                nc.vector.tensor_tensor(wts[:], acts[:], gateT[:, bass.ds(b * TB, TB)], ALU.mult).then_inc(wts_ready, 1)
                dve.wait_ge(wts_ready, b + 1)
                nc.vector.tensor_tensor(w_diag[:, par], wts[:].unsqueeze(2).to_broadcast((P, TB, TB)), eye[:],
                                        ALU.mult).then_inc(w_ready, 1)

            def finish(b, par, loads):
                dve.wait_ge(v_free, V_SLOTS + TB * b + TB)
                dve.wait_ge(resid_landed[par], 16 * loads)
                nc.vector.tensor_tensor(x_out[:], acc[:, par, :], resid[:, par, :], ALU.add).then_inc(acc_read, 1)
                dve.wait_ge(sq_done, b + 1)
                nc.vector.tensor_scalar(stat[:, 1:2], stat[:, 0:1], 1.0 / D, EPS, ALU.mult, ALU.add).then_inc(ms_done, 1)
                dve.wait_ge(rt_done, b + 1)
                nc.vector.reciprocal(stat[:, 3:4], stat[:, 2:3]).then_inc(rinv_ready, 1)
                dve.wait_ge(rinv_ready, b + 1)
                dve.wait_ge(y_free, b + 1)
                nc.vector.scalar_tensor_tensor(out=y_out[:], in0=x_out[:], scalar=stat[:, 3:4], in1=gfin[:],
                                               op0=ALU.mult, op1=ALU.mult).then_inc(y_ready, 1)
                dve.wait_ge(y_ready, b + 1)

            dve.sem_inc(acc_read, 2)
            dve.wait_ge(const_ready, 6)
            dve.wait_ge(gfin_landed, 16)
            indices_u(0, 0)
            indices_u(1, 1)
            indices_v(0, 0)
            for t in range(TB):
                dot(0, t)
            weigh(0, 0)
            with dve.Fori(0, LOOPS) as i:
                for odd in range(2):
                    indices_u(2 * i + 2 + odd, odd)
                    indices_v(2 * i + 1 + odd, 1 - odd)
                    for t in range(TB):
                        dot(2 * i + 1 + odd, t)
                    weigh(2 * i + 1 + odd, 1 - odd)
                    finish(2 * i + odd, odd, i + 1)
            finish(NB - 1, 0, LOOPS + 1)


class Consts:
    OLD = (PAST - HALF) // 16
    SK = HALF + DT * OLD


def program(nc, a, dbg=None):
    c = Consts()
    with ExitStack() as ctx:
        s = Shop(nc, ctx, "program")
        c.ident, c.ones = s.sb("ident", [P, P]), s.sb("ones", [P, P])
        c.par, c.coef = s.sb("par", [P, CC, N_ROWS]), s.sb("coef", [P, 2, CC])
        c.g_mix, c.g_ffn = s.sb("g_mix_T", [P, KC]), s.sb("g_ffn_T", [P, KC])
        x_res = nc.dram_tensor("x_res", (NTOK, D), F32, kind="Internal").ap()
        x_parts = nc.dram_tensor("x_parts", (3, NTOK, D), BF16, kind="Internal").ap()
        xT = s.sb("xT", [P, KC, NTOK])
        with ExitStack() as ctx2:
            s2 = Shop(nc, ctx2, "program")
            c.mult, c.bias = s2.sb("mult", [P, SEQ]), s2.sb("bias", [P, SEQ])
            c.s_mult, c.s_bias = s2.sb("s_mult", [NS, 2, c.SK + NS]), s2.sb("s_bias", [NS, 2, c.SK + NS])
            c.n_mult, c.n_bias = s2.sb("n_mult", [NS, DB, NS]), s2.sb("n_bias", [NS, DB, NS])
            zT, v_tok = s2.sb("zT", [P, 4 * CC, NTOK]), s2.sb("v_tok", [P, PT + 1, DR])
            with ExitStack() as ctx3:
                s3 = Shop(nc, ctx3, "program")
                c.wgate = s3.sb("wgate", [P, 2, CC, P])
                constants(nc, a, c)
                normed_T(nc, a, c, xT)
                project(nc, a, c, xT, zT, v_tok)
            if dbg:
                dbg(nc, 1, locals())
            y_tok, ysT = s2.sb("y_tok", [P, PT, DR]), s2.sb("ysT", [P, CC, NS])
            attend_prompt(nc, a, c, zT, v_tok, y_tok)
            attend_sample(nc, a, c, zT, v_tok, ysT, xT)
            if dbg:
                dbg(nc, 2, locals())
            merge(nc, a, c, zT, y_tok, ysT, xT, x_res, x_parts)
        if dbg:
            dbg(nc, 3, locals())
        idxT, gateT = s.sb("idxT", [P, NTOK + TB], I32), s.sb("gateT", [P, NTOK])
        with ExitStack() as ctx2:
            s2 = Shop(nc, ctx2, "program")
            best, best_at = s2.sb("best", [P, PT + 1, 2 * HEADS * 16]), s2.sb("best_at", [P, PT + 1, 2 * HEADS * 16], U32)
            route(nc, a, c, xT, best, best_at)
            choose(nc, a, c, best, best_at, idxT, gateT)
        if dbg:
            dbg(nc, 4, locals())
        expert_stage(nc, idxT, gateT, x_parts, x_res, a["expert_u"][0], a["expert_v"][0], a["g_final"],
                     a["y_prompt"], a["y_sample"])


_OUTS = [((1, SEQ, D), 'y_prompt'), ((DB, DT, D), 'y_sample'),
         ((1, 1, SEQ, HEADS, HD), 'k_prompt'), ((1, 1, SEQ, HEADS, HD), 'v_prompt'),
         ((1, DB, DT, HEADS, HD), 'k_sample'), ((1, DB, DT, HEADS, HD), 'v_sample'),
         ((1, 1, CW - 1, DR), 'conv_prompt'), ((1, DB, CW - 1, DR), 'conv_sample'),
         ((1, 1, DR), 'h_prompt'), ((1, DB, DR), 'h_sample')]


def rows_of(ap):
    n = len(ap.shape)
    if n == 5:
        return ap.rearrange("a b t h e -> (a b t) (h e)")
    if n == 4:
        return ap.rearrange("a b t e -> (a b t) e")
    return ap.rearrange("a b e -> (a b) e")


def kernel(**inputs):
    import numpy as _np
    import concourse.bacc as _bacc
    from concourse.bass_utils import run_bass_kernel_spmd as _run

    nc = _bacc.Bacc("TRN2", target_bir_lowering=False, num_devices=1)
    arrays, a = {}, {}
    for name, x in inputs.items():
        arrays[name] = _np.ascontiguousarray(x)
        a[name] = nc.dram_tensor(name, arrays[name].shape, mybir.dt.from_np(arrays[name].dtype), kind="ExternalInput").ap()
    for shape, name in _OUTS:
        a[name] = rows_of(nc.dram_tensor("out_" + name, shape, F32, kind="ExternalOutput").ap())
    program(nc, a)
    r = _run(nc, [arrays], core_ids=[0])
    return tuple(r.results[0]["out_" + name] for _, name in _OUTS)
```

```python
from contextlib import ExitStack

import concourse.bass as bass
from concourse import mybir

F32, BF16, I32, U32 = mybir.dt.float32, mybir.dt.bfloat16, mybir.dt.int32, mybir.dt.uint32
ALU, ACT, AX = mybir.AluOpType, mybir.ActivationFunctionType, mybir.AxisListType
EPS = 1e-6
P = 128
HALF = 512
D = 1024
KC = D // P
DR = 512
CC = DR // P
SEQ, DB, DT = 1024, 8, 4
NS = DB * DT
NTOK = SEQ + NS
PT = SEQ // P
PAST = 2048
HEADS, HD = 8, 64
LRU_C = 8.0
CW = 4
NEG = -1e30
SCALE = HD ** -0.5
NARROW = [(0, HALF), (HALF, 2 * HALF)]
TILES = [(t, P) for t in range(PT)] + [(PT, NS)]

R_CONVW, R_CONVB, R_BA, R_BX, R_LAM, R_GRNN, R_GATT, R_GMIX, R_GFFN, R_SCONV = 0, 4, 5, 6, 7, 8, 9, 10, 12, 14
R_SH = R_SCONV + DB * (CW - 1)
N_ROWS = R_SH + DB


class Shop:

    def __init__(self, nc, ctx, stage):
        self.nc, self.ctx, self.stage, self.sems = nc, ctx, stage, []
        ctx.callback(self.close)

    def close(self):
        for held, sem in self.sems:
            self.nc.sync.sem_clear(sem)
        if self.sems:
            self.nc.all_engine_barrier()
        for held, sem in self.sems:
            held.__exit__(None, None, None)

    def sb(self, name, shape, dt=F32):
        return self.ctx.enter_context(self.nc.sbuf_tensor(name, shape, dt))

    def ps(self, name, shape):
        return self.ctx.enter_context(self.nc.psum_tensor(name, shape, F32))

    def sem(self, name):
        held = self.nc.semaphore(f"{self.stage}_{name}")
        self.sems.append((held, held.__enter__()))
        return self.sems[-1][1]


def cols(tile, rows=P):
    return bass.ds(tile * P, rows)


def constants(nc, a, c):
    with ExitStack() as ctx:
        s = Shop(nc, ctx, "constants")
        table = s.sb("table", [N_ROWS, DR])
        turned = s.ps("turned", [P, CC, 64])
        delta = s.sb("delta", [P, SEQ], I32)
        bits = s.sb("bits", [P, SEQ], I32)
        deltaf = s.sb("deltaf", [P, SEQ])
        term = s.sb("term", [P, SEQ])
        w1, w2, w3 = s.sb("w1", [P, CC]), s.sb("w2", [P, CC]), s.sb("w3", [P, CC])
        rows_landed, blocks_landed = s.sem("rows_landed"), s.sem("blocks_landed")
        zeroed, pool_step, turned_ready, params_ready = (
            s.sem("zeroed"), s.sem("pool_step"), s.sem("turned_ready"), s.sem("params_ready"))
        exp_done, step = s.sem("exp_done"), s.sem("step")
        iota_ready = s.sem("iota_ready")
        jrow = s.sb("jrow", [NS, 2], I32)
        jf = s.sb("jf", [NS, 1])
        sdel = s.sb("sdel", [NS, c.SK], I32)
        sbit = s.sb("sbit", [NS, c.SK], I32)
        sdelf = s.sb("sdelf", [NS, c.SK])
        sterm = s.sb("sterm", [NS, c.SK])
        ndel = s.sb("ndel", [NS, DB, NS], I32)
        nbit = s.sb("nbit", [NS, DB, NS], I32)
        ndelf = s.sb("ndelf", [NS, DB, NS])
        nterm = s.sb("nterm", [NS, DB, NS])
        block = ctx.enter_context(nc.Block())

        @block.sync
        def _(sp):
            rows = [(R_CONVW, a["conv_w"][0]), (R_CONVB, a["conv_b"]), (R_BA, a["b_a"]), (R_BX, a["b_x"]),
                    (R_LAM, a["lru_lambda"]), (R_GRNN, a["g_rnn_out"]), (R_GATT, a["g_attn_out"]),
                    (R_GMIX, a["g_mix"][0].rearrange("(r e) -> r e", e=DR)),
                    (R_GFFN, a["g_ffn"][0].rearrange("(r e) -> r e", e=DR)),
                    (R_SCONV, a["state_conv"][0].rearrange("b w e -> (b w) e")), (R_SH, a["state_h"][0])]
            for r, src in rows:
                sp.dma_start(table[r:r + src.shape[0], :], src).then_inc(rows_landed, 16)
            sp.wait_ge(zeroed, 1)
            for g, w in enumerate(("w_a", "w_x")):
                for half in range(2):
                    sp.dma_start(c.wgate[64 * half:64 * half + 64, g, :, 64 * half:64 * half + 64],
                                 a[w][0].rearrange("(t two) i o -> two i t o", two=2)[half]).then_inc(blocks_landed, 16)
            sp.wait_ge(blocks_landed, 64)

        @block.gpsimd
        def _(pool):
            nc.gpsimd.memset(c.wgate[:], 0.0).then_inc(zeroed, 1)
            nc.gpsimd.memset(c.ident[:], 0.0).then_inc(pool_step, 1)
            nc.gpsimd.memset(c.ones[:], 1.0).then_inc(pool_step, 1)
            pool.wait_ge(pool_step, 2)
            nc.gpsimd.affine_select(out=c.ident[:], in_=c.ident[:], compare_op=ALU.not_equal, fill=1.0, base=0,
                                    pattern=[[-1, P]], channel_multiplier=1).then_inc(pool_step, 1)
            nc.gpsimd.iota(delta[:], pattern=[[-1, SEQ]], base=SEQ - P, channel_multiplier=1).then_inc(iota_ready, 1)
            nc.gpsimd.iota(jrow[:, 0:1], pattern=[[0, 1]], base=0, channel_multiplier=1).then_inc(iota_ready, 1)
            nc.gpsimd.iota(sdel[:, 0:HALF], pattern=[[-1, 4], [-4, P]], base=HALF,
                           channel_multiplier=0).then_inc(iota_ready, 1)
            nc.gpsimd.iota(sdel[:, HALF:c.SK], pattern=[[-1, 4], [-16, c.OLD]], base=PAST,
                           channel_multiplier=0).then_inc(iota_ready, 1)
            nc.gpsimd.iota(ndel[:], pattern=[[4, DB], [-1, NS]], base=0, channel_multiplier=0).then_inc(iota_ready, 1)

        @block.tensor
        def _(pe):
            pe.wait_ge(rows_landed, 16 * 11)
            pe.wait_ge(pool_step, 3)
            for t in range(CC):
                last = nc.tensor.transpose(turned[:, t, 0:N_ROWS], table[:, t * P:(t + 1) * P], c.ident[0:N_ROWS, 0:N_ROWS])
            last.then_inc(turned_ready, 1)

        @block.scalar
        def _(act):
            act.wait_ge(params_ready, 1)
            act.wait_ge(step, 1)
            nc.scalar.activation(w2[:], w1[:], ACT.Exp, scale=-1.0).then_inc(exp_done, 1)

        @block.vector
        def _(dve):
            n = [0]

            def then(ins):
                n[0] += 1
                ins.then_inc(step, 1)
                dve.wait_ge(step, n[0])

            dve.wait_ge(turned_ready, 1)
            nc.vector.tensor_copy(c.par[:, :, 0:N_ROWS], turned[:, :, 0:N_ROWS]).then_inc(params_ready, 1)
            dve.wait_ge(params_ready, 1)
            lam = c.par[:, :, R_LAM]
            then(nc.vector.scalar_tensor_tensor(out=w1[:], in0=lam, scalar=-1.0, in1=lam, op0=ALU.mult, op1=ALU.max))
            dve.wait_ge(exp_done, 1)
            then(nc.vector.tensor_scalar(w3[:], w2[:], 2.0, None, ALU.add))
            then(nc.vector.reciprocal(w1[:], w3[:]))
            then(nc.vector.tensor_tensor(w2[:], w2[:], w1[:], ALU.mult))
            then(nc.vector.tensor_tensor(w3[:], w2[:], w2[:], ALU.mult))
            then(nc.vector.tensor_scalar(w1[:], w3[:], 1.0 / 17, 1.0 / 15, ALU.mult, ALU.add))
            for k in (13, 11, 9, 7, 5, 3, 1):
                then(nc.vector.tensor_tensor(w1[:], w1[:], w3[:], ALU.mult))
                then(nc.vector.tensor_scalar(w1[:], w1[:], 1.0 / k, None, ALU.add))
            then(nc.vector.tensor_tensor(w1[:], w1[:], w2[:], ALU.mult))
            then(nc.vector.tensor_scalar(w3[:], lam, -1.0, 0.0, ALU.mult, ALU.max))
            then(nc.vector.scalar_tensor_tensor(out=w3[:], in0=w1[:], scalar=2.0, in1=w3[:], op0=ALU.mult, op1=ALU.add))
            then(nc.vector.tensor_scalar(c.coef[:, 0, :], w3[:], -LRU_C, None, ALU.mult))
            then(nc.vector.tensor_scalar(c.coef[:, 1, :], w3[:], LRU_C, None, ALU.mult))
            for g, r in ((c.g_mix, R_GMIX), (c.g_ffn, R_GFFN)):
                then(nc.vector.tensor_copy(g[:].rearrange("p (r t) -> p r t", t=CC),
                                           c.par[:, :, r:r + 2].rearrange("p t r -> p r t")))

            dve.wait_ge(iota_ready, 5)

            def multiplicity(di, df, bi, tm, out):
                then(nc.vector.tensor_copy(df, di))
                then(nc.vector.tensor_scalar(out, df, 128.0, None, ALU.is_le))
                for dil, win in ((4, 512.0), (16, 2048.0)):
                    then(nc.vector.tensor_single_scalar(bi, di, dil - 1, ALU.bitwise_and))
                    then(nc.vector.tensor_copy(tm, bi))
                    then(nc.vector.tensor_single_scalar(tm, tm, 0.0, ALU.is_equal))
                    then(nc.vector.scalar_tensor_tensor(out=tm, in0=df, scalar=win, in1=tm, op0=ALU.is_le, op1=ALU.mult))
                    then(nc.vector.tensor_tensor(out, out, tm, ALU.add))
                then(nc.vector.scalar_tensor_tensor(out=out, in0=df, scalar=0.0, in1=out, op0=ALU.is_ge, op1=ALU.mult))

            def bias_of(bias, mult):
                then(nc.vector.tensor_scalar(bias, mult, 0.0, NEG, ALU.is_equal, ALU.mult))

            multiplicity(delta[:], deltaf[:], bits[:], term[:], c.mult[:])
            bias_of(c.bias[:], c.mult[:])
            then(nc.vector.tensor_single_scalar(jrow[:, 1:2], jrow[:, 0:1], DT - 1, ALU.bitwise_and))
            then(nc.vector.tensor_copy(jf[:], jrow[:, 1:2]))
            for di, df, bi, tm, out in ((sdel[:], sdelf[:], sbit[:], sterm[:], c.s_mult[:, 0, 0:c.SK]),
                                        (ndel[:], ndelf[:], nbit[:], nterm[:], c.n_mult[:])):
                then(nc.vector.tensor_copy(df, di))
                then(nc.vector.tensor_scalar(df, df, jf[:, 0:1], None, ALU.add))
                then(nc.vector.tensor_copy(di, df))
                multiplicity(di, df, bi, tm, out)
            then(nc.vector.tensor_scalar(nterm[:], ndelf[:], jf[:, 0:1], None, ALU.is_le))
            then(nc.vector.tensor_tensor(c.n_mult[:], c.n_mult[:], nterm[:], ALU.mult))
            bias_of(c.s_bias[:, 0, 0:c.SK], c.s_mult[:, 0, 0:c.SK])
            for x in (c.s_bias, c.s_mult):
                then(nc.vector.tensor_copy(x[:, 1, 0:c.SK], x[:, 0, 0:c.SK]))
            bias_of(c.n_bias[:], c.n_mult[:])


def normed_T(nc, a, c, xnT):
    with ExitStack() as ctx:
        s = Shop(nc, ctx, "normed_T")
        x_in = s.sb("x_in", [P, 2, D])
        xn = s.sb("xn", [P, 2, D])
        squares = s.sb("squares", [P, D])
        stat = s.sb("stat", [P, 2, 4])
        tp = [s.ps(f"tp{i}", [P, KC, P]) for i in range(2)]
        x_landed = [s.sem(f"x_landed{i}") for i in range(2)]
        x_used, xn_used, tp_used = s.sem("x_used"), s.sem("xn_used"), s.sem("tp_used")
        sq_done, ms_ready, rt_done, rinv_ready = s.sem("sq_done"), s.sem("ms_ready"), s.sem("rt_done"), s.sem("rinv_ready")
        block = ctx.enter_context(nc.Block())
        LOOPS = PT // 2

        @block.sync
        def _(sp):
            sp.sem_inc(x_used, 2)

            def load(t, par, src, rows=P):
                sp.wait_ge(x_used, t + 1)
                sp.dma_start(x_in[0:rows, par, :], src).then_inc(x_landed[par], 16)

            with sp.Fori(0, LOOPS) as i:
                for par in range(2):
                    load(2 * i + par, par, a["x_prompt"][0, cols(2 * i + par), :])
            load(PT, 0, a["x_sample"].rearrange("b t d -> (b t) d"), NS)

        @block.scalar
        def _(act):
            def norm(t, par, loads, rows=P):
                act.wait_ge(x_landed[par], 16 * loads)
                nc.scalar.activation(squares[0:rows, :], x_in[0:rows, par, :], ACT.Square,
                                     accum_out=stat[0:rows, par, 0:1]).then_inc(sq_done, 1)
                act.wait_ge(ms_ready, t + 1)
                nc.scalar.activation(stat[0:rows, par, 2:3], stat[0:rows, par, 1:2], ACT.Sqrt).then_inc(rt_done, 1)
                act.wait_ge(rinv_ready, t + 1)
                act.wait_ge(xn_used, t + 1)
                nc.scalar.activation(xn[0:rows, par, :], x_in[0:rows, par, :], ACT.Copy,
                                     scale=stat[0:rows, par, 3:4]).then_inc(x_used, 1)
                act.wait_ge(x_used, t + 3)

            with act.Fori(0, LOOPS) as i:
                for par in range(2):
                    norm(2 * i + par, par, i + 1)
            norm(PT, 0, LOOPS + 1, NS)

        @block.tensor
        def _(pe):
            pe.sem_inc(xn_used, 2)

            def turn(t, par, rows=P):
                pe.wait_ge(x_used, t + 3)
                pe.wait_ge(tp_used, t + 1)
                for k in range(KC):
                    last = nc.tensor.transpose(tp[par][:, k, 0:rows], xn[0:rows, par, k * P:(k + 1) * P],
                                               c.ident[0:rows, 0:rows])
                last.then_inc(xn_used, 1)

            with pe.Fori(0, LOOPS) as i:
                for par in range(2):
                    turn(2 * i + par, par)
            turn(PT, 0, NS)

        @block.vector
        def _(dve):
            dve.sem_inc(tp_used, 2)

            def serve(t, par, rows=P):
                dve.wait_ge(sq_done, t + 1)
                nc.vector.tensor_scalar(stat[0:rows, par, 1:2], stat[0:rows, par, 0:1], 1.0 / D, EPS,
                                        ALU.mult, ALU.add).then_inc(ms_ready, 1)
                dve.wait_ge(rt_done, t + 1)
                nc.vector.reciprocal(stat[0:rows, par, 3:4], stat[0:rows, par, 2:3]).then_inc(rinv_ready, 1)
                dve.wait_ge(xn_used, t + 3)
                nc.vector.tensor_tensor(xnT[:, :, cols(t, rows)], tp[par][:, :, 0:rows],
                                        c.g_mix[:].unsqueeze(2).to_broadcast((P, KC, rows)),
                                        ALU.mult).then_inc(tp_used, 1)

            with dve.Fori(0, LOOPS) as i:
                for par in range(2):
                    serve(2 * i + par, par)
            serve(PT, 0, NS)


def project(nc, a, c, xnT, zT, v_tok):
    w_view = a["w_in"][0].rearrange("(k p) n -> p k n", p=P)
    with ExitStack() as ctx:
        s = Shop(nc, ctx, "project")
        w = s.sb("w", [P, 2, KC, P])
        wv = s.sb("wv", [P, KC, DR])
        k_tok = s.sb("k_tok", [P, 2, DR])
        xc, gr, gi, th = s.sb("xc", [P, NTOK]), s.sb("gr", [P, NTOK]), s.sb("gi", [P, NTOK]), s.sb("th", [P, NTOK])
        hist = s.sb("hist", [P, DB, CW - 1 + DT])
        last_in = s.sb("last_in", [P, CC, 36])
        last_rows = s.sb("last_rows", [36, DR])
        zp = [s.ps(f"zp{i}", [P, SEQ]) for i in range(2)]
        zs = [s.ps(f"zs{i}", [P, HALF]) for i in range(2)]
        gp = [s.ps(f"gp{i}", [P, HALF]) for i in range(2)]
        lp = gp[0][0:36, :]
        w_landed = [s.sem(f"w_landed{i}") for i in range(2)]
        wv_landed = s.sem("wv_landed")
        w_used, z_free, z_ready = s.sem("w_used"), s.sem("z_free"), s.sem("z_ready")
        tok_ready, v_done, k_done, v_landed = s.sem("tok_ready"), s.sem("v_done"), s.sem("k_done"), s.sem("v_landed")
        k_landed = [s.sem(f"k_landed{i}") for i in range(2)]
        xc_ready, gates_done, gp_free = s.sem("xc_ready"), s.sem("gates_done"), s.sem("gp_free")
        a_done, gx_ready, sq_done, gelu_done, c_done = (
            s.sem("a_done"), s.sem("gx_ready"), s.sem("sq_done"), s.sem("gelu_done"), s.sem("c_done"))
        step, lp_ready, last_ready, last_landed = s.sem("step"), s.sem("lp_ready"), s.sem("last_ready"), s.sem("last_landed")
        NZ = 4 * CC
        block = ctx.enter_context(nc.Block())

        @block.sync
        def _(sp):
            sp.sem_inc(w_used, 2)
            with sp.Fori(0, NZ // 2) as i:
                for par in range(2):
                    sp.wait_ge(w_used, 2 * i + par + 1)
                    sp.dma_start(w[:, par], w_view[:, :, bass.ds((2 * i + par) * P, P)]).then_inc(w_landed[par], 16)
            sp.dma_start(wv[:], w_view[:, :, NZ * P:]).then_inc(wv_landed, 16)
            for t, rows in TILES:
                sp.wait_ge(k_done, t + 3)
                dst = a["k_prompt"][t * P:(t + 1) * P, :] if t < PT else a["k_sample"]
                sp.dma_start(dst, k_tok[0:rows, t % 2, :]).then_inc(k_landed[t % 2], 16)
            sp.wait_ge(v_done, len(TILES) + 2)
            sp.dma_start(a["v_prompt"].rearrange("(t p) e -> p t e", p=P), v_tok[:, 0:PT, :]).then_inc(v_landed, 16)
            sp.dma_start(a["v_sample"], v_tok[0:NS, PT, :]).then_inc(v_landed, 16)
            sp.wait_ge(last_ready, 1)
            n = DB * (CW - 1)
            sp.dma_start(a["conv_sample"], last_rows[0:n, :]).then_inc(last_landed, 16)
            sp.dma_start(a["conv_prompt"], last_rows[n:n + 3, :]).then_inc(last_landed, 16)
            sp.dma_start(a["h_prompt"], last_rows[n + 3:n + 4, :]).then_inc(last_landed, 16)
            sp.dma_start(a["h_sample"], last_rows[n + 4:n + 12, :]).then_inc(last_landed, 16)
            sp.wait_ge(last_landed, 64)
            sp.wait_ge(v_landed, 32)
            for par in range(2):
                sp.wait_ge(k_landed[par], 16 * len(TILES[par::2]))

        @block.tensor
        def _(pe):
            pe.sem_inc(gp_free, 2)

            def tile(n, par, loads):
                pe.wait_ge(w_landed[par], 16 * loads)
                pe.wait_ge(z_free, n + 1)
                for k in range(KC):
                    for lo, hi in NARROW:
                        nc.tensor.matmul(zp[par][:, lo:hi], w[:, par, k, :], xnT[:, k, lo:hi],
                                         start=(k == 0), stop=(k == KC - 1))
                    last = nc.tensor.matmul(zs[par][:, 0:NS], w[:, par, k, :], xnT[:, k, SEQ:NTOK],
                                            start=(k == 0), stop=(k == KC - 1))
                last.then_inc(w_used, 1)

            def gates(t):
                pe.wait_ge(xc_ready, t + 1)
                n = 0
                for g in range(2):
                    for lo, hi in NARROW + [(SEQ, NTOK)]:
                        pe.wait_ge(gp_free, 6 * t + n + 1)
                        nc.tensor.matmul(gp[n % 2][:, 0:hi - lo], c.wgate[:, g, t, :], xc[:, lo:hi],
                                         start=True, stop=True).then_inc(z_ready, 1)
                        n += 1

            with pe.Fori(0, CC // 2) as i:
                for par in range(2):
                    tile(2 * i + par, par, i + 1)
            for t in range(CC):
                tile(CC + t, t % 2, CC // 2 + t // 2 + 1)
                gates(t)
            with pe.Fori(CC, NZ // 2) as i:
                for par in range(2):
                    tile(2 * i + par, par, i + 1)
            pe.wait_ge(wv_landed, 16)
            pe.wait_ge(z_free, NZ + 2)
            for t, rows in TILES:
                pe.wait_ge(v_done, t + 1)
                pe.wait_ge(k_done, t + 1)
                for k in range(KC):
                    last = nc.tensor.matmul(zp[t % 2][0:rows, 0:DR], xnT[:, k, t * P:t * P + rows], wv[:, k, :],
                                            start=(k == 0), stop=(k == KC - 1))
                for j in range(CC):
                    last = nc.tensor.transpose(zp[t % 2][0:rows, DR + j * P:DR + (j + 1) * P],
                                               zT[:, 3 * CC + j, t * P:t * P + rows], c.ident[:])
                last.then_inc(tok_ready, 1)
            pe.wait_ge(c_done, CC)
            for j in range(CC):
                last = nc.tensor.transpose(lp[:, j * P:(j + 1) * P], last_in[:, j, :], c.ident[:])
            last.then_inc(lp_ready, 1)

        @block.scalar
        def _(act):
            act.sem_inc(z_free, 2)
            act.sem_inc(v_done, 2)

            def keep(n, par):
                act.wait_ge(w_used, n + 3)
                nc.scalar.activation(zT[:, n, 0:SEQ], zp[par][:], ACT.Copy)
                nc.scalar.activation(zT[:, n, SEQ:NTOK], zs[par][:, 0:NS], ACT.Copy).then_inc(z_free, 1)

            def keep_at(i, par):
                n = 2 * i + par
                act.wait_ge(w_used, n + 3)
                nc.scalar.activation(zT[:, bass.ds(n, 1), 0:SEQ].rearrange("p a n -> p (a n)"), zp[par][:],
                                     ACT.Copy)
                nc.scalar.activation(zT[:, bass.ds(n, 1), SEQ:NTOK].rearrange("p a n -> p (a n)"), zs[par][:, 0:NS],
                                     ACT.Copy).then_inc(z_free, 1)

            with act.Fori(0, CC // 2) as i:
                for par in range(2):
                    keep_at(i, par)
            for t in range(CC):
                keep(CC + t, t % 2)
                n = 0
                for g, (buf, row) in enumerate(((gr, R_BA), (gi, R_BX))):
                    for lo, hi in NARROW + [(SEQ, NTOK)]:
                        act.wait_ge(z_ready, 6 * t + n + 1)
                        if t > 0 and n == 0:
                            act.wait_ge(c_done, t)
                        nc.scalar.activation(buf[:, lo:hi], gp[n % 2][:, 0:hi - lo], ACT.Sigmoid,
                                             bias=c.par[:, t, row:row + 1]).then_inc(gp_free, 1)
                        n += 1
                act.wait_ge(gp_free, 6 * t + 8)
                nc.scalar.activation(th[:], gr[:], ACT.Tanh, scale=c.coef[:, 1, t:t + 1]).then_inc(a_done, 1)
                act.wait_ge(a_done, 2 * t + 1)
                nc.scalar.activation(gr[:], gr[:], ACT.Exp, scale=c.coef[:, 0, t:t + 1]).then_inc(a_done, 1)
                act.wait_ge(gx_ready, t + 1)
                nc.scalar.activation(th[:], th[:], ACT.Sqrt).then_inc(sq_done, 1)
                gate = zT[:, CC + t, :]
                act.wait_ge(z_free, CC + t + 3)
                nc.scalar.activation(gate, gate, ACT.Gelu_apprx_tanh).then_inc(gelu_done, 1)
            with act.Fori(CC, NZ // 2) as i:
                for par in range(2):
                    keep_at(i, par)
            for t, rows in TILES:
                act.wait_ge(tok_ready, t + 1)
                nc.scalar.activation(v_tok[0:rows, t, :], zp[t % 2][0:rows, 0:DR], ACT.Copy).then_inc(v_done, 1)

        @block.vector
        def _(dve):
            n = [0]

            def then(ins):
                n[0] += 1
                ins.then_inc(step, 1)
                dve.wait_ge(step, n[0])

            dve.sem_inc(k_done, 2)
            wts = lambda t, j: c.par[:, t, R_CONVW + j:R_CONVW + j + 1]
            for t in range(CC):
                dve.wait_ge(z_free, t + 3)
                xr = zT[:, t, :]
                then(nc.vector.tensor_scalar(xc[:, 0:SEQ], xr[:, 0:SEQ], wts(t, CW - 1), c.par[:, t, R_CONVB:R_CONVB + 1],
                                             ALU.mult, ALU.add))
                for j in range(CW - 2, -1, -1):
                    d = CW - 1 - j
                    then(nc.vector.scalar_tensor_tensor(out=xc[:, d:SEQ], in0=xr[:, 0:SEQ - d], scalar=wts(t, j),
                                                        in1=xc[:, d:SEQ], op0=ALU.mult, op1=ALU.add))
                old = c.par[:, t, R_SCONV:R_SCONV + DB * (CW - 1)].rearrange("p (b w) -> p b w", b=DB)
                new = xr[:, SEQ:NTOK].rearrange("p (b w) -> p b w", b=DB)
                nc.vector.tensor_copy(hist[:, :, 0:CW - 1], old).then_inc(step, 1)
                n[0] += 1
                then(nc.vector.tensor_copy(hist[:, :, CW - 1:], new))
                xs = xc[:, SEQ:NTOK].rearrange("p (b w) -> p b w", b=DB)
                then(nc.vector.tensor_scalar(xs, hist[:, :, CW - 1:CW - 1 + DT], wts(t, CW - 1),
                                             c.par[:, t, R_CONVB:R_CONVB + 1], ALU.mult, ALU.add))
                for j in range(CW - 2, -1, -1):
                    ins = nc.vector.scalar_tensor_tensor(out=xs, in0=hist[:, :, j:j + DT], scalar=wts(t, j), in1=xs,
                                                         op0=ALU.mult, op1=ALU.add)
                    if j:
                        then(ins)
                ins.then_inc(xc_ready, 1)
                nc.vector.tensor_copy(last_in[:, t, 0:24].rearrange("p (b w) -> p b w", b=DB),
                                      new[:, :, DT - (CW - 1):]).then_inc(step, 1)
                nc.vector.tensor_copy(last_in[:, t, 24:27], xr[:, SEQ - 3:SEQ]).then_inc(step, 1)
                n[0] += 2
                dve.wait_ge(a_done, 2 * t + 2)
                sq = zT[:, t, :]
                dve.wait_ge(step, n[0])
                then(nc.vector.tensor_tensor(sq, gr[:], gr[:], ALU.mult))
                nc.vector.scalar_tensor_tensor(out=th[:], in0=sq, scalar=1.0, in1=th[:], op0=ALU.add,
                                               op1=ALU.mult).then_inc(gx_ready, 1)
                then(nc.vector.tensor_tensor(gi[:], gi[:], xc[:], ALU.mult))
                dve.wait_ge(sq_done, t + 1)
                then(nc.vector.tensor_tensor(gi[:], gi[:], th[:], ALU.mult))
                then(nc.vector.tensor_tensor_scan(th[:, 0:SEQ], gr[:, 0:SEQ], gi[:, 0:SEQ], 0.0, ALU.mult, ALU.add))
                v = lambda x: x[:, SEQ:NTOK].rearrange("p (b w) -> p b w", b=DB)
                prev = c.par[:, t, R_SH:R_SH + DB]
                for j in range(DT):
                    then(nc.vector.tensor_tensor(v(th)[:, :, j], v(gr)[:, :, j], prev, ALU.mult))
                    then(nc.vector.tensor_tensor(v(th)[:, :, j], v(th)[:, :, j], v(gi)[:, :, j], ALU.add))
                    prev = v(th)[:, :, j]
                nc.vector.tensor_copy(last_in[:, t, 27:28], th[:, SEQ - 1:SEQ]).then_inc(step, 1)
                nc.vector.tensor_copy(last_in[:, t, 28:36], prev).then_inc(step, 1)
                n[0] += 2
                dve.wait_ge(gelu_done, t + 1)
                then(nc.vector.tensor_tensor(sq, th[:], zT[:, CC + t, :], ALU.mult))
                dve.sem_inc(c_done, 1)
            for t, rows in TILES:
                dve.wait_ge(tok_ready, t + 1)
                if t >= 2:
                    dve.wait_ge(k_landed[t % 2], 16 * (t // 2))
                nc.vector.tensor_copy(k_tok[0:rows, t % 2, :], zp[t % 2][0:rows, DR:2 * DR]).then_inc(k_done, 1)
            dve.wait_ge(lp_ready, 1)
            nc.vector.tensor_copy(last_rows[:], lp).then_inc(last_ready, 1)


def attend_prompt(nc, a, c, zT, v_tok, y_tok):
    PAIRS = HEADS // 2
    UNITS = 2 * PT
    unit = [(n // PT, n % PT) for n in range(UNITS)]
    groups = []
    first_group = []
    for n, (h, i) in enumerate(unit):
        first_group.append(len(groups))
        groups += [(n, lo, min(lo + 4, i + 1)) for lo in range(0, i + 1, 4)]
    GROUPS = len(groups)
    first_group.append(GROUPS)
    of_unit = lambda n: range(first_group[n], first_group[n + 1])
    assert GROUPS % 4 == 0 and UNITS % 4 == 0
    with ExitStack() as ctx:
        s = Shop(nc, ctx, "attend_prompt")
        passed = s.sem("passed")
        qT, kT = s.sb("qT", [P, SEQ]), s.sb("kT", [P, SEQ])
        logits, prob = s.sb("logits", [P, 2, SEQ]), s.sb("prob", [P, 2, SEQ])
        probT = s.sb("probT", [P, 4, HALF])
        top, neg_top, den, rden = (s.sb(x, [P, 4]) for x in ("top", "neg_top", "den", "rden"))
        sp_ = [s.ps(f"s{i}", [P, SEQ]) for i in range(2)]
        pt = [s.ps(f"pt{i}", [P, HALF]) for i in range(2)]
        o = [s.ps(f"o{i}", [P, HALF]) for i in range(2)]
        q_ready, k_ready, s_ready, s_free = s.sem("q_ready"), s.sem("k_ready"), s.sem("s_ready"), s.sem("s_free")
        top_ready, exp_done, p_ready, rden_ready = s.sem("top_ready"), s.sem("exp_done"), s.sem("p_ready"), s.sem("rden_ready")
        pt_ready, pt_free, pv_done, o_free = s.sem("pt_ready"), s.sem("pt_free"), s.sem("pv_done"), s.sem("o_free")
        probT_free = s.sem("probT_free")
        block = ctx.enter_context(nc.Block())

        @block.gpsimd
        def _(pool):
            with pool.Fori(0, PAIRS) as i:
                pool.wait_ge(s_ready, UNITS * i + 1)
                nc.gpsimd.tensor_copy(qT[:], zT[:, bass.ds(i + 2 * CC, 1), 0:SEQ].rearrange("p a n -> p (a n)")).then_inc(q_ready, 1)
                nc.gpsimd.tensor_copy(kT[:], zT[:, bass.ds(i + 3 * CC, 1), 0:SEQ].rearrange("p a n -> p (a n)")).then_inc(k_ready, 1)

        @block.tensor
        def _(pe):
            pe.sem_inc(s_ready, 1)
            pe.sem_inc(probT_free, 4)

            def scores(it, n):
                h, i = unit[n]
                rows, L = slice(HD * h, HD * h + HD), (i + 1) * P
                if n == 0:
                    pe.wait_ge(q_ready, it + 1)
                    pe.wait_ge(k_ready, it + 1)
                pe.wait_ge(s_free, UNITS * it + n + 1)
                for lo in range(0, L, HALF):
                    hi = min(lo + HALF, L)
                    last = nc.tensor.matmul(sp_[n % 2][:, lo:hi], qT[rows, i * P:(i + 1) * P], kT[rows, lo:hi],
                                            start=True, stop=True)
                last.then_inc(s_ready, 1)

            def turn(it, n):
                pe.wait_ge(p_ready, UNITS * it + n + 1)
                for g in of_unit(n):
                    _, lo, hi = groups[g]
                    pe.wait_ge(pt_free, GROUPS * it + g + 1)
                    for b in range(lo, hi):
                        last = nc.tensor.transpose(pt[g % 2][:, (b - lo) * P:(b - lo + 1) * P],
                                                   prob[:, n % 2, b * P:(b + 1) * P], c.ident[:])
                    last.then_inc(pt_ready, 1)

            def values(it, n):
                h, i = unit[n]
                pe.wait_ge(o_free, UNITS * it + n + 1)
                for g in of_unit(n):
                    _, lo, hi = groups[g]
                    pe.wait_ge(pt_free, GROUPS * it + g + 3)
                    for b in range(lo, hi):
                        last = nc.tensor.matmul(o[n % 2][:, 0:HD], probT[:, g % 4, (b - lo) * P:(b - lo + 1) * P],
                                                v_tok[:, b, bass.ds(it * 2 * HD + h * HD, HD)],
                                                start=(b == 0), stop=(b == i))
                    last.then_inc(probT_free, 1)
                pe.wait_ge(probT_free, GROUPS * it + first_group[n + 1] + 4)
                pe.sem_inc(pv_done, 1)

            with pe.Fori(0, PAIRS) as it:
                for k in range(UNITS + 2):
                    if k < UNITS:
                        scores(it, k)
                    if k >= 2:
                        values(it, k - 2)
                    if 1 <= k <= UNITS:
                        turn(it, k - 1)

        @block.scalar
        def _(act):
            act.sem_inc(pt_free, 2)

            def exps(it, n):
                L = (unit[n][1] + 1) * P
                act.wait_ge(top_ready, UNITS * it + n + 1)
                nc.scalar.activation(prob[:, n % 2, 0:L], logits[:, n % 2, 0:L], ACT.Exp, scale=SCALE,
                                     bias=neg_top[:, n % 4:n % 4 + 1]).then_inc(exp_done, 1)

            def keep(it, n):
                for g in of_unit(n):
                    _, lo, hi = groups[g]
                    act.wait_ge(pt_ready, GROUPS * it + g + 1)
                    act.wait_ge(probT_free, GROUPS * it + g + 1)
                    nc.scalar.activation(probT[:, g % 4, 0:(hi - lo) * P], pt[g % 2][:, 0:(hi - lo) * P],
                                         ACT.Copy).then_inc(pt_free, 1)

            with act.Fori(0, PAIRS) as it:
                for k in range(UNITS + 1):
                    if k < UNITS:
                        exps(it, k)
                    if k >= 1:
                        keep(it, k - 1)

        @block.vector
        def _(dve):
            dve.sem_inc(s_free, 2)
            dve.sem_inc(o_free, 2)

            def tops(it, n):
                L = (unit[n][1] + 1) * P
                dve.wait_ge(s_ready, UNITS * it + n + 2)
                dve.sem_inc(passed, 1)
                nc.vector.tensor_tensor_reduce(out=logits[:, n % 2, 0:L], in0=sp_[n % 2][:, 0:L],
                                               in1=c.bias[:, SEQ - L:SEQ], scale=1.0, scalar=-3e38, op0=ALU.add,
                                               op1=ALU.max, accum_out=top[:, n % 4:n % 4 + 1]).then_inc(s_free, 1)
                dve.wait_ge(s_free, UNITS * it + n + 3)
                nc.vector.tensor_scalar(neg_top[:, n % 4:n % 4 + 1], top[:, n % 4:n % 4 + 1], -SCALE, None,
                                        ALU.mult).then_inc(top_ready, 1)

            def weigh(it, n):
                L = (unit[n][1] + 1) * P
                dve.wait_ge(exp_done, UNITS * it + n + 1)
                nc.vector.tensor_tensor_reduce(out=prob[:, n % 2, 0:L], in0=prob[:, n % 2, 0:L],
                                               in1=c.mult[:, SEQ - L:SEQ], scale=1.0, scalar=0.0, op0=ALU.mult,
                                               op1=ALU.add, accum_out=den[:, n % 4:n % 4 + 1]).then_inc(p_ready, 1)
                dve.wait_ge(p_ready, UNITS * it + n + 1)
                nc.vector.reciprocal(rden[:, n % 4:n % 4 + 1], den[:, n % 4:n % 4 + 1]).then_inc(rden_ready, 1)

            def divide(it, n):
                h, i = unit[n]
                dve.wait_ge(pv_done, UNITS * it + n + 1)
                dve.wait_ge(rden_ready, UNITS * it + n + 1)
                nc.vector.tensor_scalar(y_tok[:, i, bass.ds(it * 2 * HD + h * HD, HD)], o[n % 2][:, 0:HD],
                                        rden[:, n % 4:n % 4 + 1], None, ALU.mult).then_inc(o_free, 1)

            with dve.Fori(0, PAIRS) as it:
                for k in range(UNITS + 3):
                    if k < UNITS:
                        tops(it, k)
                    if 1 <= k <= UNITS:
                        weigh(it, k - 1)
                    if k >= 3:
                        divide(it, k - 3)


def attend_sample(nc, a, c, zT, v_tok, ysT, xT):
    OLD, SK = c.OLD, c.SK
    NW = SK + NS
    with ExitStack() as ctx:
        s = Shop(nc, ctx, "attend_sample")
        passed = s.sem("passed")
        spent = xT[:].rearrange("p k n -> p (k n)")
        kn, vn = (spent[:, i * 8 * DR:(i + 1) * 8 * DR].rearrange("p (a t e) -> p a t e", a=2, t=4) for i in range(2))
        ko, vo = s.sb("ko", [OLD, 2, DT, DR]), s.sb("vo", [OLD, 2, DT, DR])
        q_all = s.sb("q_all", [P, DB, CC, NS])
        q_one = s.sb("q_one", [P, 2, CC, NS])
        ktn, kto = s.sb("ktn", [P, 2, HALF]), s.sb("kto", [P, 2, DT * OLD])
        bias, mult = c.s_bias, c.s_mult
        gate = zT[0:NS, CC:2 * CC, :].rearrange("p a n -> p (a n)")
        logits = gate[:, 0:2 * NW].rearrange("p (a n) -> p a n", a=2)
        prob = gate[:, 2 * NW:4 * NW].rearrange("p (a n) -> p a n", a=2)
        probT = s.sb("probT_s", [P, 9, NS])
        top, den = s.sb("top_s", [NS, 2, 4]), s.sb("den_s", [NS, 2, 2])
        pn, po = s.ps("pn", [P, HALF]), s.ps("po", [P, HALF])
        sn = [s.ps(f"sn{i}", [NS, HALF]) for i in range(2)]
        so = [s.ps(f"so{i}", [NS, HALF]) for i in range(2)]
        pt, ot = s.ps("pt_s", [P, HALF]), s.ps("ot", [P, HALF])
        k_landed = [s.sem(f"ks_landed{i}") for i in range(2)]
        v_landed = [s.sem(f"vs_landed{i}") for i in range(2)]
        names = ("q_zero", "q_all_ready", "q_ready", "masks_ready", "pn_ready", "po_ready", "pn_free", "po_free",
                 "kt_used", "s_ready", "step", "top_ready", "exp_done", "den_ready", "p_ready", "pt_ready",
                 "pt_free", "pv_done", "out_done")
        m = {x: s.sem(x) for x in names}
        block = ctx.enter_context(nc.Block())
        LOOPS = DB // 2

        @block.sync
        def _(sp):
            with sp.Fori(0, LOOPS) as i:
                for par in range(2):
                    b = 2 * i + par
                    sp.wait_ge(m["out_done"], b + 1)
                    for x, new, old, sem in (("cache_k", kn, ko, k_landed), ("cache_v", vn, vo, v_landed)):
                        cache = a[x][0].rearrange("b t h e -> b (t h e)")
                        row = HEADS * HD
                        sp.dma_start(new[:, par].rearrange("p i e -> p (i e)"),
                                     cache[bass.ds(b, 1), (PAST - HALF) * row:PAST * row].rearrange(
                                         "a (p f) -> (a p) f", p=P)).then_inc(sem[par], 16)
                        sp.dma_start(old[:, par].rearrange("p i e -> p (i e)"),
                                     cache[bass.ds(b, 1), 0:(PAST - HALF) * row].rearrange(
                                         "a (p f) -> (a p) f", p=OLD)[:, 0:DT * row]).then_inc(sem[par], 16)

        @block.gpsimd
        def _(pool):
            nc.gpsimd.memset(q_all[:], 0.0).then_inc(m["q_zero"], 1)
            pool.wait_ge(m["q_zero"], 1)
            n = 0
            for j in range(CC):
                for half in range(2):
                    rows, col = slice(HD * half, HD * half + HD), DT * (2 * j + half)
                    nc.gpsimd.tensor_copy(q_all[rows, :, j, col:col + DT],
                                          zT[rows, 2 * CC + j, SEQ:NTOK].rearrange("p (b w) -> p b w", b=DB)
                                          ).then_inc(m["q_all_ready"], 1)
                    n += 1
            pool.wait_ge(m["q_all_ready"], n)
            with pool.Fori(0, LOOPS) as i:
                for par in range(2):
                    b = 2 * i + par
                    pool.wait_ge(m["out_done"], b + 1)
                    nc.gpsimd.tensor_copy(q_one[:, par], q_all[:, bass.ds(b, 1)].rearrange("p a j r -> p (a j) r")
                                          ).then_inc(m["q_ready"], 1)
                    nc.gpsimd.tensor_copy(bias[:, par, SK:NW], c.n_bias[:, bass.ds(b, 1), :].rearrange("p a r -> p (a r)")
                                          ).then_inc(m["masks_ready"], 1)
                    nc.gpsimd.tensor_copy(mult[:, par, SK:NW], c.n_mult[:, bass.ds(b, 1), :].rearrange("p a r -> p (a r)")
                                          ).then_inc(m["masks_ready"], 1)

        @block.tensor
        def _(pe):
            pe.sem_inc(m["kt_used"], 2)

            def scores(b, i, par):
                pe.wait_ge(k_landed[par], 32 * (i + 1))
                pe.wait_ge(m["q_ready"], b + 1)

                def product(j):
                    pe.wait_ge(m["pn_free"], CC * b + j + 2)
                    pe.wait_ge(m["po_free"], CC * b + j + 2)
                    q = q_one[:, par, j, :]
                    nc.tensor.matmul(sn[par][:], q, ktn[:, j % 2, :], start=(j == 0), stop=(j == CC - 1))
                    nc.tensor.matmul(so[par][:, 0:DT * OLD], q, kto[:, j % 2, :], start=(j == 0), stop=(j == CC - 1),
                                     skip_group_check=True)
                    nc.tensor.matmul(so[par][:, DT * OLD:DT * OLD + NS], q, zT[:, 3 * CC + j, SEQ:NTOK],
                                     start=False, stop=(j == CC - 1),
                                     skip_group_check=True).then_inc(m["kt_used"], 1)

                for j in range(CC):
                    pe.wait_ge(m["pn_free"], CC * b + j + 1)
                    for t in range(4):
                        last = nc.tensor.transpose(pn[:, t * P:(t + 1) * P], kn[:, par, t, j * P:(j + 1) * P], c.ident[:])
                    last.then_inc(m["pn_ready"], 1)
                    pe.wait_ge(m["po_free"], CC * b + j + 1)
                    for t in range(DT):
                        last = nc.tensor.transpose(po[:, t * OLD:(t + 1) * OLD], ko[:, par, t, j * P:(j + 1) * P],
                                                   c.ident[0:OLD, 0:OLD])
                    last.then_inc(m["po_ready"], 1)
                    if j:
                        product(j - 1)
                product(CC - 1)
                pe.wait_ge(m["kt_used"], CC * (b + 1) + 2)
                pe.sem_inc(m["s_ready"], 1)

            def values(b, i, par):
                pe.wait_ge(m["p_ready"], b + 1)
                pe.sem_inc(passed, 1)
                for t in range(4):
                    nc.tensor.transpose(pt[:, t * NS:(t + 1) * NS], prob[:, par, t * P:(t + 1) * P], c.ident[0:NS, 0:NS])
                for t in range(DT):
                    nc.tensor.transpose(pt[0:OLD, (4 + t) * NS:(5 + t) * NS],
                                        prob[:, par, HALF + t * OLD:HALF + (t + 1) * OLD], c.ident[0:NS, 0:NS])
                nc.tensor.transpose(pt[0:NS, 8 * NS:9 * NS], prob[:, par, SK:NW], c.ident[0:NS, 0:NS]).then_inc(m["pt_ready"], 1)
                pe.wait_ge(v_landed[par], 32 * (i + 1))
                pe.wait_ge(m["pt_free"], b + 1)
                pe.wait_ge(m["out_done"], b + 2)
                for j in range(CC):
                    r = slice(2 * DT * j, 2 * DT * (j + 1))
                    e = slice(j * P, (j + 1) * P)
                    for t in range(4):
                        nc.tensor.matmul(ot[:, 8 * j:8 * j + 8], vn[:, par, t, e], probT[:, t, r],
                                         start=(t == 0), stop=False)
                    for t in range(DT):
                        nc.tensor.matmul(ot[:, 8 * j:8 * j + 8], vo[:, par, t, e], probT[0:OLD, 4 + t, r],
                                         start=False, stop=False)
                    last = nc.tensor.matmul(ot[:, 8 * j:8 * j + 8], v_tok[0:NS, PT, e], probT[0:NS, 8, r],
                                            start=False, stop=True)
                last.then_inc(m["pv_done"], 1)

            with pe.Fori(0, LOOPS) as i:
                for par in range(2):
                    scores(2 * i + par, i, par)
                for par in range(2):
                    values(2 * i + par, i, par)

        @block.scalar
        def _(act):
            act.sem_inc(m["pn_free"], 1)

            def keys(b):
                for j in range(CC):
                    act.wait_ge(m["pn_ready"], CC * b + j + 1)
                    act.wait_ge(m["kt_used"], CC * b + j + 1)
                    nc.scalar.activation(ktn[:, j % 2, :], pn[:], ACT.Copy).then_inc(m["pn_free"], 1)

            def exps(b, par):
                act.wait_ge(m["top_ready"], b + 1)
                nc.scalar.activation(prob[:, par], logits[:, par], ACT.Exp, scale=SCALE,
                                     bias=top[:, par, 2:3]).then_inc(m["exp_done"], 1)

            def norm(b, par):
                act.wait_ge(m["den_ready"], b + 1)
                nc.scalar.activation(prob[:, par], prob[:, par], ACT.Copy, scale=den[:, par, 1:2]).then_inc(m["p_ready"], 1)

            def turned(b):
                act.wait_ge(m["pt_ready"], b + 1)
                act.wait_ge(m["pv_done"], b + 1)
                nc.scalar.activation(probT[:, 0:4], pt[:, 0:4 * NS].rearrange("p (t r) -> p t r", r=NS), ACT.Copy)
                nc.scalar.activation(probT[0:OLD, 4:8], pt[0:OLD, 4 * NS:8 * NS].rearrange("p (t r) -> p t r", r=NS), ACT.Copy)
                nc.scalar.activation(probT[0:NS, 8], pt[0:NS, 8 * NS:9 * NS], ACT.Copy).then_inc(m["pt_free"], 1)

            act.sem_inc(m["pv_done"], 1)
            with act.Fori(0, LOOPS) as i:
                for par in range(2):
                    keys(2 * i + par)
                for par in range(2):
                    exps(2 * i + par, par)
                for par in range(2):
                    norm(2 * i + par, par)
                for par in range(2):
                    turned(2 * i + par)

        @block.vector
        def _(dve):
            dve.sem_inc(m["po_free"], 1)
            dve.sem_inc(m["out_done"], 2)

            def keys(b):
                for j in range(CC):
                    dve.wait_ge(m["po_ready"], CC * b + j + 1)
                    dve.wait_ge(m["kt_used"], CC * b + j + 1)
                    nc.vector.tensor_copy(kto[:, j % 2, :], po[:, 0:DT * OLD]).then_inc(m["po_free"], 1)

            def tops(b, par):
                dve.wait_ge(m["s_ready"], b + 1)
                dve.wait_ge(m["masks_ready"], 2 * b + 2)
                dve.sem_inc(passed, 1)
                nc.vector.tensor_tensor_reduce(out=logits[:, par, 0:HALF], in0=sn[par][:], in1=bias[:, par, 0:HALF],
                                               scale=1.0, scalar=-3e38, op0=ALU.add, op1=ALU.max,
                                               accum_out=top[:, par, 0:1]).then_inc(m["step"], 1)
                dve.wait_ge(m["step"], 2 * b + 1)
                dve.sem_inc(passed, 1)
                nc.vector.tensor_tensor_reduce(out=logits[:, par, HALF:NW], in0=so[par][:, 0:NW - HALF],
                                               in1=bias[:, par, HALF:NW], scale=1.0, scalar=top[:, par, 0:1],
                                               op0=ALU.add, op1=ALU.max, accum_out=top[:, par, 1:2]).then_inc(m["step"], 1)
                dve.wait_ge(m["step"], 2 * b + 2)
                nc.vector.tensor_scalar(top[:, par, 2:3], top[:, par, 1:2], -SCALE, None, ALU.mult).then_inc(m["top_ready"], 1)

            def sums(b, par):
                dve.wait_ge(m["exp_done"], b + 1)
                nc.vector.tensor_tensor_reduce(out=prob[:, par], in0=prob[:, par], in1=mult[:, par], scale=1.0, scalar=0.0,
                                               op0=ALU.mult, op1=ALU.add, accum_out=den[:, par, 0:1]).then_inc(m["q_zero"], 1)
                dve.wait_ge(m["q_zero"], b + 2)
                nc.vector.reciprocal(den[:, par, 1:2], den[:, par, 0:1]).then_inc(m["den_ready"], 1)

            def keep(b, par):
                dve.wait_ge(m["pv_done"], b + 2)
                for half in range(2):
                    rows = slice(HD * half, HD * half + HD)
                    last = nc.vector.tensor_copy(
                        ysT[rows, :, bass.ds(b * DT, DT)],
                        ot[rows, 0:8 * CC].rearrange("p (j h w) -> p j h w", j=CC, h=2)[:, :, half, :])
                last.then_inc(m["out_done"], 1)

            with dve.Fori(0, LOOPS) as i:
                for par in range(2):
                    keys(2 * i + par)
                for par in range(2):
                    tops(2 * i + par, par)
                for par in range(2):
                    sums(2 * i + par, par)
                for par in range(2):
                    keep(2 * i + par, par)


def merge(nc, a, c, zT, y_tok, ysT, xT, x_res, x_parts, x_turned):
    with ExitStack() as ctx:
        s = Shop(nc, ctx, "merge")
        passed = s.sem("passed")
        spent = zT[:, CC:4 * CC, :].rearrange("p a n -> p (a n)")
        w_out = spent[:, 0:KC * D].rearrange("p (k n) -> p k n", k=KC)
        x_in = spent[:, KC * D:(KC + 2) * D].rearrange("p (k n) -> p k n", k=2)
        x2 = spent[:, (KC + 2) * D:(KC + 4) * D].rearrange("p (k n) -> p k n", k=2)
        g_row = s.sb("g_row", [P, D])
        sq, sg, ya = s.sb("sq", [P, CC, P]), s.sb("sg", [P, 2, CC, P]), s.sb("ya", [P, 2, CC, P])
        rr = s.sb("rr", [P, 3, P])
        yn = s.sb("yn", [P, DR])
        xn, xf = s.sb("xn2", [P, D]), s.sb("xf", [P, D])
        squares = s.sb("squares2", [P, D])
        pieces = s.sb("pieces", [P, 3, D], BF16)
        stat = s.sb("stat2", [P, 2, 8])
        acc = [s.ps(f"acc{i}", [P, D]) for i in range(2)]
        ssb, yp, tp = s.ps("ssb", [P, HALF]), s.ps("yp", [P, HALF]), s.ps("tp2", [P, KC, P])
        x_landed = [s.sem(f"mx_landed{i}") for i in range(2)]
        x2_stored = [s.sem(f"x2_stored{i}") for i in range(2)]
        w_landed, turned_stored = s.sem("w_out_landed"), s.sem("turned_stored")
        nothing, nothing_ready = s.sb("nothing", [P, KC, P - NS]), s.sem("nothing_ready")
        m = {x: s.sem(x) for x in (
            "sq_ready ssb_ready msr_ready rtr_done rr_ready sg_ready sga_done msa_ready rta_done ra_ready yn_ready "
            "yp_ready ya_ready summed x2_half x2_ready sqb_done msb_ready rtb_done rb_ready xn_ready xt_ready xt_done "
            "xf_ready hi_ready r1_ready mid_ready lo_ready stored sqa_ready").split()}
        block = ctx.enter_context(nc.Block())

        def run(eng, step):
            step(0, 0)
            step(1, 1)
            with eng.Fori(1, PT // 2) as i:
                step(2 * i, 0)
                step(2 * i + 1, 1)
            step(PT, 0)
            step(PT + 1, 1)
            step(PT + 2, 0)

        def has(k, back):
            if not isinstance(k, int):
                return P
            t = k - back
            return 0 if t < 0 or t > PT else (NS if t == PT else P)

        @block.sync
        def _(sp):
            sp.dma_start(w_out, a["w_out"][0].rearrange("(k p) n -> p k n", p=P)).then_inc(w_landed, 16)
            sp.dma_start(g_row[:], a["g_ffn"].to_broadcast((P, D))).then_inc(w_landed, 16)

            def step(k, par):
                rows = has(k, 0)
                if rows:
                    if not (isinstance(k, int) and k < 2):
                        sp.wait_ge(m["x2_ready"], k - 1)
                        sp.sem_inc(passed, 1)
                    src = a["x_prompt"][0, cols(k), :] if rows == P else a["x_sample"].rearrange("b t d -> (b t) d")
                    sp.dma_start(x_in[0:rows, par, :], src).then_inc(x_landed[par], 16)
                rows = has(k, 2)
                if rows:
                    t = k - 2
                    sp.dma_start(x_res[bass.ds(t * P, rows), :], x2[0:rows, par, :]).then_inc(x2_stored[par], 16)
                    sp.wait_ge(m["lo_ready"], t + 1)
                    sp.sem_inc(passed, 1)
                    for part in range(3):
                        sp.dma_start(x_parts[part, bass.ds(t * P, rows), :], pieces[0:rows, part, :]).then_inc(m["stored"], 16)
                    sp.wait_ge(m["xt_done"], t + 1)
                    sp.sem_inc(passed, 1)
                    sp.dma_start(x_turned[bass.ds(t, 1), :, :, 0:rows].rearrange("a p k n -> (a p) k n"),
                                 xT[:, :, cols(t, rows)]).then_inc(turned_stored, 16)

            def step2(k, par):
                if has(k, 2):
                    sp.wait_ge(m["x2_ready"], k - 1)
                step(k, par)

            sp.wait_ge(nothing_ready, 1)
            sp.dma_start(x_turned[PT, :, :, NS:P], nothing[:]).then_inc(turned_stored, 16)
            run(sp, step2)
            sp.wait_ge(turned_stored, 16 * (PT + 2))
            sp.wait_ge(m["stored"], 48 * (PT + 1))
            sp.wait_ge(x2_stored[0], 16 * (PT // 2 + 1))
            sp.wait_ge(x2_stored[1], 16 * (PT // 2))

        @block.tensor
        def _(pe):
            def groups(k, par, rows):
                pe.wait_ge(m["sq_ready"], k + 1)
                if not (isinstance(k, int) and k == 0):
                    pe.wait_ge(m["msr_ready"], k)
                for j in range(CC):
                    last = nc.tensor.matmul(ssb[:, 0:rows], c.ones[:], sq[:, j, 0:rows], start=(j == 0), stop=(j == CC - 1))
                last.then_inc(m["ssb_ready"], 1)
                if rows == P:
                    pe.wait_ge(m["yn_ready"], k + 1)
                    if not (isinstance(k, int) and k == 0):
                        pe.wait_ge(m["ya_ready"], k)
                    for j in range(CC):
                        last = nc.tensor.transpose(yp[:, j * P:(j + 1) * P], yn[:, j * P:(j + 1) * P], c.ident[:])
                    last.then_inc(m["yp_ready"], 1)
                else:
                    pe.wait_ge(m["sqa_ready"], 1)
                    for j in range(CC):
                        last = nc.tensor.matmul(yp[:, 0:rows], c.ones[:], sq[:, j, P - NS:P], start=(j == 0), stop=(j == CC - 1))
                    last.then_inc(m["yp_ready"], 1)

            def product(t, par, rows):
                pe.wait_ge(m["sg_ready"], t + 1)
                pe.wait_ge(m["ya_ready"], t + 1)
                if not (isinstance(t, int) and t < 2):
                    pe.wait_ge(m["x2_ready"], t - 1)
                for n, y in enumerate((sg, ya)):
                    for j in range(CC):
                        for lo, hi in NARROW:
                            last = nc.tensor.matmul(acc[par][0:rows, lo:hi], y[:, par, j, 0:rows], w_out[:, CC * n + j, lo:hi],
                                                    start=(n + j == 0), stop=(n == 1 and j == CC - 1))
                last.then_inc(m["summed"], 1)

            def second_norm(t, rows):
                pe.wait_ge(m["xn_ready"], t + 1)
                if not (isinstance(t, int) and t == 0):
                    pe.wait_ge(m["xt_done"], t)
                for j in range(KC):
                    last = nc.tensor.transpose(tp[:, j, 0:rows], xn[0:rows, j * P:(j + 1) * P], c.ident[0:rows, 0:rows])
                last.then_inc(m["xt_ready"], 1)

            def step(k, par):
                if has(k, 0):
                    groups(k, par, has(k, 0))
                if has(k, 1):
                    product(k - 1, 1 - par, has(k, 1))
                if has(k, 2):
                    second_norm(k - 2, has(k, 2))

            pe.wait_ge(w_landed, 32)
            run(pe, step)

        @block.scalar
        def _(act):
            def groups(k, par, rows):
                if rows == P:
                    if not (isinstance(k, int) and k == 0):
                        act.wait_ge(m["yn_ready"], k)
                        act.sem_inc(passed, 1)
                    nc.scalar.activation(squares[:, 0:DR], y_tok[:, bass.ds(k, 1), :].rearrange("p a e -> p (a e)"),
                                         ACT.Square, accum_out=stat[:, par, 0:1]).then_inc(m["sga_done"], 1)
                act.wait_ge(m["msr_ready"], k + 1)
                nc.scalar.activation(rr[:, 1, 0:rows], rr[:, 0, 0:rows], ACT.Sqrt).then_inc(m["rtr_done"], 1)
                act.wait_ge(m["msa_ready"], k + 1)
                if rows == P:
                    nc.scalar.activation(stat[:, par, 2:3], stat[:, par, 1:2], ACT.Sqrt).then_inc(m["rta_done"], 1)
                    act.wait_ge(m["ra_ready"], k + 1)
                    if not (isinstance(k, int) and k == 0):
                        act.wait_ge(m["yp_ready"], k)
                        act.sem_inc(passed, 1)
                    nc.scalar.activation(yn[:], y_tok[:, bass.ds(k, 1), :].rearrange("p a e -> p (a e)"), ACT.Copy,
                                         scale=stat[:, par, 3:4]).then_inc(m["yn_ready"], 1)
                else:
                    nc.scalar.activation(rr[:, 1, P - NS:P], rr[:, 0, P - NS:P], ACT.Sqrt).then_inc(m["rta_done"], 1)

            def second_norm(t, par, rows):
                act.wait_ge(m["x2_ready"], t + 1)
                nc.scalar.activation(squares[0:rows, :], x2[0:rows, par, :], ACT.Square,
                                     accum_out=stat[0:rows, par, 4:5]).then_inc(m["sqb_done"], 1)
                act.wait_ge(m["msb_ready"], t + 1)
                nc.scalar.activation(stat[0:rows, par, 6:7], stat[0:rows, par, 5:6], ACT.Sqrt).then_inc(m["rtb_done"], 1)
                act.wait_ge(m["rb_ready"], t + 1)
                if not (isinstance(t, int) and t == 0):
                    act.wait_ge(m["xt_ready"], t)
                    act.wait_ge(m["xf_ready"], t)
                nc.scalar.activation(xn[0:rows, :], x2[0:rows, par, :], ACT.Copy,
                                     scale=stat[0:rows, par, 7:8]).then_inc(m["xn_ready"], 1)
                act.wait_ge(m["xf_ready"], t + 1)
                if not (isinstance(t, int) and t == 0):
                    act.wait_ge(m["stored"], 48 * t)
                nc.scalar.activation(pieces[0:rows, 0, :], xf[0:rows, :], ACT.Copy).then_inc(m["hi_ready"], 1)
                act.wait_ge(m["r1_ready"], t + 1)
                nc.scalar.activation(pieces[0:rows, 1, :], xf[0:rows, :], ACT.Copy).then_inc(m["mid_ready"], 1)

            def step(k, par):
                if has(k, 0):
                    groups(k, par, has(k, 0))
                if has(k, 2):
                    second_norm(k - 2, par, has(k, 2))

            run(act, step)

        @block.gpsimd
        def _(pool):
            def step(k, par):
                rows = has(k, 2)
                if rows:
                    t = k - 2
                    pool.wait_ge(m["xn_ready"], t + 1)
                    if not (isinstance(t, int) and t == 0):
                        pool.wait_ge(m["lo_ready"], t)
                    nc.gpsimd.tensor_tensor(xf[0:rows, :], xn[0:rows, :], g_row[0:rows, :], ALU.mult).then_inc(m["xf_ready"], 1)
                    pool.wait_ge(m["hi_ready"], t + 1)
                    nc.gpsimd.tensor_tensor(xf[0:rows, :], xf[0:rows, :], pieces[0:rows, 0, :], ALU.subtract).then_inc(m["r1_ready"], 1)
                    pool.wait_ge(m["mid_ready"], t + 1)
                    nc.gpsimd.tensor_tensor(pieces[0:rows, 2, :], xf[0:rows, :], pieces[0:rows, 1, :],
                                            ALU.subtract).then_inc(m["lo_ready"], 1)

            nc.gpsimd.memset(nothing[:], 0.0).then_inc(nothing_ready, 1)
            pool.wait_ge(w_landed, 32)
            run(pool, step)

        @block.vector
        def _(dve):
            wide = lambda x, rows: x.unsqueeze(2).to_broadcast((P, CC, rows))

            def groups(k, par, rows):
                y = zT[:, 0:CC, cols(k, rows)]
                if not (isinstance(k, int) and k == 0):
                    dve.wait_ge(m["ssb_ready"], k)
                nc.vector.tensor_tensor(sq[:, :, 0:rows], y, y, ALU.mult).then_inc(m["sq_ready"], 1)
                if not (isinstance(k, int) and k < 2):
                    dve.wait_ge(m["summed"], k - 1)
                nc.vector.tensor_tensor(sg[:, par, :, 0:rows], y, wide(c.par[:, :, R_GRNN], rows), ALU.mult)
                if rows != P:
                    nc.vector.tensor_tensor(sq[:, :, P - NS:P], ysT[:], ysT[:], ALU.mult).then_inc(m["sqa_ready"], 1)
                dve.wait_ge(m["ssb_ready"], k + 1)
                nc.vector.tensor_scalar(rr[:, 0, 0:rows], ssb[:, 0:rows], 1.0 / DR, EPS, ALU.mult, ALU.add).then_inc(m["msr_ready"], 1)
                if rows == P:
                    dve.wait_ge(m["sga_done"], k + 1)
                    nc.vector.tensor_scalar(stat[:, par, 1:2], stat[:, par, 0:1], 1.0 / DR, EPS, ALU.mult, ALU.add).then_inc(m["msa_ready"], 1)
                else:
                    dve.wait_ge(m["yp_ready"], k + 1)
                    nc.vector.tensor_scalar(rr[:, 0, P - NS:P], yp[:, 0:rows], 1.0 / DR, EPS, ALU.mult, ALU.add).then_inc(m["msa_ready"], 1)
                dve.wait_ge(m["rtr_done"], k + 1)
                nc.vector.reciprocal(rr[:, 2, 0:rows], rr[:, 1, 0:rows]).then_inc(m["rr_ready"], 1)
                dve.wait_ge(m["rr_ready"], k + 1)
                nc.vector.tensor_tensor(sg[:, par, :, 0:rows], sg[:, par, :, 0:rows],
                                        rr[:, 2:3, 0:rows].to_broadcast((P, CC, rows)), ALU.mult).then_inc(m["sg_ready"], 1)
                dve.wait_ge(m["rta_done"], k + 1)
                if rows == P:
                    nc.vector.reciprocal(stat[:, par, 3:4], stat[:, par, 2:3]).then_inc(m["ra_ready"], 1)
                    dve.wait_ge(m["yp_ready"], k + 1)
                    nc.vector.tensor_tensor(ya[:, par], yp[:].rearrange("p (j n) -> p j n", j=CC),
                                            wide(c.par[:, :, R_GATT], rows), ALU.mult).then_inc(m["ya_ready"], 1)
                else:
                    nc.vector.reciprocal(rr[:, 2, P - NS:P], rr[:, 1, P - NS:P]).then_inc(m["ra_ready"], 1)
                    dve.wait_ge(m["ra_ready"], k + 1)
                    nc.vector.tensor_tensor(ya[:, par, :, 0:rows], ysT[:], wide(c.par[:, :, R_GATT], rows), ALU.mult).then_inc(m["ra_ready"], 1)
                    dve.wait_ge(m["ra_ready"], k + 2)
                    nc.vector.tensor_tensor(ya[:, par, :, 0:rows], ya[:, par, :, 0:rows],
                                            rr[:, 2:3, P - NS:P].to_broadcast((P, CC, rows)), ALU.mult).then_inc(m["ya_ready"], 1)

            def product(t, par, rows):
                dve.wait_ge(m["summed"], t + 1)
                dve.wait_ge(x_landed[par], x_count(t))
                if not (isinstance(t, int) and t < 2):
                    dve.wait_ge(x2_stored[par], x_count(t) - 16)
                    dve.wait_ge(m["xn_ready"], t - 1)
                nc.vector.tensor_tensor(x2[0:rows, par, :], acc[par][0:rows, :], x_in[0:rows, par, :], ALU.add).then_inc(m["x2_ready"], 1)

            def x_count(t):
                return 16 * (t // 2 + 1) if isinstance(t, int) else count[0]

            count = [0]

            def second_norm(t, par, rows):
                dve.wait_ge(m["sqb_done"], t + 1)
                nc.vector.tensor_scalar(stat[0:rows, par, 5:6], stat[0:rows, par, 4:5], 1.0 / D, EPS, ALU.mult, ALU.add).then_inc(m["msb_ready"], 1)
                dve.wait_ge(m["rtb_done"], t + 1)
                nc.vector.reciprocal(stat[0:rows, par, 7:8], stat[0:rows, par, 6:7]).then_inc(m["rb_ready"], 1)
                dve.wait_ge(m["xt_ready"], t + 1)
                nc.vector.tensor_tensor(xT[:, :, cols(t, rows)], tp[:, :, 0:rows],
                                        c.g_ffn[:].unsqueeze(2).to_broadcast((P, KC, rows)), ALU.mult).then_inc(m["xt_done"], 1)

            def step(k, par):
                if has(k, 0):
                    groups(k, par, has(k, 0))
                if has(k, 1):
                    product(k - 1, 1 - par, has(k, 1))
                if has(k, 2):
                    second_norm(k - 2, par, has(k, 2))

            step(0, 0)
            step(1, 1)
            with dve.Fori(1, PT // 2) as i:
                count[0] = 16 * i
                step(2 * i, 0)
                count[0] = 16 * (i + 1)
                step(2 * i + 1, 1)
            step(PT, 0)
            step(PT + 1, 1)
            step(PT + 2, 0)


TB = 32
QB = P // TB
U_SLOTS = 8
V_SLOTS = 4
XB_SLOTS = 2
TOPK = 16
NG = 4
GSTEPS = 10
FIND = 10
CHOOSE = 44
EXPS = 58
RSTEPS = 75
R_COUNT = 117
TURN = 19


def expert_stage(nc, a, c, x_parts, x_res, x_turned):
    expert_u, expert_v = a["expert_u"][0], a["expert_v"][0]
    y_prompt, y_sample = a["y_prompt"], a["y_sample"]
    NB = NTOK // TB
    assert NB == QB * PT + 1 and NS == TB
    U_USES, V_USES = TB // U_SLOTS, TB // V_SLOTS
    HALVES = [slice(h, h + HALF) for h in range(0, D, HALF)]
    w_view = a["w_query"][0].rearrange("(k p) n -> p k n", p=P)
    H, K = HEADS, TOPK
    with ExitStack() as ctx:
        shop = Shop(nc, ctx, "expert_stage")
        sb, sem, ps = shop.sb, shop.sem, shop.ps
        passed = sem("passed")
        w, xt = sb("wq", [P, KC, NG * HALF]), sb("xt", [P, KC, P])
        keyT = sb("keyT", [P, 2 * H, P])
        q_tok, qT = sb("q_tok", [P, HALF]), sb("qT_r", [P, 4, P])
        sc = sb("sc", [P, 2, 4, P])
        best, best_at = sb("best", [P, 2 * H * K]), sb("best_at", [P, 2 * H * K], U32)
        cand, left = sb("cand", [P, H, K * K]), sb("left", [P, H, K * K])
        at = cand[:, 0]
        rest = left[:, 0:2].rearrange("p a n -> p (a n)").rearrange("p (a e) -> p a e", e=P)
        keys = left[:].rearrange("p a n -> p (a n)").rearrange("p (a e) -> p a e", e=P)
        hit = left[:].rearrange("p h (q k) -> p (h q) k", k=K)
        score, pos = sb("score", [P, H * K]), sb("pos", [P, H * K], U32)
        digit, dig = sb("digit", [P, 2, H * K], U32), sb("dig", [P, 2, H * K])
        opt, opt_i = sb("opt", [P, K]), sb("opt_i", [P, K], I32)
        number = sb("number", [P, 3, H * K])
        gate, total, share = sb("gate", [P, H * K]), sb("total", [P, 2, H]), sb("share", [P, H * K])
        idxT, gateT = sb("idxT", [P, (PT + 1) * P], I32), sb("gateT", [P, (PT + 1) * P])
        u_rows, v_rows = sb("u_rows", [P, U_SLOTS, D]), sb("v_rows", [P, V_SLOTS, D])
        idx_u = [sb(f"idx_u{i}", [P, TB], I32) for i in range(2)]
        idx_v = [sb(f"idx_v{i}", [P, TB], I32) for i in range(2)]
        parts = sb("parts", [3 * TB, 2, D], BF16)
        resid = sb("resid", [TB, D])
        pick, eye = sb("pick", [3 * TB, TB, P], BF16), sb("eye", [P, TB, TB])
        dots, acts, wts = sb("dots", [P, TB]), sb("acts", [P, TB]), sb("wts", [P, TB])
        w_diag = sb("w_diag", [P, 2, TB, TB])
        x_out, y_out, stat, gfin = sb("x_out", [TB, D]), sb("y_out", [TB, D]), sb("y_stat", [TB, 4]), sb("gfin", [TB, D])
        qp, tp = ps("qp", [P, HALF]), ps("tp_r", [P, 4, P])
        xb, acc = ps("xb", [P, XB_SLOTS, D]), ps("y_acc", [TB, D])

        wq_landed = [sem(f"wq_landed{g}") for g in range(NG)]
        xt_landed, xt_used, keys_landed = sem("xt_landed"), sem("xt_used"), sem("keys_landed")
        keys_turned, keys_kept = sem("keys_turned"), sem("keys_kept")
        q_summed, q_kept, q_turned, qT_kept = sem("q_summed"), sem("q_kept"), sem("q_turned"), sem("qT_kept")
        scored, sc_kept = sem("scored"), sem("sc_kept")
        opt_ready, step = sem("opt_ready"), sem("step")
        exp_in, exp_done, chosen, turned, kept = (
            sem("exp_in"), sem("exp_done"), sem("chosen"), sem("turned"), sem("kept"))
        u_landed = [sem(f"u_landed{i}") for i in range(U_SLOTS)]
        v_landed = [sem(f"v_landed{i}") for i in range(V_SLOTS)]
        parts_landed = [sem(f"parts_landed{i}") for i in range(2)]
        resid_landed, gfin_landed, out_landed = sem("resid_landed"), sem("gfin_landed"), sem("out_landed")
        const_ready = sem("const_ready")
        idx_u_ready, idx_v_ready = sem("idx_u_ready"), sem("idx_v_ready")
        xb_ready, dot_done, v_free = sem("xb_ready"), sem("dot_done"), sem("v_free")
        gelu_done, w_ready, acc_read = sem("gelu_done"), sem("w_ready"), sem("acc_read")
        wts_ready, sq_done, ms_done, rt_done, rinv_ready = (
            sem("wts_ready"), sem("sq_done"), sem("ms_done"), sem("rt_done"), sem("rinv_ready"))
        y_ready, y_free = sem("y_ready"), sem("y_free")

        block = ctx.enter_context(nc.Block())
        first = lambda r: isinstance(r, int) and r == 0

        @block.gpsimd
        def _(pool):
            nc.gpsimd.iota(opt_i[:], pattern=[[1, K]], base=0, channel_multiplier=0).then_inc(opt_ready, 1)
            nc.gpsimd.memset(pick[:], 0.0).then_inc(const_ready, 1)
            nc.gpsimd.memset(eye[:], 0.0).then_inc(const_ready, 1)
            pool.wait_ge(const_ready, 2)
            for part in range(3):
                nc.gpsimd.affine_select(out=pick[:], in_=pick[:], compare_op=ALU.not_equal, fill=1.0,
                                        base=-TB * part, pattern=[[-1, TB], [0, P]],
                                        channel_multiplier=1).then_inc(const_ready, 1)
                pool.wait_ge(const_ready, 3 + part)
            nc.gpsimd.affine_select(out=eye[:], in_=eye[:], compare_op=ALU.not_equal, fill=1.0, base=0,
                                    pattern=[[1, TB], [-1, TB]], channel_multiplier=0).then_inc(const_ready, 1)
            pool.sem_inc(v_free, V_SLOTS)

            def gather_u(b, t, par):
                if t == 0:
                    pool.wait_ge(idx_u_ready, b + 1)
                if not isinstance(b, int) or TB * b + t >= U_SLOTS:
                    pool.wait_ge(dot_done, TB * b + t - U_SLOTS + 1)
                pool.sem_inc(passed, 1)
                nc.gpsimd.indirect_dma_start(
                    u_rows[:, t % U_SLOTS, :], None, expert_u,
                    bass.IndirectOffsetOnAxis(ap=idx_u[par][:, t:t + 1], axis=0)).then_inc(u_landed[t % U_SLOTS], 16)

            def gather_v(b, t, par):
                if t == 0:
                    pool.wait_ge(idx_v_ready, b + 1)
                pool.wait_ge(v_free, TB * b + t + 1)
                pool.sem_inc(passed, 1)
                nc.gpsimd.indirect_dma_start(
                    v_rows[:, t % V_SLOTS, :], None, expert_v,
                    bass.IndirectOffsetOnAxis(ap=idx_v[par][:, t:t + 1], axis=0)).then_inc(v_landed[t % V_SLOTS], 16)

            for t in range(TB):
                gather_u(0, t, 0)
            with pool.Fori(0, PT) as tile:
                for j in range(QB):
                    for t in range(TB):
                        gather_u(QB * tile + j + 1, t, (j + 1) % 2)
                        gather_v(QB * tile + j, t, j % 2)
            for t in range(TB):
                gather_v(NB - 1, t, 0)

        @block.sync
        def _(sp):
            def load_tokens(r):
                sp.dma_start(xt[:].rearrange("p k n -> p (k n)"),
                             x_turned[bass.ds(r, 1)].rearrange("a p k n -> (a p) (k n)")).then_inc(xt_landed, 16)

            def load_parts(b, par):
                for part in range(3):
                    sp.dma_start(parts[part * TB:(part + 1) * TB, par, :],
                                 x_parts[part, bass.ds(b * TB, TB), :]).then_inc(parts_landed[par], 16)

            def load_resid(b):
                sp.dma_start(resid[:], x_res[bass.ds(b * TB, TB), :]).then_inc(resid_landed, 16)

            def store(b, rows):
                sp.wait_ge(y_ready, b + 1)
                sp.dma_start(rows, y_out[:]).then_inc(out_landed, 16)
                sp.wait_ge(out_landed, 16 * b + 16)
                sp.sem_inc(y_free, 1)

            sp.sem_inc(y_free, 1)
            load_tokens(0)
            for g in range(NG):
                cut = slice(g * HALF, (g + 1) * HALF)
                sp.dma_start(w[:, :, cut], w_view[:, :, cut]).then_inc(wq_landed[g], 16)
                if g == 0:
                    sp.dma_start(keys, a["sub_keys"][0].rearrange("h s n e -> n (h s) e")).then_inc(keys_landed, 16)
            sp.dma_start(gfin[:], a["g_final"].unsqueeze(0).to_broadcast((TB, D))).then_inc(gfin_landed, 16)
            load_parts(0, 0)
            load_parts(1, 1)
            load_resid(0)
            sp.wait_ge(xt_used, 1)
            load_tokens(1)

            def block_done(b, j, rows):
                sp.wait_ge(dot_done, TB * (b + 1))
                if not isinstance(b, int) or b + 2 < NB:
                    load_parts(b + 2, j % 2)
                store(b, rows)
                if not isinstance(b, int) or b + 1 < NB:
                    load_resid(b + 1)

            with sp.Fori(0, PT - 1) as tile:
                for j in range(QB):
                    if j == 2:
                        sp.wait_ge(xt_used, tile + 2)
                        load_tokens(tile + 2)
                    b = QB * tile + j
                    block_done(b, j, y_prompt[bass.ds(b * TB, TB), :])
            for b in range(QB * (PT - 1), NB - 1):
                block_done(b, b % QB, y_prompt[b * TB:(b + 1) * TB, :])
            block_done(NB - 1, 0, y_sample)

        @block.tensor
        def _(pe):
            def turn_keys(g):
                if g:
                    pe.wait_ge(keys_kept, g)
                for n in range(4):
                    last = nc.tensor.transpose(tp[:, n, :], keys[:, 4 * g + n, :], c.ident[:])
                last.then_inc(keys_turned, 1)

            def route(r, i):
                g, part = divmod(i, GSTEPS)
                if g < NG and part < KC:
                    if i == 0:
                        pe.wait_ge(xt_landed, 16 * (r + 1))
                    if first(r) and part == 0:
                        pe.wait_ge(wq_landed[g], 16)
                    if part == 0 and not (first(r) and g == 0):
                        pe.wait_ge(q_kept, NG * r + g)
                    last = nc.tensor.matmul(qp[:], xt[:, part, :], w[:, part, g * HALF:(g + 1) * HALF],
                                            start=(part == 0), stop=(part == KC - 1))
                    if part == KC - 1:
                        last.then_inc(q_summed, 1)
                        if g == NG - 1:
                            pe.wait_ge(q_summed, NG * r + g + 1)
                            pe.sem_inc(xt_used, 1)
                elif g < NG and part == KC:
                    pe.wait_ge(q_kept, NG * r + g + 1)
                    if g:
                        pe.wait_ge(sc_kept, NG * r + g)
                    elif first(r):
                        pe.wait_ge(keys_kept, NG)
                    else:
                        pe.wait_ge(kept, r)
                    for n in range(4):
                        last = nc.tensor.transpose(tp[:, n, :], q_tok[:, n * P:(n + 1) * P], c.ident[:])
                    last.then_inc(q_turned, 1)
                elif g < NG:
                    pe.wait_ge(qT_kept, NG * r + g + 1)
                    for n in range(4):
                        last = nc.tensor.matmul(tp[:, n, :], qT[:, n, :], keyT[:, 4 * g + n, :], start=True, stop=True)
                    last.then_inc(scored, 1)
                elif i == RSTEPS - 1:
                    pe.wait_ge(chosen, r + 1)
                    nc.tensor.transpose(tp[:, 0, :], share[:], c.ident[:])
                    nc.tensor.transpose(tp[:, 1, :], number[:, 2, :], c.ident[:]).then_inc(turned, 1)

            def broadcast(b, t, par, loads):
                if t == 0:
                    pe.wait_ge(parts_landed[par], 48 * loads)
                if not isinstance(b, int) or TB * b + t >= XB_SLOTS:
                    pe.wait_ge(dot_done, TB * b + t - XB_SLOTS + 1)
                for half in HALVES:
                    last = nc.tensor.matmul(xb[:, t % XB_SLOTS, half], pick[:, t, :], parts[:, par, half],
                                            start=True, stop=True)
                last.then_inc(xb_ready, 1)

            def combine(b, t, par):
                if t == 0:
                    pe.wait_ge(w_ready, b + 1)
                    pe.wait_ge(acc_read, b + 1)
                pe.wait_ge(v_landed[t % V_SLOTS], 16 * (V_USES * b + t // V_SLOTS + 1))
                for half in HALVES:
                    last = nc.tensor.matmul(acc[:, half], w_diag[:, par, t, :], v_rows[:, t % V_SLOTS, half],
                                            start=(t == 0), stop=(t == TB - 1))
                last.then_inc(v_free, 1)

            pe.wait_ge(keys_landed, 16)
            for g in range(NG):
                turn_keys(g)
            for i in range(RSTEPS):
                route(0, i)
            pe.wait_ge(const_ready, 6)
            for t in range(TB):
                broadcast(0, t, 0, 1)
            with pe.Fori(0, PT) as tile:
                for j in range(QB):
                    b = QB * tile + j
                    for t in range(TB):
                        broadcast(b + 1, t, (j + 1) % 2, 2 * tile + (j + 1) // 2 + 1)
                        combine(b, t, j % 2)
                        route(tile + 1, TB * j + t)
            for t in range(TB):
                combine(NB - 1, t, 0)

        @block.scalar
        def _(act):
            def route(r, i):
                g, part = divmod(i, GSTEPS)
                if g < NG and part == KC - 1:
                    act.wait_ge(q_summed, NG * r + g + 1)
                    if not (first(r) and g == 0):
                        act.wait_ge(q_turned, NG * r + g)
                    nc.scalar.activation(q_tok[:], qp[:], ACT.Copy).then_inc(q_kept, 1)
                elif g < NG and part == KC:
                    act.wait_ge(q_turned, NG * r + g + 1)
                    nc.scalar.activation(qT[:], tp[:], ACT.Copy).then_inc(qT_kept, 1)
                elif g < NG and part == KC + 1:
                    act.wait_ge(scored, NG * r + g + 1)
                    if g >= 2:
                        act.wait_ge(step, R_COUNT * r + 16 * (g - 1))
                    elif not first(r):
                        act.wait_ge(step, R_COUNT * (r - 1) + 16 * (g + 3))
                    nc.scalar.activation(sc[:, g % 2], tp[:], ACT.Copy).then_inc(sc_kept, 1)
                elif i == EXPS:
                    act.wait_ge(exp_in, r + 1)
                    nc.scalar.activation(gate[:], gate[:], ACT.Exp).then_inc(exp_done, 1)
                elif i == RSTEPS - 1:
                    act.wait_ge(turned, r + 1)
                    act.sem_inc(passed, 1)
                    nc.scalar.activation(gateT[:, cols(r)], tp[:, 0, :], ACT.Copy)
                    nc.scalar.activation(idxT[:, cols(r)], tp[:, 1, :], ACT.Copy).then_inc(kept, 1)

            def gelu(b):
                act.wait_ge(dot_done, TB * b + TB)
                nc.scalar.activation(acts[:], dots[:], ACT.Gelu_apprx_tanh).then_inc(gelu_done, 1)

            def norm(b):
                act.wait_ge(acc_read, b + 2)
                act.wait_ge(y_free, b + 1)
                nc.scalar.activation(y_out[:], x_out[:], ACT.Square, accum_out=stat[:, 0:1]).then_inc(sq_done, 1)
                act.wait_ge(ms_done, b + 1)
                nc.scalar.activation(stat[:, 2:3], stat[:, 1:2], ACT.Sqrt).then_inc(rt_done, 1)

            for g in range(NG):
                act.wait_ge(keys_turned, g + 1)
                nc.scalar.activation(keyT[:, 4 * g:4 * g + 4, :], tp[:], ACT.Copy).then_inc(keys_kept, 1)
            for i in range(RSTEPS):
                route(0, i)
            gelu(0)
            with act.Fori(0, PT) as tile:
                for j in range(QB):
                    for t in range(TB):
                        route(tile + 1, TB * j + t)
                    gelu(QB * tile + j + 1)
                    norm(QB * tile + j)
            norm(NB - 1)

        @block.vector
        def _(dve):
            done = [0]

            def best_keys(r, i):
                g, part = divmod(i - FIND, GSTEPS)
                part_of = lambda x, n, lo: x[:, (4 * g + n) * K + lo:(4 * g + n) * K + lo + 8]
                if part == 0:
                    dve.wait_ge(sc_kept, NG * r + g + 1)
                    dve.sem_inc(passed, 1)
                    for n in range(4):
                        nc.vector.max(part_of(best, n, 0), sc[:, g % 2, n, :]).then_inc(step, 1)
                elif part == 1:
                    for n in range(4):
                        nc.vector.max_index(part_of(best_at, n, 0), part_of(best, n, 0), sc[:, g % 2, n, :])
                        nc.vector.match_replace(rest[:, n, :], part_of(best, n, 0), sc[:, g % 2, n, :], NEG).then_inc(step, 1)
                elif part == 2:
                    for n in range(4):
                        nc.vector.max(part_of(best, n, 8), rest[:, n, :]).then_inc(step, 1)
                else:
                    for n in range(4):
                        nc.vector.max_index(part_of(best_at, n, 8), part_of(best, n, 8), rest[:, n, :]).then_inc(step, 1)
                return 4

            def choose(r, k):
                eight = lambda x, h, lo: x[:, h * K + lo:h * K + lo + 8]
                sv, gv = score[:].rearrange("p (h k) -> p h k", k=K), gate[:].rearrange("p (h k) -> p h k", k=K)
                if k < 2:
                    heads = slice(4 * k, 4 * k + 4)
                    b = best[:].rearrange("p (h s k) -> p h s k", s=2, k=K)[:, heads]
                    nc.vector.tensor_tensor(cand[:, heads].rearrange("p h (i j) -> p h i j", i=K),
                                            b[:, :, 0, :].unsqueeze(3).to_broadcast((P, 4, K, K)),
                                            b[:, :, 1, :].unsqueeze(2).to_broadcast((P, 4, K, K)), ALU.add).then_inc(step, 1)
                    return 1
                if k < 4:
                    for h in range(4 * (k - 2), 4 * (k - 1)):
                        nc.vector.max(eight(score, h, 0), cand[:, h]).then_inc(step, 1)
                    return 4
                if k < 8:
                    for h in range(2 * (k - 4), 2 * (k - 3)):
                        nc.vector.max_index(eight(pos, h, 0), eight(score, h, 0), cand[:, h])
                        nc.vector.match_replace(left[:, h], eight(score, h, 0), cand[:, h], NEG).then_inc(step, 1)
                    return 2
                if k < 10:
                    for h in range(4 * (k - 8), 4 * (k - 7)):
                        nc.vector.max(eight(score, h, 8), left[:, h]).then_inc(step, 1)
                    return 4
                if k < 12:
                    for h in range(4 * (k - 10), 4 * (k - 9)):
                        nc.vector.max_index(eight(pos, h, 8), eight(score, h, 8), left[:, h]).then_inc(step, 1)
                    return 4
                if k == 12:
                    nc.vector.tensor_single_scalar(digit[:, 0], pos[:], 4, ALU.logical_shift_right).then_inc(step, 1)
                    nc.vector.tensor_single_scalar(digit[:, 1], pos[:], K - 1, ALU.bitwise_and).then_inc(step, 1)
                    nc.vector.tensor_tensor(gv, sv, sv[:, :, 0:1].to_broadcast((P, H, K)), ALU.subtract).then_inc(exp_in, 1)
                    return 2
                if k == 13:
                    nc.vector.tensor_copy(dig[:], digit[:]).then_inc(step, 1)
                    nc.vector.tensor_copy(at, best_at[:]).then_inc(step, 1)
                    return 2
                if k < 26:
                    side, k = divmod(k - 14, 6)
                    heads, ranks = slice(4 * (k % 2), 4 * (k % 2) + 4), slice(4 * K * (k % 2), 4 * K * (k % 2) + 4 * K)
                    h4 = hit.rearrange("p (h q) k -> p h q k", q=K)[:, heads]
                    if k < 2:
                        nc.vector.tensor_tensor(hit[:, ranks], dig[:, side, ranks].unsqueeze(2).to_broadcast((P, 4 * K, K)),
                                                opt[:].unsqueeze(1).to_broadcast((P, 4 * K, K)), ALU.is_equal).then_inc(step, 1)
                    elif k < 4:
                        av = at.rearrange("p (h s k) -> p h s k", s=2, k=K)[:, heads, side, :]
                        nc.vector.tensor_tensor(h4, h4, av.unsqueeze(2).to_broadcast((P, 4, K, K)), ALU.mult).then_inc(step, 1)
                    else:
                        nc.vector.tensor_reduce(number[:, side, ranks], hit[:, ranks], AX.X, ALU.add).then_inc(step, 1)
                    return 1
                if k == 26:
                    if not first(r):
                        dve.wait_ge(turned, r)
                    nc.vector.scalar_tensor_tensor(out=number[:, 2], in0=number[:, 0], scalar=float(P), in1=number[:, 1],
                                                   op0=ALU.mult, op1=ALU.add).then_inc(step, 1)
                    dve.wait_ge(exp_done, r + 1)
                    nc.vector.tensor_reduce(total[:, 0], gv, AX.X, ALU.add).then_inc(step, 1)
                    return 2
                if k == 27:
                    nc.vector.reciprocal(total[:, 1], total[:, 0]).then_inc(step, 1)
                    return 1
                nc.vector.tensor_tensor(share[:].rearrange("p (h k) -> p h k", k=K), gv,
                                        total[:, 1].unsqueeze(2).to_broadcast((P, H, K)), ALU.mult).then_inc(chosen, 1)
                return 0

            def route(r, i):
                if i == 0:
                    done[0] = 0
                find = FIND <= i < FIND + GSTEPS * NG and (i - FIND) % GSTEPS < 4
                if not find and not CHOOSE <= i < CHOOSE + 29:
                    return
                if done[0]:
                    dve.wait_ge(step, R_COUNT * r + done[0])
                    dve.sem_inc(passed, 1)
                elif not first(r):
                    dve.wait_ge(chosen, r)
                done[0] += best_keys(r, i) if find else choose(r, i - CHOOSE)
                assert done[0] <= R_COUNT and (i < CHOOSE + 28 or done[0] == R_COUNT), done[0]

            def indices_u(b, par):
                nc.vector.tensor_copy(idx_u[par][:], idxT[:, bass.ds(b * TB, TB)]).then_inc(idx_u_ready, 1)

            def indices_v(b, par):
                nc.vector.tensor_copy(idx_v[par][:], idxT[:, bass.ds(b * TB, TB)]).then_inc(idx_v_ready, 1)

            def dot(b, t):
                dve.wait_ge(u_landed[t % U_SLOTS], 16 * (U_USES * b + t // U_SLOTS + 1))
                dve.wait_ge(xb_ready, TB * b + t + 1)
                nc.vector.tensor_tensor_reduce(
                    out=u_rows[:, t % U_SLOTS, :], in0=u_rows[:, t % U_SLOTS, :], in1=xb[:, t % XB_SLOTS, :],
                    scale=1.0, scalar=0.0, op0=ALU.mult, op1=ALU.add, accum_out=dots[:, t:t + 1]).then_inc(dot_done, 1)

            def weigh(b, par):
                dve.wait_ge(gelu_done, b + 1)
                nc.vector.tensor_tensor(wts[:], acts[:], gateT[:, bass.ds(b * TB, TB)], ALU.mult).then_inc(wts_ready, 1)
                dve.wait_ge(wts_ready, b + 1)
                nc.vector.tensor_tensor(w_diag[:, par], wts[:].unsqueeze(2).to_broadcast((P, TB, TB)), eye[:],
                                        ALU.mult).then_inc(w_ready, 1)

            def finish(b):
                dve.wait_ge(v_free, V_SLOTS + TB * b + TB)
                dve.wait_ge(resid_landed, 16 * (b + 1))
                nc.vector.tensor_tensor(x_out[:], acc[:], resid[:], ALU.add).then_inc(acc_read, 1)
                dve.wait_ge(sq_done, b + 1)
                nc.vector.tensor_scalar(stat[:, 1:2], stat[:, 0:1], 1.0 / D, EPS, ALU.mult, ALU.add).then_inc(ms_done, 1)
                dve.wait_ge(rt_done, b + 1)
                nc.vector.reciprocal(stat[:, 3:4], stat[:, 2:3]).then_inc(rinv_ready, 1)
                dve.wait_ge(rinv_ready, b + 1)
                nc.vector.scalar_tensor_tensor(out=y_out[:], in0=x_out[:], scalar=stat[:, 3:4], in1=gfin[:],
                                               op0=ALU.mult, op1=ALU.mult).then_inc(y_ready, 1)
                dve.wait_ge(y_ready, b + 1)
                dve.sem_inc(passed, 1)

            dve.sem_inc(acc_read, 1)
            dve.wait_ge(opt_ready, 1)
            nc.vector.tensor_copy(opt[:], opt_i[:])
            dve.wait_ge(keys_kept, NG)
            for i in range(RSTEPS):
                route(0, i)
            dve.wait_ge(const_ready, 6)
            dve.wait_ge(gfin_landed, 16)
            dve.wait_ge(kept, 1)
            indices_u(0, 0)
            indices_u(1, 1)
            indices_v(0, 0)
            for t in range(TB):
                dot(0, t)
            weigh(0, 0)
            with dve.Fori(0, PT) as tile:
                for j in range(QB):
                    b = QB * tile + j
                    indices_v(b + 1, (j + 1) % 2)
                    for t in range(TB):
                        dot(b + 1, t)
                        route(tile + 1, TB * j + t)
                        if t == TURN:
                            if j == 2:
                                dve.wait_ge(kept, tile + 2)
                                dve.sem_inc(passed, 1)
                            indices_u(b + 2, j % 2)
                    weigh(b + 1, (j + 1) % 2)
                    finish(b)
            finish(NB - 1)


class Consts:
    OLD = (PAST - HALF) // 16
    SK = HALF + DT * OLD


def program(nc, a, dbg=None):
    c = Consts()
    with ExitStack() as ctx:
        s = Shop(nc, ctx, "program")
        c.ident, c.ones = s.sb("ident", [P, P]), s.sb("ones", [P, P])
        c.par, c.coef = s.sb("par", [P, CC, N_ROWS]), s.sb("coef", [P, 2, CC])
        c.g_mix, c.g_ffn = s.sb("g_mix_T", [P, KC]), s.sb("g_ffn_T", [P, KC])
        x_res = nc.dram_tensor("x_res", (NTOK, D), F32, kind="Internal").ap()
        x_parts = nc.dram_tensor("x_parts", (3, NTOK, D), BF16, kind="Internal").ap()
        x_turned = nc.dram_tensor("x_turned", (PT + 1, P, KC, P), F32, kind="Internal").ap()
        with ExitStack() as ctx2:
            s2 = Shop(nc, ctx2, "program")
            xT = s2.sb("xT", [P, KC, NTOK])
            c.mult, c.bias = s2.sb("mult", [P, SEQ]), s2.sb("bias", [P, SEQ])
            c.s_mult, c.s_bias = s2.sb("s_mult", [NS, 2, c.SK + NS]), s2.sb("s_bias", [NS, 2, c.SK + NS])
            c.n_mult, c.n_bias = s2.sb("n_mult", [NS, DB, NS]), s2.sb("n_bias", [NS, DB, NS])
            zT, v_tok = s2.sb("zT", [P, 4 * CC, NTOK]), s2.sb("v_tok", [P, PT + 1, DR])
            with ExitStack() as ctx3:
                s3 = Shop(nc, ctx3, "program")
                c.wgate = s3.sb("wgate", [P, 2, CC, P])
                constants(nc, a, c)
                normed_T(nc, a, c, xT)
                project(nc, a, c, xT, zT, v_tok)
            if dbg:
                dbg(nc, 1, locals())
            y_tok, ysT = s2.sb("y_tok", [P, PT, DR]), s2.sb("ysT", [P, CC, NS])
            attend_prompt(nc, a, c, zT, v_tok, y_tok)
            attend_sample(nc, a, c, zT, v_tok, ysT, xT)
            if dbg:
                dbg(nc, 2, locals())
            merge(nc, a, c, zT, y_tok, ysT, xT, x_res, x_parts, x_turned)
        if dbg:
            dbg(nc, 3, locals())
        expert_stage(nc, a, c, x_parts, x_res, x_turned)


_OUTS = [((1, SEQ, D), 'y_prompt'), ((DB, DT, D), 'y_sample'),
         ((1, 1, SEQ, HEADS, HD), 'k_prompt'), ((1, 1, SEQ, HEADS, HD), 'v_prompt'),
         ((1, DB, DT, HEADS, HD), 'k_sample'), ((1, DB, DT, HEADS, HD), 'v_sample'),
         ((1, 1, CW - 1, DR), 'conv_prompt'), ((1, DB, CW - 1, DR), 'conv_sample'),
         ((1, 1, DR), 'h_prompt'), ((1, DB, DR), 'h_sample')]


def rows_of(ap):
    n = len(ap.shape)
    if n == 5:
        return ap.rearrange("a b t h e -> (a b t) (h e)")
    if n == 4:
        return ap.rearrange("a b t e -> (a b t) e")
    return ap.rearrange("a b e -> (a b) e")


def kernel(**inputs):
    import numpy as _np
    import concourse.bacc as _bacc
    from concourse.bass_utils import run_bass_kernel_spmd as _run

    nc = _bacc.Bacc("TRN2", target_bir_lowering=False, num_devices=1)
    arrays, a = {}, {}
    for name, x in inputs.items():
        arrays[name] = _np.ascontiguousarray(x)
        a[name] = nc.dram_tensor(name, arrays[name].shape, mybir.dt.from_np(arrays[name].dtype), kind="ExternalInput").ap()
    for shape, name in _OUTS:
        a[name] = rows_of(nc.dram_tensor("out_" + name, shape, F32, kind="ExternalOutput").ap())
    program(nc, a)
    r = _run(nc, [arrays], core_ids=[0])
    return tuple(r.results[0]["out_" + name] for _, name in _OUTS)
```

```python
from contextlib import ExitStack

import concourse.bass as bass
from concourse import mybir

F32, BF16, I32, U32 = mybir.dt.float32, mybir.dt.bfloat16, mybir.dt.int32, mybir.dt.uint32
ALU, ACT, AX = mybir.AluOpType, mybir.ActivationFunctionType, mybir.AxisListType
EPS = 1e-6
P = 128
HALF = 512
D = 1024
KC = D // P
DR = 512
CC = DR // P
SEQ, DB, DT = 1024, 8, 4
NS = DB * DT
NTOK = SEQ + NS
PT = SEQ // P
PAST = 2048
HEADS, HD = 8, 64
LRU_C = 8.0
CW = 4
NEG = -1e30
TAKEN = -3e38
SCALE = HD ** -0.5
NARROW = [(0, HALF), (HALF, 2 * HALF)]
TILES = [(t, P) for t in range(PT)] + [(PT, NS)]

R_CONVW, R_CONVB, R_BA, R_BX, R_LAM, R_GRNN, R_GATT, R_GMIX, R_GFFN, R_SCONV = 0, 4, 5, 6, 7, 8, 9, 10, 12, 14
R_SH = R_SCONV + DB * (CW - 1)
N_ROWS = R_SH + DB


class Shop:

    def __init__(self, nc, ctx, stage):
        self.nc, self.ctx, self.stage, self.sems = nc, ctx, stage, []
        ctx.callback(self.close)

    def close(self):
        for held, sem in self.sems:
            self.nc.sync.sem_clear(sem)
        if self.sems:
            self.nc.all_engine_barrier()
        for held, sem in self.sems:
            held.__exit__(None, None, None)

    def sb(self, name, shape, dt=F32):
        return self.ctx.enter_context(self.nc.sbuf_tensor(name, shape, dt))

    def ps(self, name, shape):
        return self.ctx.enter_context(self.nc.psum_tensor(name, shape, F32))

    def sem(self, name):
        held = self.nc.semaphore(f"{self.stage}_{name}")
        self.sems.append((held, held.__enter__()))
        return self.sems[-1][1]


def cols(tile, rows=P):
    return bass.ds(tile * P, rows)


def constants(nc, a, c):
    with ExitStack() as ctx:
        s = Shop(nc, ctx, "constants")
        table = s.sb("table", [N_ROWS, DR])
        turned = s.ps("turned", [P, CC, 64])
        w1, w2 = c.w1, c.w2
        rows_landed, blocks_landed = s.sem("rows_landed"), s.sem("blocks_landed")
        zeroed, pool_step, turned_ready, params_ready = (
            s.sem("zeroed"), s.sem("pool_step"), s.sem("turned_ready"), s.sem("params_ready"))
        exp_done, step = s.sem("exp_done"), s.sem("step")
        block = ctx.enter_context(nc.Block())

        @block.sync
        def _(sp):
            rows = [(R_CONVW, a["conv_w"][0]), (R_CONVB, a["conv_b"]), (R_BA, a["b_a"]), (R_BX, a["b_x"]),
                    (R_LAM, a["lru_lambda"]), (R_GRNN, a["g_rnn_out"]), (R_GATT, a["g_attn_out"]),
                    (R_GMIX, a["g_mix"][0].rearrange("(r e) -> r e", e=DR)),
                    (R_GFFN, a["g_ffn"][0].rearrange("(r e) -> r e", e=DR)),
                    (R_SCONV, a["state_conv"][0].rearrange("b w e -> (b w) e")), (R_SH, a["state_h"][0])]
            for r, src in rows:
                sp.dma_start(table[r:r + src.shape[0], :], src).then_inc(rows_landed, 16)
            sp.wait_ge(zeroed, 1)
            for g, w in enumerate(("w_a", "w_x")):
                for half in range(2):
                    sp.dma_start(c.wgate[64 * half:64 * half + 64, g, :, 64 * half:64 * half + 64],
                                 a[w][0].rearrange("(t two) i o -> two i t o", two=2)[half]).then_inc(blocks_landed, 16)
            sp.wait_ge(blocks_landed, 64)

        @block.gpsimd
        def _(pool):
            nc.gpsimd.memset(c.wgate[:], 0.0).then_inc(zeroed, 1)
            nc.gpsimd.memset(c.ident[:], 0.0).then_inc(pool_step, 1)
            nc.gpsimd.memset(c.ones[:], 1.0).then_inc(pool_step, 1)
            pool.wait_ge(pool_step, 2)
            nc.gpsimd.affine_select(out=c.ident[:], in_=c.ident[:], compare_op=ALU.not_equal, fill=1.0, base=0,
                                    pattern=[[-1, P]], channel_multiplier=1).then_inc(pool_step, 1)

        @block.tensor
        def _(pe):
            pe.wait_ge(rows_landed, 16 * 11)
            pe.wait_ge(pool_step, 3)
            for t in range(CC):
                last = nc.tensor.transpose(turned[:, t, 0:N_ROWS], table[:, t * P:(t + 1) * P], c.ident[0:N_ROWS, 0:N_ROWS])
            last.then_inc(turned_ready, 1)

        @block.scalar
        def _(act):
            act.wait_ge(params_ready, 1)
            act.wait_ge(step, 1)
            nc.scalar.activation(w2[:], w1[:], ACT.Exp, scale=-1.0).then_inc(exp_done, 1)

        @block.vector
        def _(dve):
            n = [0]

            def then(ins):
                n[0] += 1
                ins.then_inc(step, 1)
                dve.wait_ge(step, n[0])

            dve.wait_ge(turned_ready, 1)
            nc.vector.tensor_copy(c.par[:, :, 0:N_ROWS], turned[:, :, 0:N_ROWS]).then_inc(params_ready, 1)
            dve.wait_ge(params_ready, 1)
            lam = c.par[:, :, R_LAM]
            then(nc.vector.scalar_tensor_tensor(out=w1[:], in0=lam, scalar=-1.0, in1=lam, op0=ALU.mult, op1=ALU.max))
            for g, r in ((c.g_mix, R_GMIX), (c.g_ffn, R_GFFN)):
                then(nc.vector.tensor_copy(g[:].rearrange("p (r t) -> p r t", t=CC),
                                           c.par[:, :, r:r + 2].rearrange("p t r -> p r t")))


def normed_T(nc, a, c, xnT):
    with ExitStack() as ctx:
        s = Shop(nc, ctx, "normed_T")
        XS = 4
        x_in = s.sb("x_in", [P, XS, D])
        xn = s.sb("xn", [P, 2, D])
        squares = s.sb("squares", [P, 2, D])
        stat = s.sb("stat", [P, 2, 4])
        tp = [s.ps(f"tp{i}", [P, KC, P]) for i in range(2)]
        x_landed = [s.sem(f"x_landed{i}") for i in range(XS)]
        x_used, xn_used, tp_used = s.sem("x_used"), s.sem("xn_used"), s.sem("tp_used")
        sq_done, ms_ready, rt_done, rinv_ready = s.sem("sq_done"), s.sem("ms_ready"), s.sem("rt_done"), s.sem("rinv_ready")
        block = ctx.enter_context(nc.Block())
        LOOPS = PT // 2

        @block.sync
        def _(sp):
            sp.sem_inc(x_used, XS)

            def load(t, slot, src, rows=P):
                sp.wait_ge(x_used, t + 1)
                sp.dma_start(x_in[0:rows, slot, :], src).then_inc(x_landed[slot], 16)

            with sp.Fori(0, PT // XS) as i:
                for slot in range(XS):
                    load(XS * i + slot, slot, a["x_prompt"][0, cols(XS * i + slot), :])
            load(PT, 0, a["x_sample"].rearrange("b t d -> (b t) d"), NS)

        @block.scalar
        def _(act):
            def square(t, rows):
                act.wait_ge(x_landed[t % XS], 16 * (t // XS + 1))
                nc.scalar.activation(squares[0:rows, t % 2, :], x_in[0:rows, t % XS, :], ACT.Square,
                                     accum_out=stat[0:rows, t % 2, 0:1]).then_inc(sq_done, 1)

            def norm(t, rows):
                act.wait_ge(ms_ready, t + 1)
                nc.scalar.activation(stat[0:rows, t % 2, 2:3], stat[0:rows, t % 2, 1:2], ACT.Sqrt).then_inc(rt_done, 1)
                act.wait_ge(rinv_ready, t + 1)
                act.wait_ge(xn_used, t + 1)
                nc.scalar.activation(xn[0:rows, t % 2, :], x_in[0:rows, t % XS, :], ACT.Copy,
                                     scale=stat[0:rows, t % 2, 3:4]).then_inc(x_used, 1)

            square(*TILES[0])
            for tile, following in zip(TILES, TILES[1:]):
                square(*following)
                norm(*tile)
            norm(*TILES[-1])

        @block.tensor
        def _(pe):
            pe.sem_inc(xn_used, 2)

            def turn(t, par, rows=P):
                pe.wait_ge(x_used, t + XS + 1)
                pe.wait_ge(tp_used, t + 1)
                for k in range(KC):
                    last = nc.tensor.transpose(tp[par][:, k, 0:rows], xn[0:rows, par, k * P:(k + 1) * P],
                                               c.ident[0:rows, 0:rows])
                last.then_inc(xn_used, 1)

            with pe.Fori(0, LOOPS) as i:
                for par in range(2):
                    turn(2 * i + par, par)
            turn(PT, 0, NS)

        @block.vector
        def _(dve):
            dve.sem_inc(tp_used, 2)

            def root(t, par, rows=P):
                dve.wait_ge(sq_done, t + 1)
                nc.vector.tensor_scalar(stat[0:rows, par, 1:2], stat[0:rows, par, 0:1], 1.0 / D, EPS,
                                        ALU.mult, ALU.add).then_inc(ms_ready, 1)
                dve.wait_ge(rt_done, t + 1)
                nc.vector.reciprocal(stat[0:rows, par, 3:4], stat[0:rows, par, 2:3]).then_inc(rinv_ready, 1)

            def keep(t, par, rows=P):
                dve.wait_ge(xn_used, t + 3)
                nc.vector.tensor_tensor(xnT[:, :, cols(t, rows)], tp[par][:, :, 0:rows],
                                        c.g_mix[:].unsqueeze(2).to_broadcast((P, KC, rows)),
                                        ALU.mult).then_inc(tp_used, 1)

            root(0, 0)
            with dve.Fori(0, LOOPS - 1) as i:
                for par in range(2):
                    root(2 * i + par + 1, 1 - par)
                    keep(2 * i + par, par)
            root(PT - 1, 1)
            keep(PT - 2, 0)
            root(PT, 0, NS)
            keep(PT - 1, 1)
            keep(PT, 0, NS)


def project(nc, a, c, xnT, zT, v_tok):
    w_view = a["w_in"][0].rearrange("(k p) n -> p k n", p=P)
    with ExitStack() as ctx:
        s = Shop(nc, ctx, "project")
        w = s.sb("w", [P, 2, KC, P])
        wv = s.sb("wv", [P, KC, DR])
        k_tok = s.sb("k_tok", [P, 2, DR])
        xc, gr, gi, th = s.sb("xc", [P, NTOK]), s.sb("gr", [P, NTOK]), s.sb("gi", [P, NTOK]), s.sb("th", [P, NTOK])
        dist, bits = gr[:].bitcast(I32), gi[:].bitcast(I32)
        jrow, jf = s.sb("jrow", [NS, 2], I32), s.sb("jf", [NS, 1])
        iota_ready, mask_done, coef_ready = s.sem("iota_ready"), s.sem("mask_done"), s.sem("coef_ready")
        hist = s.sb("hist", [P, DB, CW - 1 + DT])
        last_in = s.sb("last_in", [P, CC, 36])
        last_rows = s.sb("last_rows", [36, DR])
        zp = [s.ps(f"zp{i}", [P, SEQ]) for i in range(2)]
        zs = [s.ps(f"zs{i}", [P, HALF]) for i in range(2)]
        gp = [s.ps(f"gp{i}", [P, HALF]) for i in range(2)]
        lp = gp[0][0:36, :]
        w_landed = [s.sem(f"w_landed{i}") for i in range(2)]
        wv_landed = s.sem("wv_landed")
        w_used, z_free, z_ready = s.sem("w_used"), s.sem("z_free"), s.sem("z_ready")
        tok_ready, v_done, k_done, v_landed = s.sem("tok_ready"), s.sem("v_done"), s.sem("k_done"), s.sem("v_landed")
        k_landed = [s.sem(f"k_landed{i}") for i in range(2)]
        xc_ready, gp_free = s.sem("xc_ready"), s.sem("gp_free")
        a_done, gx_ready, sq_done, gelu_done, c_done = (
            s.sem("a_done"), s.sem("gx_ready"), s.sem("sq_done"), s.sem("gelu_done"), s.sem("c_done"))
        step, lp_ready, last_ready, last_landed = s.sem("step"), s.sem("lp_ready"), s.sem("last_ready"), s.sem("last_landed")
        NZ = 4 * CC
        block = ctx.enter_context(nc.Block())

        @block.sync
        def _(sp):
            sp.sem_inc(w_used, 2)

            def load(place, tile, par):
                sp.wait_ge(w_used, place + 1)
                sp.dma_start(w[:, par], w_view[:, :, bass.ds(tile * P, P)]).then_inc(w_landed[par], 16)

            with sp.Fori(0, CC // 2) as i:
                for par in range(2):
                    load(2 * i + par, 2 * i + par, par)
            with sp.Fori(0, CC) as t:
                load(CC + 2 * t, CC + t, 0)
                load(CC + 2 * t + 1, 2 * CC + t, 1)
            with sp.Fori(3 * CC // 2, NZ // 2) as i:
                for par in range(2):
                    load(2 * i + par, 2 * i + par, par)
            sp.dma_start(wv[:], w_view[:, :, NZ * P:]).then_inc(wv_landed, 16)
            for t, rows in TILES:
                sp.wait_ge(k_done, t + 3)
                dst = a["k_prompt"][t * P:(t + 1) * P, :] if t < PT else a["k_sample"]
                sp.dma_start(dst, k_tok[0:rows, t % 2, :]).then_inc(k_landed[t % 2], 16)
                sp.wait_ge(v_done, t + 3)
                dst = a["v_prompt"][t * P:(t + 1) * P, :] if t < PT else a["v_sample"]
                sp.dma_start(dst, v_tok[0:rows, t, :]).then_inc(v_landed, 16)
            sp.wait_ge(last_ready, 1)
            n = DB * (CW - 1)
            sp.dma_start(a["conv_sample"], last_rows[0:n, :]).then_inc(last_landed, 16)
            sp.dma_start(a["conv_prompt"], last_rows[n:n + 3, :]).then_inc(last_landed, 16)
            sp.dma_start(a["h_prompt"], last_rows[n + 3:n + 4, :]).then_inc(last_landed, 16)
            sp.dma_start(a["h_sample"], last_rows[n + 4:n + 12, :]).then_inc(last_landed, 16)
            sp.wait_ge(last_landed, 64)
            sp.wait_ge(v_landed, 16 * len(TILES))
            for par in range(2):
                sp.wait_ge(k_landed[par], 16 * len(TILES[par::2]))

        @block.gpsimd
        def _(pool):
            nc.gpsimd.iota(jrow[:, 0:1], pattern=[[0, 1]], base=0, channel_multiplier=1).then_inc(iota_ready, 1)
            pool.wait_ge(c_done, CC)
            nc.gpsimd.iota(dist[:, 0:SEQ], pattern=[[-1, SEQ]], base=SEQ - P, channel_multiplier=1).then_inc(iota_ready, 1)
            pool.wait_ge(mask_done, 1)
            nc.gpsimd.iota(dist[0:NS, 0:HALF], pattern=[[-1, 4], [-4, P]], base=HALF,
                           channel_multiplier=0).then_inc(iota_ready, 1)
            nc.gpsimd.iota(dist[0:NS, HALF:c.SK], pattern=[[-1, 4], [-16, c.OLD]], base=PAST,
                           channel_multiplier=0).then_inc(iota_ready, 1)
            pool.wait_ge(mask_done, 2)
            nc.gpsimd.iota(dist[0:NS, 0:DB * NS].rearrange("p (b n) -> p b n", b=DB), pattern=[[4, DB], [-1, NS]], base=0,
                           channel_multiplier=0).then_inc(iota_ready, 1)

        @block.tensor
        def _(pe):
            pe.sem_inc(gp_free, 2)

            def tile(n, par, loads):
                pe.wait_ge(w_landed[par], 16 * loads)
                pe.wait_ge(z_free, n + 1)
                for k in range(KC):
                    for lo, hi in NARROW:
                        nc.tensor.matmul(zp[par][:, lo:hi], w[:, par, k, :], xnT[:, k, lo:hi],
                                         start=(k == 0), stop=(k == KC - 1))
                    last = nc.tensor.matmul(zs[par][:, 0:NS], w[:, par, k, :], xnT[:, k, SEQ:NTOK],
                                            start=(k == 0), stop=(k == KC - 1))
                last.then_inc(w_used, 1)

            def gates(t):
                pe.wait_ge(xc_ready, t + 1)
                n = 0
                for g in range(2):
                    for lo, hi in NARROW + [(SEQ, NTOK)]:
                        pe.wait_ge(gp_free, 6 * t + n + 1)
                        nc.tensor.matmul(gp[n % 2][:, 0:hi - lo], c.wgate[:, g, t, :], xc[:, lo:hi],
                                         start=True, stop=True).then_inc(z_ready, 1)
                        n += 1

            with pe.Fori(0, CC // 2) as i:
                for par in range(2):
                    tile(2 * i + par, par, i + 1)
            for t in range(CC):
                for par in range(2):
                    tile(CC + 2 * t + par, par, CC // 2 + t + 1)
                gates(t)
            with pe.Fori(3 * CC // 2, NZ // 2) as i:
                for par in range(2):
                    tile(2 * i + par, par, i + 1)
            pe.wait_ge(wv_landed, 16)
            pe.wait_ge(z_free, NZ + 2)
            for t, rows in TILES:
                pe.wait_ge(v_done, t + 1)
                pe.wait_ge(k_done, t + 1)
                for k in range(KC):
                    last = nc.tensor.matmul(zp[t % 2][0:rows, 0:DR], xnT[:, k, t * P:t * P + rows], wv[:, k, :],
                                            start=(k == 0), stop=(k == KC - 1))
                for j in range(CC):
                    last = nc.tensor.transpose(zp[t % 2][0:rows, DR + j * P:DR + (j + 1) * P],
                                               zT[:, 3 * CC + j, t * P:t * P + rows], c.ident[:])
                last.then_inc(tok_ready, 1)
            pe.wait_ge(c_done, CC)
            for j in range(CC):
                last = nc.tensor.transpose(lp[:, j * P:(j + 1) * P], last_in[:, j, :], c.ident[:])
            last.then_inc(lp_ready, 1)

        @block.scalar
        def _(act):
            act.sem_inc(z_free, 2)
            act.sem_inc(v_done, 2)

            def keep(place, n, par):
                act.wait_ge(w_used, place + 3)
                nc.scalar.activation(zT[:, n, 0:SEQ], zp[par][:], ACT.Copy)
                nc.scalar.activation(zT[:, n, SEQ:NTOK], zs[par][:, 0:NS], ACT.Copy).then_inc(z_free, 1)

            def keep_at(i, par):
                n = 2 * i + par
                act.wait_ge(w_used, n + 3)
                nc.scalar.activation(zT[:, bass.ds(n, 1), 0:SEQ].rearrange("p a n -> p (a n)"), zp[par][:],
                                     ACT.Copy)
                nc.scalar.activation(zT[:, bass.ds(n, 1), SEQ:NTOK].rearrange("p a n -> p (a n)"), zs[par][:, 0:NS],
                                     ACT.Copy).then_inc(z_free, 1)

            with act.Fori(0, CC // 2) as i:
                for par in range(2):
                    keep_at(i, par)
            for t in range(CC):
                keep(CC + 2 * t, CC + t, 0)
                keep(CC + 2 * t + 1, 2 * CC + t, 1)
                n = 0
                for g, (buf, row) in enumerate(((gr, R_BA), (gi, R_BX))):
                    for lo, hi in NARROW + [(SEQ, NTOK)]:
                        act.wait_ge(z_ready, 6 * t + n + 1)
                        if t > 0 and n == 0:
                            act.wait_ge(c_done, t)
                        nc.scalar.activation(buf[:, lo:hi], gp[n % 2][:, 0:hi - lo], ACT.Sigmoid,
                                             bias=c.par[:, t, row:row + 1]).then_inc(gp_free, 1)
                        n += 1
                act.wait_ge(gp_free, 6 * t + 8)
                act.wait_ge(coef_ready, 1)
                nc.scalar.activation(th[:], gr[:], ACT.Tanh, scale=c.coef[:, 1, t:t + 1]).then_inc(a_done, 1)
                act.wait_ge(a_done, 2 * t + 1)
                nc.scalar.activation(gr[:], gr[:], ACT.Exp, scale=c.coef[:, 0, t:t + 1]).then_inc(a_done, 1)
                act.wait_ge(gx_ready, t + 1)
                nc.scalar.activation(th[:], th[:], ACT.Sqrt).then_inc(sq_done, 1)
                gate = zT[:, CC + t, :]
                act.wait_ge(z_free, CC + 2 * t + 3)
                nc.scalar.activation(gate, gate, ACT.Gelu_apprx_tanh).then_inc(gelu_done, 1)
            with act.Fori(3 * CC // 2, NZ // 2) as i:
                for par in range(2):
                    keep_at(i, par)
            for t, rows in TILES:
                act.wait_ge(tok_ready, t + 1)
                nc.scalar.activation(v_tok[0:rows, t, :], zp[t % 2][0:rows, 0:DR], ACT.Copy).then_inc(v_done, 1)

        @block.vector
        def _(dve):
            n = [0]

            def then(ins):
                n[0] += 1
                ins.then_inc(step, 1)
                dve.wait_ge(step, n[0])

            w1, w2, w3 = c.w1, c.w2, c.w3
            lam = c.par[:, :, R_LAM]
            then(nc.vector.tensor_scalar(w3[:], w2[:], 2.0, None, ALU.add))
            then(nc.vector.reciprocal(w1[:], w3[:]))
            then(nc.vector.tensor_tensor(w2[:], w2[:], w1[:], ALU.mult))
            then(nc.vector.tensor_tensor(w3[:], w2[:], w2[:], ALU.mult))
            then(nc.vector.tensor_scalar(w1[:], w3[:], 1.0 / 17, 1.0 / 15, ALU.mult, ALU.add))
            for k in (13, 11, 9, 7, 5, 3, 1):
                then(nc.vector.tensor_tensor(w1[:], w1[:], w3[:], ALU.mult))
                then(nc.vector.tensor_scalar(w1[:], w1[:], 1.0 / k, None, ALU.add))
            then(nc.vector.tensor_tensor(w1[:], w1[:], w2[:], ALU.mult))
            then(nc.vector.tensor_scalar(w3[:], lam, -1.0, 0.0, ALU.mult, ALU.max))
            then(nc.vector.scalar_tensor_tensor(out=w3[:], in0=w1[:], scalar=2.0, in1=w3[:], op0=ALU.mult, op1=ALU.add))
            then(nc.vector.tensor_scalar(c.coef[:, 0, :], w3[:], -LRU_C, None, ALU.mult))
            then(nc.vector.tensor_scalar(c.coef[:, 1, :], w3[:], LRU_C, None, ALU.mult))
            dve.sem_inc(coef_ready, 1)
            dve.sem_inc(k_done, 2)
            wts = lambda t, j: c.par[:, t, R_CONVW + j:R_CONVW + j + 1]
            for t in range(CC):
                dve.wait_ge(z_free, t + 3)
                xr = zT[:, t, :]
                then(nc.vector.tensor_scalar(xc[:, 0:SEQ], xr[:, 0:SEQ], wts(t, CW - 1), c.par[:, t, R_CONVB:R_CONVB + 1],
                                             ALU.mult, ALU.add))
                for j in range(CW - 2, -1, -1):
                    d = CW - 1 - j
                    then(nc.vector.scalar_tensor_tensor(out=xc[:, d:SEQ], in0=xr[:, 0:SEQ - d], scalar=wts(t, j),
                                                        in1=xc[:, d:SEQ], op0=ALU.mult, op1=ALU.add))
                old = c.par[:, t, R_SCONV:R_SCONV + DB * (CW - 1)].rearrange("p (b w) -> p b w", b=DB)
                new = xr[:, SEQ:NTOK].rearrange("p (b w) -> p b w", b=DB)
                nc.vector.tensor_copy(hist[:, :, 0:CW - 1], old).then_inc(step, 1)
                n[0] += 1
                then(nc.vector.tensor_copy(hist[:, :, CW - 1:], new))
                xs = xc[:, SEQ:NTOK].rearrange("p (b w) -> p b w", b=DB)
                then(nc.vector.tensor_scalar(xs, hist[:, :, CW - 1:CW - 1 + DT], wts(t, CW - 1),
                                             c.par[:, t, R_CONVB:R_CONVB + 1], ALU.mult, ALU.add))
                for j in range(CW - 2, -1, -1):
                    ins = nc.vector.scalar_tensor_tensor(out=xs, in0=hist[:, :, j:j + DT], scalar=wts(t, j), in1=xs,
                                                         op0=ALU.mult, op1=ALU.add)
                    if j:
                        then(ins)
                ins.then_inc(xc_ready, 1)
                nc.vector.tensor_copy(last_in[:, t, 0:24].rearrange("p (b w) -> p b w", b=DB),
                                      new[:, :, DT - (CW - 1):]).then_inc(step, 1)
                nc.vector.tensor_copy(last_in[:, t, 24:27], xr[:, SEQ - 3:SEQ]).then_inc(step, 1)
                n[0] += 2
                dve.wait_ge(a_done, 2 * t + 2)
                sq = zT[:, t, :]
                dve.wait_ge(step, n[0])
                then(nc.vector.tensor_tensor(sq, gr[:], gr[:], ALU.mult))
                nc.vector.scalar_tensor_tensor(out=th[:], in0=sq, scalar=1.0, in1=th[:], op0=ALU.add,
                                               op1=ALU.mult).then_inc(gx_ready, 1)
                then(nc.vector.tensor_tensor(gi[:], gi[:], xc[:], ALU.mult))
                dve.wait_ge(sq_done, t + 1)
                then(nc.vector.tensor_tensor(gi[:], gi[:], th[:], ALU.mult))
                then(nc.vector.tensor_tensor_scan(th[:, 0:SEQ], gr[:, 0:SEQ], gi[:, 0:SEQ], 0.0, ALU.mult, ALU.add))
                v = lambda x: x[:, SEQ:NTOK].rearrange("p (b w) -> p b w", b=DB)
                prev = c.par[:, t, R_SH:R_SH + DB]
                for j in range(DT):
                    then(nc.vector.tensor_tensor(v(th)[:, :, j], v(gr)[:, :, j], prev, ALU.mult))
                    then(nc.vector.tensor_tensor(v(th)[:, :, j], v(th)[:, :, j], v(gi)[:, :, j], ALU.add))
                    prev = v(th)[:, :, j]
                nc.vector.tensor_copy(last_in[:, t, 27:28], th[:, SEQ - 1:SEQ]).then_inc(step, 1)
                nc.vector.tensor_copy(last_in[:, t, 28:36], prev).then_inc(step, 1)
                n[0] += 2
                dve.wait_ge(gelu_done, t + 1)
                then(nc.vector.tensor_tensor(sq, th[:], zT[:, CC + t, :], ALU.mult))
                dve.sem_inc(c_done, 1)

            def multiplicity(rows, width, out):
                di, bi, df, tm = (x[0:rows, 0:width] for x in (dist, bits, xc, th))
                then(nc.vector.tensor_copy(df, di))
                then(nc.vector.tensor_scalar(out, df, 128.0, None, ALU.is_le))
                for dil, win in ((4, 512.0), (16, 2048.0)):
                    then(nc.vector.tensor_single_scalar(bi, di, dil - 1, ALU.bitwise_and))
                    then(nc.vector.tensor_copy(tm, bi))
                    then(nc.vector.tensor_single_scalar(tm, tm, 0.0, ALU.is_equal))
                    then(nc.vector.scalar_tensor_tensor(out=tm, in0=df, scalar=win, in1=tm, op0=ALU.is_le, op1=ALU.mult))
                    then(nc.vector.tensor_tensor(out, out, tm, ALU.add))
                then(nc.vector.scalar_tensor_tensor(out=out, in0=df, scalar=0.0, in1=out, op0=ALU.is_ge, op1=ALU.mult))

            def bias_of(bias, mult):
                then(nc.vector.tensor_scalar(bias, mult, 0.0, NEG, ALU.is_equal, ALU.mult))

            dve.wait_ge(iota_ready, 2)
            multiplicity(P, SEQ, c.mult[:])
            bias_of(c.bias[:], c.mult[:])
            dve.sem_inc(mask_done, 1)
            then(nc.vector.tensor_single_scalar(jrow[:, 1:2], jrow[:, 0:1], DT - 1, ALU.bitwise_and))
            then(nc.vector.tensor_copy(jf[:], jrow[:, 1:2]))
            new_mult, new_bias = (x[:].rearrange("p b n -> p (b n)") for x in (c.n_mult, c.n_bias))
            for k, (width, out) in enumerate(((c.SK, c.s_mult[:, 0, 0:c.SK]), (DB * NS, new_mult))):
                dve.wait_ge(iota_ready, 4 + k)
                df = xc[0:NS, 0:width]
                then(nc.vector.tensor_copy(df, dist[0:NS, 0:width]))
                then(nc.vector.tensor_scalar(df, df, jf[:, 0:1], None, ALU.add))
                then(nc.vector.tensor_copy(dist[0:NS, 0:width], df))
                multiplicity(NS, width, out)
                if k == 0:
                    dve.sem_inc(mask_done, 1)
            then(nc.vector.tensor_scalar(th[0:NS, 0:DB * NS], df, jf[:, 0:1], None, ALU.is_le))
            then(nc.vector.tensor_tensor(new_mult, new_mult, th[0:NS, 0:DB * NS], ALU.mult))
            bias_of(c.s_bias[:, 0, 0:c.SK], c.s_mult[:, 0, 0:c.SK])
            for x in (c.s_bias, c.s_mult):
                then(nc.vector.tensor_copy(x[:, 1, 0:c.SK], x[:, 0, 0:c.SK]))
            bias_of(new_bias, new_mult)
            for t, rows in TILES:
                dve.wait_ge(tok_ready, t + 1)
                if t >= 2:
                    dve.wait_ge(k_landed[t % 2], 16 * (t // 2))
                nc.vector.tensor_copy(k_tok[0:rows, t % 2, :], zp[t % 2][0:rows, DR:2 * DR]).then_inc(k_done, 1)
            dve.wait_ge(lp_ready, 1)
            nc.vector.tensor_copy(last_rows[:], lp).then_inc(last_ready, 1)


def attend_prompt(nc, a, c, zT, v_tok, yaT):
    PAIRS = HEADS // 2
    UNITS = 2 * PT
    unit = [(0, i) for i in range(PT)] + [(1, i) for i in range(PT - 1, -1, -1)]
    groups = []
    first_group = []
    for n, (h, i) in enumerate(unit):
        first_group.append(len(groups))
        groups += [(n, lo, min(lo + 4, i + 1)) for lo in range(0, i + 1, 4)]
    GROUPS = len(groups)
    first_group.append(GROUPS)
    of_unit = lambda n: range(first_group[n], first_group[n + 1])
    assert GROUPS % 4 == 0 and UNITS % 4 == 0
    with ExitStack() as ctx:
        s = Shop(nc, ctx, "attend_prompt")
        passed = s.sem("passed")
        qT, kT, v = s.sb("qT", [P, SEQ]), s.sb("kT", [P, SEQ]), s.sb("v_pair", [P, PT, 2 * HD])
        logits, prob = s.sb("logits", [P, 2, SEQ]), s.sb("prob", [P, 4, SEQ])
        probT = s.sb("probT", [P, 4, HALF])
        top, neg_top, den, rden = (s.sb(x, [P, 4]) for x in ("top", "neg_top", "den", "rden"))
        sp_ = [s.ps(f"s{i}", [P, SEQ]) for i in range(2)]
        pt = [s.ps(f"pt{i}", [P, HALF]) for i in range(2)]
        o = [s.ps(f"o{i}", [P, HALF]) for i in range(2)]
        q_ready, k_ready, s_ready, s_free = s.sem("q_ready"), s.sem("k_ready"), s.sem("s_ready"), s.sem("s_free")
        v_ready, den_ready = s.sem("v_ready"), s.sem("den_ready")
        top_ready, exp_done, p_ready, rden_ready = s.sem("top_ready"), s.sem("exp_done"), s.sem("p_ready"), s.sem("rden_ready")
        pt_ready, pt_free, o_free = s.sem("pt_ready"), s.sem("pt_free"), s.sem("o_free")
        probT_free = s.sem("probT_free")
        block = ctx.enter_context(nc.Block())

        @block.gpsimd
        def _(pool):
            with pool.Fori(0, PAIRS) as i:
                pool.wait_ge(s_ready, UNITS * i + 1)
                nc.gpsimd.tensor_copy(qT[:], zT[:, bass.ds(i + 2 * CC, 1), 0:SEQ].rearrange("p a n -> p (a n)")).then_inc(q_ready, 1)
                nc.gpsimd.tensor_copy(kT[:], zT[:, bass.ds(i + 3 * CC, 1), 0:SEQ].rearrange("p a n -> p (a n)")).then_inc(k_ready, 1)
                pool.wait_ge(probT_free, GROUPS * i + 4)
                nc.gpsimd.tensor_copy(v[:], v_tok[:, 0:PT, bass.ds(i * 2 * HD, 2 * HD)]).then_inc(v_ready, 1)

        @block.tensor
        def _(pe):
            pe.sem_inc(s_ready, 1)
            pe.sem_inc(probT_free, 4)

            def scores(it, n):
                h, i = unit[n]
                rows, L = slice(HD * h, HD * h + HD), (i + 1) * P
                if n == 0:
                    pe.wait_ge(q_ready, it + 1)
                    pe.wait_ge(k_ready, it + 1)
                pe.wait_ge(s_free, UNITS * it + n + 1)
                for lo in range(0, L, HALF):
                    hi = min(lo + HALF, L)
                    last = nc.tensor.matmul(sp_[n % 2][:, lo:hi], qT[rows, i * P:(i + 1) * P], kT[rows, lo:hi],
                                            start=True, stop=True)
                last.then_inc(s_ready, 1)

            def turn(it, n):
                pe.wait_ge(p_ready, UNITS * it + n + 1)
                for g in of_unit(n):
                    _, lo, hi = groups[g]
                    pe.wait_ge(pt_free, GROUPS * it + g + 1)
                    for b in range(lo, hi):
                        last = nc.tensor.transpose(pt[g % 2][:, (b - lo) * P:(b - lo + 1) * P],
                                                   prob[:, n % 4, b * P:(b + 1) * P], c.ident[:])
                    last.then_inc(pt_ready, 1)

            def values(it, n):
                h, i = unit[n]
                if n == 0:
                    pe.wait_ge(v_ready, it + 1)
                pe.wait_ge(o_free, UNITS * it + n + 1)
                for g in of_unit(n):
                    _, lo, hi = groups[g]
                    pe.wait_ge(pt_free, GROUPS * it + g + 3)
                    for b in range(lo, hi):
                        last = nc.tensor.matmul(o[n % 2][HD * h:HD * h + HD, 0:P], v[:, b, HD * h:HD * h + HD],
                                                probT[:, g % 4, (b - lo) * P:(b - lo + 1) * P],
                                                start=(b == 0), stop=(b == i))
                    last.then_inc(probT_free, 1)

            with pe.Fori(0, PAIRS) as it:
                for k in range(UNITS + 3):
                    if k < UNITS:
                        scores(it, k)
                    if k >= 3:
                        values(it, k - 3)
                    if 2 <= k <= UNITS + 1:
                        turn(it, k - 2)

        @block.scalar
        def _(act):
            act.sem_inc(pt_free, 2)

            def exps(it, n):
                L = (unit[n][1] + 1) * P
                act.wait_ge(top_ready, UNITS * it + n + 1)
                nc.scalar.activation(prob[:, n % 4, 0:L], logits[:, n % 2, 0:L], ACT.Exp, scale=SCALE,
                                     bias=neg_top[:, n % 4:n % 4 + 1]).then_inc(exp_done, 1)

            def keep(it, n):
                for g in of_unit(n):
                    _, lo, hi = groups[g]
                    act.wait_ge(pt_ready, GROUPS * it + g + 1)
                    act.wait_ge(probT_free, GROUPS * it + g + 1)
                    nc.scalar.activation(probT[:, g % 4, 0:(hi - lo) * P], pt[g % 2][:, 0:(hi - lo) * P],
                                         ACT.Copy).then_inc(pt_free, 1)

            def norm(it, n):
                L = (unit[n][1] + 1) * P
                act.wait_ge(rden_ready, UNITS * it + n + 1)
                nc.scalar.activation(prob[:, n % 4, 0:L], prob[:, n % 4, 0:L], ACT.Copy,
                                     scale=rden[:, n % 4:n % 4 + 1]).then_inc(p_ready, 1)

            with act.Fori(0, PAIRS) as it:
                for k in range(UNITS + 2):
                    if k < UNITS:
                        exps(it, k)
                    if 1 <= k <= UNITS:
                        norm(it, k - 1)
                    if k >= 2:
                        keep(it, k - 2)

        @block.vector
        def _(dve):
            dve.sem_inc(s_free, 2)
            dve.sem_inc(o_free, 2)

            def tops(it, n):
                L = (unit[n][1] + 1) * P
                dve.wait_ge(s_ready, UNITS * it + n + 2)
                dve.sem_inc(passed, 1)
                nc.vector.tensor_tensor_reduce(out=logits[:, n % 2, 0:L], in0=sp_[n % 2][:, 0:L],
                                               in1=c.bias[:, SEQ - L:SEQ], scale=1.0, scalar=-3e38, op0=ALU.add,
                                               op1=ALU.max, accum_out=top[:, n % 4:n % 4 + 1]).then_inc(s_free, 1)
                dve.wait_ge(s_free, UNITS * it + n + 3)
                nc.vector.tensor_scalar(neg_top[:, n % 4:n % 4 + 1], top[:, n % 4:n % 4 + 1], -SCALE, None,
                                        ALU.mult).then_inc(top_ready, 1)

            def weigh(it, n):
                L = (unit[n][1] + 1) * P
                dve.wait_ge(exp_done, UNITS * it + n + 1)
                nc.vector.tensor_tensor_reduce(out=prob[:, n % 4, 0:L], in0=prob[:, n % 4, 0:L],
                                               in1=c.mult[:, SEQ - L:SEQ], scale=1.0, scalar=0.0, op0=ALU.mult,
                                               op1=ALU.add, accum_out=den[:, n % 4:n % 4 + 1]).then_inc(den_ready, 1)
                dve.wait_ge(den_ready, UNITS * it + n + 1)
                nc.vector.reciprocal(rden[:, n % 4:n % 4 + 1], den[:, n % 4:n % 4 + 1]).then_inc(rden_ready, 1)

            def keep(it, n):
                h, i = unit[n]
                rows = slice(HD * h, HD * h + HD)
                dve.wait_ge(probT_free, GROUPS * it + first_group[n + 1] + 4)
                dve.sem_inc(passed, 1)
                nc.vector.tensor_copy(yaT[rows, bass.ds(it, 1), i * P:(i + 1) * P].rearrange("p a n -> p (a n)"),
                                      o[n % 2][rows, 0:P]).then_inc(o_free, 1)

            with dve.Fori(0, PAIRS) as it:
                for k in range(UNITS + 4):
                    if k < UNITS:
                        tops(it, k)
                    if 1 <= k <= UNITS:
                        weigh(it, k - 1)
                    if k >= 4:
                        keep(it, k - 4)


def attend_sample(nc, a, c, zT, v_tok, yaT, xT, w_early, early_landed):
    OLD, SK = c.OLD, c.SK
    NW = SK + NS
    with ExitStack() as ctx:
        s = Shop(nc, ctx, "attend_sample")
        passed = s.sem("passed")
        spent = xT[:].rearrange("p k n -> p (k n)")
        kn, vn = (spent[:, i * 8 * DR:(i + 1) * 8 * DR].rearrange("p (a t e) -> p a t e", a=2, t=4) for i in range(2))
        ko, vo = s.sb("ko", [OLD, 2, DT, DR]), s.sb("vo", [OLD, 2, DT, DR])
        q_all = s.sb("q_all", [P, DB, CC, NS])
        q_one = s.sb("q_one", [P, 2, CC, NS])
        ktn, kto = s.sb("ktn", [P, 2, HALF]), s.sb("kto", [P, 2, DT * OLD])
        bias, mult = c.s_bias, c.s_mult
        gate = zT[0:NS, CC:2 * CC, :].rearrange("p a n -> p (a n)")
        logits = gate[:, 0:2 * NW].rearrange("p (a n) -> p a n", a=2)
        prob = gate[:, 2 * NW:4 * NW].rearrange("p (a n) -> p a n", a=2)
        probT = s.sb("probT_s", [P, 9, NS])
        top, den = s.sb("top_s", [NS, 2, 4]), s.sb("den_s", [NS, 2, 2])
        pn, po = s.ps("pn", [P, HALF]), s.ps("po", [P, HALF])
        sn = [s.ps(f"sn{i}", [NS, HALF]) for i in range(2)]
        so = [s.ps(f"so{i}", [NS, HALF]) for i in range(2)]
        pt, ot = s.ps("pt_s", [P, HALF]), s.ps("ot", [NS, HALF])
        o_tok = s.sb("o_tok", [NS, HALF])
        k_landed = [s.sem(f"ks_landed{i}") for i in range(2)]
        v_landed = [s.sem(f"vs_landed{i}") for i in range(2)]
        names = ("s_used", "q_zero", "q_all_ready", "q_ready", "masks_ready", "pn_ready", "po_ready", "pn_free", "po_free",
                 "kt_used", "step", "top_ready", "exp_done", "den_summed", "den_ready", "p_ready", "pt_ready",
                 "pt_free", "pv_done", "o_ready", "o_turned", "out_done")
        m = {x: s.sem(x) for x in names}
        block = ctx.enter_context(nc.Block())
        LOOPS = DB // 2

        @block.sync
        def _(sp):
            row = HEADS * HD

            def load(x, new, old, sem, b, par):
                cache = a[x][0].rearrange("b t h e -> b (t h e)")[bass.ds(b, 1)]
                sp.dma_start(new[:, par].rearrange("p i e -> p (i e)"),
                             cache[:, (PAST - HALF) * row:PAST * row].rearrange(
                                 "a (p f) -> (a p) f", p=P)).then_inc(sem[par], 16)
                sp.dma_start(old[:, par].rearrange("p i e -> p (i e)"),
                             cache[:, 0:(PAST - HALF) * row].rearrange(
                                 "a (p f) -> (a p) f", p=OLD)[:, 0:DT * row]).then_inc(sem[par], 16)

            def load_k(b, par):
                if not (isinstance(b, int) and b < 2):
                    sp.wait_ge(m["kt_used"], CC * (b - 1) + 2)
                load("cache_k", kn, ko, k_landed, b, par)

            def load_v(b, par):
                sp.wait_ge(m["out_done"], b + 1)
                load("cache_v", vn, vo, v_landed, b, par)

            load_k(0, 0)
            load_k(1, 1)
            load_v(0, 0)
            sp.dma_start(w_early, a["w_out"][0, 0:DR, :].rearrange("(j p) n -> p j n", p=P)).then_inc(early_landed, 16)
            with sp.Fori(1, LOOPS) as i:
                load_k(2 * i, 0)
                load_v(2 * i - 1, 1)
                load_k(2 * i + 1, 1)
                load_v(2 * i, 0)
            load_v(DB - 1, 1)

        @block.gpsimd
        def _(pool):
            nc.gpsimd.memset(q_all[:], 0.0).then_inc(m["q_zero"], 1)
            pool.wait_ge(m["q_zero"], 1)
            n = 0
            for j in range(CC):
                for half in range(2):
                    rows, col = slice(HD * half, HD * half + HD), DT * (2 * j + half)
                    nc.gpsimd.tensor_copy(q_all[rows, :, j, col:col + DT],
                                          zT[rows, 2 * CC + j, SEQ:NTOK].rearrange("p (b w) -> p b w", b=DB)
                                          ).then_inc(m["q_all_ready"], 1)
                    n += 1
            pool.wait_ge(m["q_all_ready"], n)
            pool.sem_inc(m["s_used"], 2)
            with pool.Fori(0, LOOPS) as i:
                for par in range(2):
                    b = 2 * i + par
                    pool.wait_ge(m["s_used"], b + 1)
                    nc.gpsimd.tensor_copy(q_one[:, par], q_all[:, bass.ds(b, 1)].rearrange("p a j r -> p (a j) r")
                                          ).then_inc(m["q_ready"], 1)
                    pool.wait_ge(m["out_done"], b + 1)
                    nc.gpsimd.tensor_copy(bias[:, par, SK:NW], c.n_bias[:, bass.ds(b, 1), :].rearrange("p a r -> p (a r)")
                                          ).then_inc(m["masks_ready"], 1)
                    nc.gpsimd.tensor_copy(mult[:, par, SK:NW], c.n_mult[:, bass.ds(b, 1), :].rearrange("p a r -> p (a r)")
                                          ).then_inc(m["masks_ready"], 1)

        @block.tensor
        def _(pe):
            pe.sem_inc(m["kt_used"], 2)

            def scores(b, i, par):
                pe.wait_ge(k_landed[par], 32 * (i + 1))
                pe.wait_ge(m["q_ready"], b + 1)

                def product(j):
                    pe.wait_ge(m["pn_free"], CC * b + j + 2)
                    pe.wait_ge(m["po_free"], CC * b + j + 2)
                    q = q_one[:, par, j, :]
                    nc.tensor.matmul(sn[par][:], q, ktn[:, j % 2, :], start=(j == 0), stop=(j == CC - 1))
                    nc.tensor.matmul(so[par][:, 0:DT * OLD], q, kto[:, j % 2, :], start=(j == 0), stop=(j == CC - 1),
                                     skip_group_check=True)
                    last = nc.tensor.matmul(so[par][:, DT * OLD:DT * OLD + NS], q, zT[:, 3 * CC + j, SEQ:NTOK],
                                            start=False, stop=(j == CC - 1), skip_group_check=True)
                    last.then_inc(m["kt_used"], 1)

                for j in range(CC):
                    pe.wait_ge(m["pn_free"], CC * b + j + 1)
                    for t in range(4):
                        last = nc.tensor.transpose(pn[:, t * P:(t + 1) * P], kn[:, par, t, j * P:(j + 1) * P], c.ident[:])
                    last.then_inc(m["pn_ready"], 1)
                    pe.wait_ge(m["po_free"], CC * b + j + 1)
                    for t in range(DT):
                        last = nc.tensor.transpose(po[:, t * OLD:(t + 1) * OLD], ko[:, par, t, j * P:(j + 1) * P],
                                                   c.ident[0:OLD, 0:OLD])
                    last.then_inc(m["po_ready"], 1)
                    if j:
                        product(j - 1)
                product(CC - 1)

            def values(b, i, par):
                pe.wait_ge(m["out_done"], b + 2)
                pe.wait_ge(m["p_ready"], b + 1)
                pe.sem_inc(passed, 1)
                for t in range(4):
                    nc.tensor.transpose(pt[:, t * NS:(t + 1) * NS], prob[:, par, t * P:(t + 1) * P], c.ident[0:NS, 0:NS])
                for t in range(DT):
                    nc.tensor.transpose(pt[0:OLD, (4 + t) * NS:(5 + t) * NS],
                                        prob[:, par, HALF + t * OLD:HALF + (t + 1) * OLD], c.ident[0:NS, 0:NS])
                nc.tensor.transpose(pt[0:NS, 8 * NS:9 * NS], prob[:, par, SK:NW], c.ident[0:NS, 0:NS]).then_inc(m["pt_ready"], 1)
                pe.wait_ge(v_landed[par], 32 * (i + 1))
                pe.wait_ge(m["pt_free"], b + 1)
                for t in range(4):
                    nc.tensor.matmul(ot[:], probT[:, t, :], vn[:, par, t, :], start=(t == 0), stop=False)
                for t in range(DT):
                    nc.tensor.matmul(ot[:], probT[0:OLD, 4 + t, :], vo[:, par, t, :], start=False, stop=False)
                nc.tensor.matmul(ot[:], probT[0:NS, 8, :], v_tok[0:NS, PT, :], start=False, stop=True).then_inc(m["pv_done"], 1)
                pe.wait_ge(m["o_ready"], b + 1)
                pe.sem_inc(passed, 1)
                for j in range(CC):
                    last = nc.tensor.transpose(pt[:, (9 + j) * NS:(10 + j) * NS], o_tok[:, j * P:(j + 1) * P], c.ident[0:NS, 0:NS])
                last.then_inc(m["o_turned"], 1)

            scores(0, 0, 0)
            with pe.Fori(0, LOOPS - 1) as i:
                scores(2 * i + 1, i, 1)
                values(2 * i, i, 0)
                scores(2 * i + 2, i + 1, 0)
                values(2 * i + 1, i, 1)
            scores(DB - 1, LOOPS - 1, 1)
            values(DB - 2, LOOPS - 1, 0)
            values(DB - 1, LOOPS - 1, 1)

        @block.scalar
        def _(act):
            act.sem_inc(m["pn_free"], 1)

            def keys(b, j):
                act.wait_ge(m["pn_ready"], CC * b + j + 1)
                act.wait_ge(m["kt_used"], CC * b + j + 1)
                nc.scalar.activation(ktn[:, j % 2, :], pn[:], ACT.Copy).then_inc(m["pn_free"], 1)

            def exps(b, par):
                act.wait_ge(m["top_ready"], b + 1)
                nc.scalar.activation(prob[:, par], logits[:, par], ACT.Exp, scale=SCALE,
                                     bias=top[:, par, 2:3]).then_inc(m["exp_done"], 1)

            def norm(b, par):
                act.wait_ge(m["den_ready"], b + 1)
                nc.scalar.activation(prob[:, par], prob[:, par], ACT.Copy, scale=den[:, par, 1:2]).then_inc(m["p_ready"], 1)

            def turned(b):
                act.wait_ge(m["pt_ready"], b + 1)
                act.wait_ge(m["pv_done"], b + 1)
                nc.scalar.activation(probT[:, 0:4], pt[:, 0:4 * NS].rearrange("p (t r) -> p t r", r=NS), ACT.Copy)
                nc.scalar.activation(probT[0:OLD, 4:8], pt[0:OLD, 4 * NS:8 * NS].rearrange("p (t r) -> p t r", r=NS), ACT.Copy)
                nc.scalar.activation(probT[0:NS, 8], pt[0:NS, 8 * NS:9 * NS], ACT.Copy).then_inc(m["pt_free"], 1)

            act.sem_inc(m["pv_done"], 1)
            def rest_of(b, par):
                exps(b, par)
                norm(b, par)
                turned(b)

            def both(b, par):
                keys(b, 0)
                keys(b, 1)
                exps(b - 1, 1 - par)
                keys(b, 2)
                norm(b - 1, 1 - par)
                keys(b, 3)
                turned(b - 1)

            for j in range(CC):
                keys(0, j)
            with act.Fori(0, LOOPS - 1) as i:
                both(2 * i + 1, 1)
                both(2 * i + 2, 0)
            both(DB - 1, 1)
            rest_of(DB - 1, 1)

        @block.vector
        def _(dve):
            dve.sem_inc(m["po_free"], 1)
            dve.sem_inc(m["out_done"], 2)

            def keys(b, j):
                dve.wait_ge(m["po_ready"], CC * b + j + 1)
                dve.wait_ge(m["kt_used"], CC * b + j + 1)
                nc.vector.tensor_copy(kto[:, j % 2, :], po[:, 0:DT * OLD]).then_inc(m["po_free"], 1)

            def tops(b, par):
                dve.wait_ge(m["kt_used"], CC * (b + 1) + 2)
                dve.wait_ge(m["masks_ready"], 2 * b + 2)
                dve.sem_inc(passed, 1)
                nc.vector.tensor_tensor_reduce(out=logits[:, par, 0:HALF], in0=sn[par][:], in1=bias[:, par, 0:HALF],
                                               scale=1.0, scalar=-3e38, op0=ALU.add, op1=ALU.max,
                                               accum_out=top[:, par, 0:1]).then_inc(m["step"], 1)
                dve.wait_ge(m["step"], 2 * b + 1)
                dve.sem_inc(passed, 1)
                nc.vector.tensor_tensor_reduce(out=logits[:, par, HALF:NW], in0=so[par][:, 0:NW - HALF],
                                               in1=bias[:, par, HALF:NW], scale=1.0, scalar=top[:, par, 0:1],
                                               op0=ALU.add, op1=ALU.max, accum_out=top[:, par, 1:2]).then_inc(m["step"], 1)
                dve.wait_ge(m["step"], 2 * b + 2)
                dve.sem_inc(m["s_used"], 1)
                nc.vector.tensor_scalar(top[:, par, 2:3], top[:, par, 1:2], -SCALE, None, ALU.mult).then_inc(m["top_ready"], 1)

            def sums(b, par):
                dve.wait_ge(m["exp_done"], b + 1)
                nc.vector.tensor_tensor_reduce(out=prob[:, par], in0=prob[:, par], in1=mult[:, par], scale=1.0, scalar=0.0,
                                               op0=ALU.mult, op1=ALU.add, accum_out=den[:, par, 0:1]).then_inc(m["den_summed"], 1)
                dve.wait_ge(m["den_summed"], b + 1)
                nc.vector.reciprocal(den[:, par, 1:2], den[:, par, 0:1]).then_inc(m["den_ready"], 1)

            def keep(b, par):
                dve.wait_ge(m["pv_done"], b + 2)
                nc.vector.tensor_copy(o_tok[:], ot[:]).then_inc(m["o_ready"], 1)
                dve.wait_ge(m["o_turned"], b + 1)
                dve.sem_inc(passed, 1)
                for half in range(2):
                    rows = slice(HD * half, HD * half + HD)
                    start, turn = 9 * NS + DT * half, NS + 2 * DT
                    last = nc.vector.tensor_copy(
                        yaT[rows, :, bass.ds(b * DT + SEQ, DT)],
                        pt[rows, start:start + CC * turn].rearrange("p (j w) -> p j w", j=CC)[:, :, 0:DT])
                last.then_inc(m["out_done"], 1)

            def both(b, par):
                keys(b, 0)
                tops(b - 1, 1 - par)
                keys(b, 1)
                keys(b, 2)
                sums(b - 1, 1 - par)
                keys(b, 3)
                keep(b - 1, 1 - par)

            for j in range(CC):
                keys(0, j)
            with dve.Fori(0, LOOPS - 1) as i:
                both(2 * i + 1, 1)
                both(2 * i + 2, 0)
            both(DB - 1, 1)
            tops(DB - 1, 1)
            sums(DB - 1, 1)
            keep(DB - 1, 1)


def merge(nc, a, c, zT, yaT, xT, w_early, early_landed, x_res, x_parts, x_turned):
    with ExitStack() as ctx:
        s = Shop(nc, ctx, "merge")
        passed = s.sem("passed")
        spent = zT[:, CC:4 * CC, :].rearrange("p a n -> p (a n)")
        w_late = spent[:, 0:CC * D].rearrange("p (k n) -> p k n", k=CC)
        x_in = spent[:, CC * D:(CC + 2) * D].rearrange("p (k n) -> p k n", k=2)
        x2 = spent[:, (CC + 2) * D:(CC + 4) * D].rearrange("p (k n) -> p k n", k=2)
        g_row = s.sb("g_row", [P, D])
        sq, yg = s.sb("sq", [P, 2, CC, P]), s.sb("yg", [P, 2, 2, CC, P])
        part_sum, rr = s.sb("part_sum", [P, 2, P]), s.sb("rr", [P, 3, 2, P])
        xn, xf = s.sb("xn2", [P, D]), s.sb("xf", [P, D])
        squares = s.sb("squares2", [P, D])
        pieces = s.sb("pieces", [P, 3, D], BF16)
        stat = s.sb("stat2", [P, 2, 4])
        nothing = s.sb("nothing", [P, KC, P - NS])
        acc = [s.ps(f"acc{i}", [P, D]) for i in range(2)]
        ssb, tp = s.ps("ssb", [P, 2, P]), s.ps("tp2", [P, KC, P])
        x_landed = [s.sem(f"mx_landed{i}") for i in range(2)]
        x2_stored = [s.sem(f"x2_stored{i}") for i in range(2)]
        w_landed, turned_stored, nothing_ready = s.sem("w_out_landed"), s.sem("turned_stored"), s.sem("nothing_ready")
        m = {x: s.sem(x) for x in (
            "w_scaled sq_ready part_ready ssb_ready ms_ready rt_done rr_ready yg_ready summed x2_ready sqb_done msb_ready "
            "rtb_done rb_ready xn_ready xt_ready xt_done xf_ready hi_ready r1_ready mid_ready lo_ready stored").split()}
        block = ctx.enter_context(nc.Block())
        groups_of = ((0, zT, R_GRNN, w_early), (1, yaT, R_GATT, w_late))

        def run(eng, step):
            for k in range(4):
                step(k, k % 2)
            with eng.Fori(2, PT // 2) as i:
                step(2 * i, 0)
                step(2 * i + 1, 1)
            step(PT, 0)
            step(PT + 1, 1)
            step(PT + 2, 0)

        def has(k, back):
            if not isinstance(k, int):
                return P
            t = k - back
            return 0 if t < 0 or t > PT else (NS if t == PT else P)

        def fixed(t, least):
            return isinstance(t, int) and t < least

        @block.sync
        def _(sp):
            for j in range(CC):
                sp.dma_start(w_late[:, j, :], a["w_out"][0, DR + j * P:DR + (j + 1) * P, :]).then_inc(w_landed, 16)
            sp.dma_start(g_row[:], a["g_ffn"].to_broadcast((P, D))).then_inc(w_landed, 16)

            def step(k, par):
                if has(k, 2):
                    sp.wait_ge(m["x2_ready"], k - 1)
                    sp.sem_inc(passed, 1)
                rows = has(k, 0)
                if rows:
                    src = a["x_prompt"][0, cols(k), :] if rows == P else a["x_sample"].rearrange("b t d -> (b t) d")
                    sp.dma_start(x_in[0:rows, par, :], src).then_inc(x_landed[par], 16)
                rows = has(k, 2)
                if rows:
                    t = k - 2
                    sp.dma_start(x_res[bass.ds(t * P, rows), :], x2[0:rows, par, :]).then_inc(x2_stored[par], 16)
                    sp.wait_ge(m["lo_ready"], t + 1)
                    sp.sem_inc(passed, 1)
                    for part in range(3):
                        sp.dma_start(x_parts[part, bass.ds(t * P, rows), :], pieces[0:rows, part, :]).then_inc(m["stored"], 16)
                    sp.wait_ge(m["xt_done"], t + 1)
                    sp.sem_inc(passed, 1)
                    sp.dma_start(x_turned[bass.ds(t, 1), :, :, 0:rows].rearrange("a p k n -> (a p) k n"),
                                 xT[:, :, cols(t, rows)]).then_inc(turned_stored, 16)

            sp.wait_ge(nothing_ready, 1)
            sp.dma_start(x_turned[PT, :, :, NS:P], nothing[:]).then_inc(turned_stored, 16)
            run(sp, step)
            sp.wait_ge(turned_stored, 16 * (PT + 2))
            sp.wait_ge(m["stored"], 48 * (PT + 1))
            sp.wait_ge(x2_stored[0], 16 * (PT // 2 + 1))
            sp.wait_ge(x2_stored[1], 16 * (PT // 2))

        @block.tensor
        def _(pe):
            def groups(k, rows):
                pe.wait_ge(m["part_ready"], k + 1)
                if not fixed(k, 1):
                    pe.wait_ge(m["ms_ready"], k)
                for g in range(2):
                    last = nc.tensor.matmul(ssb[:, g, 0:rows], c.ones[:], part_sum[:, g, 0:rows], start=True, stop=True)
                last.then_inc(m["ssb_ready"], 1)

            def product(t, par, rows):
                pe.wait_ge(m["yg_ready"], t + 1)
                if not fixed(t, 2):
                    pe.wait_ge(m["x2_ready"], t - 1)
                for g, _, _, w_out in groups_of:
                    if isinstance(t, int) and t == 0:
                        pe.wait_ge(m["w_scaled"], CC * (g + 1))
                    for j in range(CC):
                        for lo, hi in NARROW:
                            last = nc.tensor.matmul(acc[par][0:rows, lo:hi], yg[:, par, g, j, 0:rows], w_out[:, j, lo:hi],
                                                    start=(g + j == 0), stop=(g == 1 and j == CC - 1))
                last.then_inc(m["summed"], 1)

            def second_norm(t, rows):
                pe.wait_ge(m["xn_ready"], t + 1)
                if not fixed(t, 1):
                    pe.wait_ge(m["xt_done"], t)
                for j in range(KC):
                    last = nc.tensor.transpose(tp[:, j, 0:rows], xn[0:rows, j * P:(j + 1) * P], c.ident[0:rows, 0:rows])
                last.then_inc(m["xt_ready"], 1)

            def step(k, par):
                if has(k, 0):
                    groups(k, has(k, 0))
                if has(k, 1):
                    product(k - 1, 1 - par, has(k, 1))
                if has(k, 2):
                    second_norm(k - 2, has(k, 2))

            run(pe, step)

        @block.scalar
        def _(act):
            def squares_of(k, rows):
                if not fixed(k, 1):
                    act.wait_ge(m["part_ready"], k)
                    act.sem_inc(passed, 1)
                for g, y, _, _ in groups_of:
                    last = nc.scalar.activation(sq[:, g, :, 0:rows], y[:, 0:CC, cols(k, rows)], ACT.Square)
                last.then_inc(m["sq_ready"], 1)

            def groups(k, rows):
                act.wait_ge(m["ms_ready"], k + 1)
                nc.scalar.activation(rr[:, 1, :, 0:rows], rr[:, 0, :, 0:rows], ACT.Sqrt).then_inc(m["rt_done"], 1)

            def second_norm(t, par, rows):
                act.wait_ge(m["x2_ready"], t + 1)
                nc.scalar.activation(squares[0:rows, :], x2[0:rows, par, :], ACT.Square,
                                     accum_out=stat[0:rows, par, 0:1]).then_inc(m["sqb_done"], 1)
                act.wait_ge(m["msb_ready"], t + 1)
                nc.scalar.activation(stat[0:rows, par, 2:3], stat[0:rows, par, 1:2], ACT.Sqrt).then_inc(m["rtb_done"], 1)
                act.wait_ge(m["rb_ready"], t + 1)
                if not fixed(t, 1):
                    act.wait_ge(m["xt_ready"], t)
                    act.wait_ge(m["xf_ready"], t)
                nc.scalar.activation(xn[0:rows, :], x2[0:rows, par, :], ACT.Copy,
                                     scale=stat[0:rows, par, 3:4]).then_inc(m["xn_ready"], 1)

            def split(t, rows):
                act.wait_ge(m["xf_ready"], t + 1)
                if not fixed(t, 1):
                    act.wait_ge(m["stored"], 48 * t)
                nc.scalar.activation(pieces[0:rows, 0, :], xf[0:rows, :], ACT.Copy).then_inc(m["hi_ready"], 1)
                act.wait_ge(m["r1_ready"], t + 1)
                nc.scalar.activation(pieces[0:rows, 1, :], xf[0:rows, :], ACT.Copy).then_inc(m["mid_ready"], 1)

            def step(k, par):
                if has(k, 0):
                    groups(k, has(k, 0))
                if has(k + 1, 0):
                    squares_of(k + 1, has(k + 1, 0))
                if has(k, 2):
                    second_norm(k - 2, par, has(k, 2))
                    split(k - 2, has(k, 2))

            squares_of(0, P)
            step(0, 0)
            for g, _, row, w_out in groups_of:
                if g == 0:
                    act.wait_ge(early_landed, 16)
                else:
                    act.wait_ge(w_landed, 16 * (CC + 1))
                for j in range(CC):
                    nc.scalar.activation(w_out[:, j, :], w_out[:, j, :], ACT.Copy,
                                         scale=c.par[:, j, row:row + 1]).then_inc(m["w_scaled"], 1)
            for k in range(1, 4):
                step(k, k % 2)
            with act.Fori(2, PT // 2 - 1) as i:
                step(2 * i, 0)
                step(2 * i + 1, 1)
            step(PT - 2, 0)
            step(PT - 1, 1)
            step(PT, 0)
            step(PT + 1, 1)
            step(PT + 2, 0)

        @block.gpsimd
        def _(pool):
            def step(k, par):
                rows = has(k, 2)
                if rows:
                    t = k - 2
                    pool.wait_ge(m["xn_ready"], t + 1)
                    if not fixed(t, 1):
                        pool.wait_ge(m["lo_ready"], t)
                    nc.gpsimd.tensor_tensor(xf[0:rows, :], xn[0:rows, :], g_row[0:rows, :], ALU.mult).then_inc(m["xf_ready"], 1)
                    pool.wait_ge(m["hi_ready"], t + 1)
                    nc.gpsimd.tensor_tensor(xf[0:rows, :], xf[0:rows, :], pieces[0:rows, 0, :], ALU.subtract).then_inc(m["r1_ready"], 1)
                    pool.wait_ge(m["mid_ready"], t + 1)
                    nc.gpsimd.tensor_tensor(pieces[0:rows, 2, :], xf[0:rows, :], pieces[0:rows, 1, :],
                                            ALU.subtract).then_inc(m["lo_ready"], 1)

            nc.gpsimd.memset(nothing[:], 0.0).then_inc(nothing_ready, 1)
            pool.wait_ge(w_landed, 16 * (CC + 1))
            run(pool, step)

        @block.vector
        def _(dve):
            count = [0]

            def partial(k, rows):
                dve.wait_ge(m["sq_ready"], k + 1)
                if not fixed(k, 1):
                    dve.wait_ge(m["ssb_ready"], k)
                nc.vector.tensor_reduce(part_sum[:, :, 0:rows], sq[:, :, :, 0:rows].rearrange("p g j n -> p g n j"),
                                        AX.X, ALU.add).then_inc(m["part_ready"], 1)

            def groups(k, par, rows):
                dve.wait_ge(m["ssb_ready"], k + 1)
                nc.vector.tensor_scalar(rr[:, 0, :, 0:rows], ssb[:, :, 0:rows], 1.0 / DR, EPS, ALU.mult, ALU.add).then_inc(m["ms_ready"], 1)
                dve.wait_ge(m["rt_done"], k + 1)
                nc.vector.reciprocal(rr[:, 2, :, 0:rows], rr[:, 1, :, 0:rows]).then_inc(m["rr_ready"], 1)
                dve.wait_ge(m["rr_ready"], k + 1)
                if not fixed(k, 2):
                    dve.wait_ge(m["summed"], k - 1)
                for g, y, _, _ in groups_of:
                    last = nc.vector.tensor_tensor(yg[:, par, g, :, 0:rows], y[:, 0:CC, cols(k, rows)],
                                                   rr[:, 2, g:g + 1, 0:rows].to_broadcast((P, CC, rows)), ALU.mult)
                last.then_inc(m["yg_ready"], 1)

            def landed(t):
                return 16 * (t // 2 + 1) if isinstance(t, int) else count[0]

            def product(t, par, rows):
                dve.wait_ge(m["summed"], t + 1)
                dve.wait_ge(x_landed[par], landed(t))
                if not fixed(t, 2):
                    dve.wait_ge(x2_stored[par], landed(t) - 16)
                    dve.wait_ge(m["xn_ready"], t - 1)
                nc.vector.tensor_tensor(x2[0:rows, par, :], acc[par][0:rows, :], x_in[0:rows, par, :], ALU.add).then_inc(m["x2_ready"], 1)

            def root(t, par, rows):
                dve.wait_ge(m["sqb_done"], t + 1)
                nc.vector.tensor_scalar(stat[0:rows, par, 1:2], stat[0:rows, par, 0:1], 1.0 / D, EPS, ALU.mult, ALU.add).then_inc(m["msb_ready"], 1)
                dve.wait_ge(m["rtb_done"], t + 1)
                nc.vector.reciprocal(stat[0:rows, par, 3:4], stat[0:rows, par, 2:3]).then_inc(m["rb_ready"], 1)

            def turned(t, rows):
                dve.wait_ge(m["xt_ready"], t + 1)
                nc.vector.tensor_tensor(xT[:, :, cols(t, rows)], tp[:, :, 0:rows],
                                        c.g_ffn[:].unsqueeze(2).to_broadcast((P, KC, rows)), ALU.mult).then_inc(m["xt_done"], 1)

            def step(k, par):
                if has(k, 0):
                    groups(k, par, has(k, 0))
                if has(k + 1, 0):
                    partial(k + 1, has(k + 1, 0))
                if has(k, 2):
                    root(k - 2, par, has(k, 2))
                if has(k, 1):
                    product(k - 1, 1 - par, has(k, 1))
                if has(k, 2):
                    turned(k - 2, has(k, 2))

            partial(0, P)
            for k in range(4):
                step(k, k % 2)
            with dve.Fori(2, PT // 2 - 1) as i:
                count[0] = 16 * i
                step(2 * i, 0)
                count[0] = 16 * (i + 1)
                step(2 * i + 1, 1)
            step(PT - 2, 0)
            step(PT - 1, 1)
            step(PT, 0)
            step(PT + 1, 1)
            step(PT + 2, 0)


TB = 32
QB = P // TB
U_SLOTS = 8
V_SLOTS = 4
XB_SLOTS = 2
TOPK = 16
NG = 4
GSTEPS = 10
FIND = 10
VSTEPS = 14
V_FOUND, V_COUNT = 16, 33
R_COUNT = NG * V_COUNT + 3
EXPS = FIND + NG * VSTEPS
RSTEPS = EXPS + 5
TURN = 19


def expert_stage(nc, a, c, x_parts, x_res, x_turned):
    expert_u, expert_v = a["expert_u"][0], a["expert_v"][0]
    y_prompt, y_sample = a["y_prompt"], a["y_sample"]
    NB = NTOK // TB
    assert NB == QB * PT + 1 and NS == TB
    U_USES, V_USES = TB // U_SLOTS, TB // V_SLOTS
    HALVES = [slice(h, h + HALF) for h in range(0, D, HALF)]
    w_view = a["w_query"][0].rearrange("(k p) n -> p k n", p=P)
    H, K = HEADS, TOPK
    with ExitStack() as ctx:
        shop = Shop(nc, ctx, "expert_stage")
        sb, sem, ps = shop.sb, shop.sem, shop.ps
        passed = sem("passed")
        w, xt = sb("wq", [P, KC, NG * HALF]), sb("xt", [P, KC, P])
        keyT = sb("keyT", [P, 2 * H, P])
        q_tok, qT = sb("q_tok", [P, HALF]), sb("qT_r", [P, 4, P])
        sc = sb("sc", [P, 2, 4, P])
        best, best_at = sb("best", [P, 2 * H * K]), sb("best_at", [P, 2 * H * K], U32)
        cand, left = sb("cand", [P, 2, K * K]), sb("left", [P, 2, K * K])
        hit = sb("hit", [P, 2, 2 * K, K])
        at = cand[:, 0, 0:4 * K]
        rest = left[:].rearrange("p a n -> p (a n)").rearrange("p (a e) -> p a e", e=P)
        score, pos = sb("score", [P, H * K]), sb("pos", [P, H * K], U32)
        digit, dig = sb("digit", [P, 2, 2 * K], U32), sb("dig", [P, 2, 2 * K])
        opt, opt_i = sb("opt", [P, K]), sb("opt_i", [P, K], I32)
        number = sb("number", [P, 3, H * K])
        gate, total, share = sb("gate", [P, H * K]), sb("total", [P, 2, H]), sb("share", [P, H * K])
        idxT, gateT = sb("idxT", [P, (PT + 1) * P], I32), sb("gateT", [P, (PT + 1) * P])
        u_rows, v_rows = sb("u_rows", [P, U_SLOTS, D]), sb("v_rows", [P, V_SLOTS, D])
        keys = v_rows[:, 0:2, :].rearrange("p a (n e) -> p (a n) e", e=P)
        idx_u = [sb(f"idx_u{i}", [P, TB], I32) for i in range(2)]
        idx_v = [sb(f"idx_v{i}", [P, TB], I32) for i in range(2)]
        parts = sb("parts", [3 * TB, 2, D], BF16)
        resid = sb("resid", [TB, D])
        pick, eye = sb("pick", [3 * TB, TB, P], BF16), sb("eye", [P, TB, TB])
        dots, acts, wts = sb("dots", [P, TB]), sb("acts", [P, TB]), sb("wts", [P, TB])
        w_diag = sb("w_diag", [P, 2, TB, TB])
        x_out, y_out, stat, gfin = sb("x_out", [TB, D]), sb("y_out", [TB, D]), sb("y_stat", [TB, 4]), sb("gfin", [TB, D])
        qp, tp = ps("qp", [P, HALF]), ps("tp_r", [P, 4, P])
        xb, acc = ps("xb", [P, XB_SLOTS, D]), ps("y_acc", [TB, D])

        wq_landed = [sem(f"wq_landed{g}") for g in range(NG)]
        xt_landed, xt_used, keys_landed = sem("xt_landed"), sem("xt_used"), sem("keys_landed")
        keys_turned, keys_kept = sem("keys_turned"), sem("keys_kept")
        q_summed, q_kept, q_turned, qT_kept = sem("q_summed"), sem("q_kept"), sem("q_turned"), sem("qT_kept")
        scored, sc_kept = sem("scored"), sem("sc_kept")
        opt_ready, step = sem("opt_ready"), sem("step")
        exp_in, exp_done, chosen, turned, kept = (
            sem("exp_in"), sem("exp_done"), sem("chosen"), sem("turned"), sem("kept"))
        u_landed = [sem(f"u_landed{i}") for i in range(U_SLOTS)]
        v_landed = [sem(f"v_landed{i}") for i in range(V_SLOTS)]
        parts_landed = [sem(f"parts_landed{i}") for i in range(2)]
        resid_landed, gfin_landed, out_landed = sem("resid_landed"), sem("gfin_landed"), sem("out_landed")
        const_ready = sem("const_ready")
        idx_u_ready, idx_v_ready = sem("idx_u_ready"), sem("idx_v_ready")
        xb_ready, dot_done, v_free = sem("xb_ready"), sem("dot_done"), sem("v_free")
        gelu_done, w_ready, acc_read = sem("gelu_done"), sem("w_ready"), sem("acc_read")
        wts_ready, sq_done, ms_done, rt_done, rinv_ready = (
            sem("wts_ready"), sem("sq_done"), sem("ms_done"), sem("rt_done"), sem("rinv_ready"))
        y_ready, y_free = sem("y_ready"), sem("y_free")

        block = ctx.enter_context(nc.Block())
        first = lambda r: isinstance(r, int) and r == 0

        @block.gpsimd
        def _(pool):
            nc.gpsimd.iota(opt_i[:], pattern=[[1, K]], base=0, channel_multiplier=0).then_inc(opt_ready, 1)
            nc.gpsimd.memset(pick[:], 0.0).then_inc(const_ready, 1)
            nc.gpsimd.memset(eye[:], 0.0).then_inc(const_ready, 1)
            pool.wait_ge(const_ready, 2)
            for part in range(3):
                nc.gpsimd.affine_select(out=pick[:], in_=pick[:], compare_op=ALU.not_equal, fill=1.0,
                                        base=-TB * part, pattern=[[-1, TB], [0, P]],
                                        channel_multiplier=1).then_inc(const_ready, 1)
                pool.wait_ge(const_ready, 3 + part)
            nc.gpsimd.affine_select(out=eye[:], in_=eye[:], compare_op=ALU.not_equal, fill=1.0, base=0,
                                    pattern=[[1, TB], [-1, TB]], channel_multiplier=0).then_inc(const_ready, 1)
            pool.sem_inc(v_free, V_SLOTS)

            def gather_u(b, t, par):
                if t == 0:
                    pool.wait_ge(idx_u_ready, b + 1)
                if not isinstance(b, int) or TB * b + t >= U_SLOTS:
                    pool.wait_ge(dot_done, TB * b + t - U_SLOTS + 1)
                pool.sem_inc(passed, 1)
                nc.gpsimd.indirect_dma_start(
                    u_rows[:, t % U_SLOTS, :], None, expert_u,
                    bass.IndirectOffsetOnAxis(ap=idx_u[par][:, t:t + 1], axis=0)).then_inc(u_landed[t % U_SLOTS], 16)

            def gather_v(b, t, par):
                if t == 0:
                    pool.wait_ge(idx_v_ready, b + 1)
                pool.wait_ge(v_free, TB * b + t + 1)
                pool.sem_inc(passed, 1)
                nc.gpsimd.indirect_dma_start(
                    v_rows[:, t % V_SLOTS, :], None, expert_v,
                    bass.IndirectOffsetOnAxis(ap=idx_v[par][:, t:t + 1], axis=0)).then_inc(v_landed[t % V_SLOTS], 16)

            for t in range(TB):
                gather_u(0, t, 0)
            with pool.Fori(0, PT) as tile:
                for j in range(QB):
                    for t in range(TB):
                        gather_u(QB * tile + j + 1, t, (j + 1) % 2)
                        gather_v(QB * tile + j, t, j % 2)
            for t in range(TB):
                gather_v(NB - 1, t, 0)

        @block.sync
        def _(sp):
            def load_tokens(r):
                sp.dma_start(xt[:].rearrange("p k n -> p (k n)"),
                             x_turned[bass.ds(r, 1)].rearrange("a p k n -> (a p) (k n)")).then_inc(xt_landed, 16)

            def load_parts(b, par):
                for part in range(3):
                    sp.dma_start(parts[part * TB:(part + 1) * TB, par, :],
                                 x_parts[part, bass.ds(b * TB, TB), :]).then_inc(parts_landed[par], 16)

            def load_resid(b):
                sp.dma_start(resid[:], x_res[bass.ds(b * TB, TB), :]).then_inc(resid_landed, 16)

            def store(b, rows):
                sp.wait_ge(y_ready, b + 1)
                sp.dma_start(rows, y_out[:]).then_inc(out_landed, 16)
                sp.wait_ge(out_landed, 16 * b + 16)
                sp.sem_inc(y_free, 1)

            sp.sem_inc(y_free, 1)
            sp.dma_start(keys, a["sub_keys"][0].rearrange("h s n e -> n (h s) e")).then_inc(keys_landed, 16)
            load_tokens(0)
            for g in range(NG):
                cut = slice(g * HALF, (g + 1) * HALF)
                sp.dma_start(w[:, :, cut], w_view[:, :, cut]).then_inc(wq_landed[g], 16)
            sp.dma_start(gfin[:], a["g_final"].unsqueeze(0).to_broadcast((TB, D))).then_inc(gfin_landed, 16)
            load_parts(0, 0)
            load_parts(1, 1)
            load_resid(0)
            sp.wait_ge(xt_used, 1)
            load_tokens(1)

            def block_done(b, j, rows):
                sp.wait_ge(dot_done, TB * (b + 1))
                if not isinstance(b, int) or b + 2 < NB:
                    load_parts(b + 2, j % 2)
                store(b, rows)
                if not isinstance(b, int) or b + 1 < NB:
                    load_resid(b + 1)

            with sp.Fori(0, PT - 1) as tile:
                for j in range(QB):
                    if j == 2:
                        sp.wait_ge(xt_used, tile + 2)
                        load_tokens(tile + 2)
                    b = QB * tile + j
                    block_done(b, j, y_prompt[bass.ds(b * TB, TB), :])
            for b in range(QB * (PT - 1), NB - 1):
                block_done(b, b % QB, y_prompt[b * TB:(b + 1) * TB, :])
            block_done(NB - 1, 0, y_sample)

        @block.tensor
        def _(pe):
            def turn_keys(g):
                if g:
                    pe.wait_ge(keys_kept, g)
                for n in range(4):
                    last = nc.tensor.transpose(tp[:, n, :], keys[:, 4 * g + n, :], c.ident[:])
                last.then_inc(keys_turned, 1)

            def route(r, i):
                g, part = divmod(i, GSTEPS)
                if g < NG and part < KC:
                    if i == 0:
                        pe.wait_ge(xt_landed, 16 * (r + 1))
                    if first(r) and part == 0:
                        pe.wait_ge(wq_landed[g], 16)
                    if part == 0 and not (first(r) and g == 0):
                        pe.wait_ge(q_kept, NG * r + g)
                    last = nc.tensor.matmul(qp[:], xt[:, part, :], w[:, part, g * HALF:(g + 1) * HALF],
                                            start=(part == 0), stop=(part == KC - 1))
                    if part == KC - 1:
                        last.then_inc(q_summed, 1)
                        if g == NG - 1:
                            pe.wait_ge(q_summed, NG * r + g + 1)
                            pe.sem_inc(xt_used, 1)
                elif g < NG and part == KC:
                    pe.wait_ge(q_kept, NG * r + g + 1)
                    if g:
                        pe.wait_ge(sc_kept, NG * r + g)
                    elif first(r):
                        pe.wait_ge(keys_kept, NG)
                    else:
                        pe.wait_ge(kept, r)
                    for n in range(4):
                        last = nc.tensor.transpose(tp[:, n, :], q_tok[:, n * P:(n + 1) * P], c.ident[:])
                    last.then_inc(q_turned, 1)
                elif g < NG:
                    pe.wait_ge(qT_kept, NG * r + g + 1)
                    for n in range(4):
                        last = nc.tensor.matmul(tp[:, n, :], qT[:, n, :], keyT[:, 4 * g + n, :], start=True, stop=True)
                    last.then_inc(scored, 1)
                elif i == RSTEPS - 1:
                    pe.wait_ge(chosen, r + 1)
                    nc.tensor.transpose(tp[:, 0, :], share[:], c.ident[:])
                    nc.tensor.transpose(tp[:, 1, :], number[:, 2, :], c.ident[:]).then_inc(turned, 1)

            def broadcast(b, t, par, loads):
                if t == 0:
                    pe.wait_ge(parts_landed[par], 48 * loads)
                if not isinstance(b, int) or TB * b + t >= XB_SLOTS:
                    pe.wait_ge(dot_done, TB * b + t - XB_SLOTS + 1)
                for half in HALVES:
                    last = nc.tensor.matmul(xb[:, t % XB_SLOTS, half], pick[:, t, :], parts[:, par, half],
                                            start=True, stop=True)
                last.then_inc(xb_ready, 1)

            def combine(b, t, par):
                if t == 0:
                    pe.wait_ge(w_ready, b + 1)
                    pe.wait_ge(acc_read, b + 1)
                pe.wait_ge(v_landed[t % V_SLOTS], 16 * (V_USES * b + t // V_SLOTS + 1))
                for half in HALVES:
                    last = nc.tensor.matmul(acc[:, half], w_diag[:, par, t, :], v_rows[:, t % V_SLOTS, half],
                                            start=(t == 0), stop=(t == TB - 1))
                last.then_inc(v_free, 1)

            pe.wait_ge(keys_landed, 16)
            for g in range(NG):
                turn_keys(g)
            for i in range(RSTEPS):
                route(0, i)
            pe.wait_ge(const_ready, 6)
            for t in range(TB):
                broadcast(0, t, 0, 1)
            with pe.Fori(0, PT) as tile:
                for j in range(QB):
                    b = QB * tile + j
                    for t in range(TB):
                        broadcast(b + 1, t, (j + 1) % 2, 2 * tile + (j + 1) // 2 + 1)
                        combine(b, t, j % 2)
                        route(tile + 1, TB * j + t)
            for t in range(TB):
                combine(NB - 1, t, 0)

        @block.scalar
        def _(act):
            def route(r, i):
                g, part = divmod(i, GSTEPS)
                if g < NG and part == KC - 1:
                    act.wait_ge(q_summed, NG * r + g + 1)
                    if not (first(r) and g == 0):
                        act.wait_ge(q_turned, NG * r + g)
                    nc.scalar.activation(q_tok[:], qp[:], ACT.Copy).then_inc(q_kept, 1)
                elif g < NG and part == KC:
                    act.wait_ge(q_turned, NG * r + g + 1)
                    nc.scalar.activation(qT[:], tp[:], ACT.Copy).then_inc(qT_kept, 1)
                elif g < NG and part == KC + 1:
                    act.wait_ge(scored, NG * r + g + 1)
                    if g >= 2:
                        act.wait_ge(step, R_COUNT * r + V_COUNT * (g - 2) + V_FOUND)
                    elif not first(r):
                        act.wait_ge(step, R_COUNT * (r - 1) + V_COUNT * (g + 2) + V_FOUND)
                    nc.scalar.activation(sc[:, g % 2], tp[:], ACT.Copy).then_inc(sc_kept, 1)
                elif i == EXPS:
                    act.wait_ge(exp_in, r + 1)
                    nc.scalar.activation(gate[:], gate[:], ACT.Exp).then_inc(exp_done, 1)
                elif i == RSTEPS - 1:
                    act.wait_ge(turned, r + 1)
                    act.sem_inc(passed, 1)
                    nc.scalar.activation(gateT[:, cols(r)], tp[:, 0, :], ACT.Copy)
                    nc.scalar.activation(idxT[:, cols(r)], tp[:, 1, :], ACT.Copy).then_inc(kept, 1)

            def gelu(b):
                act.wait_ge(dot_done, TB * b + TB)
                nc.scalar.activation(acts[:], dots[:], ACT.Gelu_apprx_tanh).then_inc(gelu_done, 1)

            def norm(b):
                act.wait_ge(acc_read, b + 2)
                act.wait_ge(y_free, b + 1)
                nc.scalar.activation(y_out[:], x_out[:], ACT.Square, accum_out=stat[:, 0:1]).then_inc(sq_done, 1)
                act.wait_ge(ms_done, b + 1)
                nc.scalar.activation(stat[:, 2:3], stat[:, 1:2], ACT.Sqrt).then_inc(rt_done, 1)

            for g in range(NG):
                act.wait_ge(keys_turned, g + 1)
                nc.scalar.activation(keyT[:, 4 * g:4 * g + 4, :], tp[:], ACT.Copy).then_inc(keys_kept, 1)
            for i in range(RSTEPS):
                route(0, i)
            gelu(0)
            with act.Fori(0, PT) as tile:
                for j in range(QB):
                    for t in range(TB):
                        route(tile + 1, TB * j + t)
                    gelu(QB * tile + j + 1)
                    norm(QB * tile + j)
            norm(NB - 1)

        @block.vector
        def _(dve):
            done = [0]

            def group(r, g, part):
                pair = lambda x, n, lo: x[:, (4 * g + n) * K + lo:(4 * g + n) * K + lo + 8]
                head = lambda x, h, lo: x[:, (2 * g + h) * K + lo:(2 * g + h) * K + lo + 8]
                ranks = slice(2 * K * g, 2 * K * (g + 1))
                if part == 0:
                    dve.wait_ge(sc_kept, NG * r + g + 1)
                    dve.sem_inc(passed, 1)
                    for n in range(4):
                        nc.vector.max(pair(best, n, 0), sc[:, g % 2, n, :]).then_inc(step, 1)
                    return 4
                if part == 1:
                    for n in range(4):
                        nc.vector.max_index(pair(best_at, n, 0), pair(best, n, 0), sc[:, g % 2, n, :])
                        nc.vector.match_replace(rest[:, n, :], pair(best, n, 0), sc[:, g % 2, n, :], TAKEN).then_inc(step, 1)
                    return 4
                if part == 2:
                    for n in range(4):
                        nc.vector.max(pair(best, n, 8), rest[:, n, :]).then_inc(step, 1)
                    return 4
                if part == 3:
                    for n in range(4):
                        nc.vector.max_index(pair(best_at, n, 8), pair(best, n, 8), rest[:, n, :]).then_inc(step, 1)
                    return 4
                if part == 4:
                    b = best[:].rearrange("p (h s k) -> p h s k", s=2, k=K)[:, 2 * g:2 * g + 2]
                    nc.vector.tensor_tensor(cand[:].rearrange("p h (i j) -> p h i j", i=K),
                                            b[:, :, 0, :].unsqueeze(3).to_broadcast((P, 2, K, K)),
                                            b[:, :, 1, :].unsqueeze(2).to_broadcast((P, 2, K, K)), ALU.add).then_inc(step, 1)
                    return 1
                if part == 5:
                    for h in range(2):
                        nc.vector.max(head(score, h, 0), cand[:, h]).then_inc(step, 1)
                    return 2
                if part == 6:
                    for h in range(2):
                        nc.vector.max_index(head(pos, h, 0), head(score, h, 0), cand[:, h])
                        nc.vector.match_replace(left[:, h], head(score, h, 0), cand[:, h], TAKEN).then_inc(step, 1)
                    return 2
                if part == 7:
                    for h in range(2):
                        nc.vector.max(head(score, h, 8), left[:, h]).then_inc(step, 1)
                    return 2
                if part == 8:
                    for h in range(2):
                        nc.vector.max_index(head(pos, h, 8), head(score, h, 8), left[:, h]).then_inc(step, 1)
                    return 2
                if part == 9:
                    nc.vector.tensor_single_scalar(digit[:, 0], pos[:, ranks], 4, ALU.logical_shift_right).then_inc(step, 1)
                    nc.vector.tensor_single_scalar(digit[:, 1], pos[:, ranks], K - 1, ALU.bitwise_and).then_inc(step, 1)
                    return 2
                if part == 10:
                    nc.vector.tensor_copy(dig[:], digit[:]).then_inc(step, 1)
                    nc.vector.tensor_copy(at, best_at[:, 2 * ranks.start:2 * ranks.stop]).then_inc(step, 1)
                    return 2
                if part == 11:
                    nc.vector.tensor_tensor(hit[:], dig[:].unsqueeze(3).to_broadcast((P, 2, 2 * K, K)),
                                            opt[:].unsqueeze(1).unsqueeze(1).to_broadcast((P, 2, 2 * K, K)),
                                            ALU.is_equal).then_inc(step, 1)
                    return 1
                if part == 12:
                    for side in range(2):
                        h4 = hit[:, side].rearrange("p (h q) k -> p h q k", q=K)
                        av = at.rearrange("p (h s k) -> p h s k", s=2, k=K)[:, :, side, :]
                        nc.vector.tensor_tensor(h4, h4, av.unsqueeze(2).to_broadcast((P, 2, K, K)), ALU.mult).then_inc(step, 1)
                    return 2
                nc.vector.tensor_reduce(number[:, 0:2, ranks], hit[:], AX.X, ALU.add).then_inc(step, 1)
                return 1

            def end(r, part):
                sv, gv = score[:].rearrange("p (h k) -> p h k", k=K), gate[:].rearrange("p (h k) -> p h k", k=K)
                if part == 0:
                    nc.vector.tensor_tensor(gv, sv, sv[:, :, 0:1].to_broadcast((P, H, K)), ALU.subtract).then_inc(exp_in, 1)
                    if not first(r):
                        dve.wait_ge(turned, r)
                    nc.vector.scalar_tensor_tensor(out=number[:, 2], in0=number[:, 0], scalar=float(P), in1=number[:, 1],
                                                   op0=ALU.mult, op1=ALU.add).then_inc(step, 1)
                    return 1
                if part == 1:
                    dve.wait_ge(exp_done, r + 1)
                    nc.vector.tensor_reduce(total[:, 0], gv, AX.X, ALU.add).then_inc(step, 1)
                    return 1
                if part == 2:
                    nc.vector.reciprocal(total[:, 1], total[:, 0]).then_inc(step, 1)
                    return 1
                nc.vector.tensor_tensor(share[:].rearrange("p (h k) -> p h k", k=K), gv,
                                        total[:, 1].unsqueeze(2).to_broadcast((P, H, K)), ALU.mult).then_inc(chosen, 1)
                return 0

            def route(r, i):
                if i < FIND or i >= RSTEPS - 1:
                    return
                g, part = divmod(i - FIND, VSTEPS)
                if i == FIND:
                    done[0] = 0
                    if not first(r):
                        dve.wait_ge(chosen, r)
                else:
                    dve.wait_ge(step, R_COUNT * r + done[0])
                    dve.sem_inc(passed, 1)
                done[0] += group(r, g, part) if g < NG else end(r, part)
                assert g == NG or part > 3 or done[0] == V_COUNT * g + 4 * (part + 1), (g, part, done)

            def indices_u(b, par):
                nc.vector.tensor_copy(idx_u[par][:], idxT[:, bass.ds(b * TB, TB)]).then_inc(idx_u_ready, 1)

            def indices_v(b, par):
                nc.vector.tensor_copy(idx_v[par][:], idxT[:, bass.ds(b * TB, TB)]).then_inc(idx_v_ready, 1)

            def dot(b, t):
                dve.wait_ge(u_landed[t % U_SLOTS], 16 * (U_USES * b + t // U_SLOTS + 1))
                dve.wait_ge(xb_ready, TB * b + t + 1)
                nc.vector.tensor_tensor_reduce(
                    out=u_rows[:, t % U_SLOTS, :], in0=u_rows[:, t % U_SLOTS, :], in1=xb[:, t % XB_SLOTS, :],
                    scale=1.0, scalar=0.0, op0=ALU.mult, op1=ALU.add, accum_out=dots[:, t:t + 1]).then_inc(dot_done, 1)

            def weigh(b, par):
                dve.wait_ge(gelu_done, b + 1)
                nc.vector.tensor_tensor(wts[:], acts[:], gateT[:, bass.ds(b * TB, TB)], ALU.mult).then_inc(wts_ready, 1)
                dve.wait_ge(wts_ready, b + 1)
                nc.vector.tensor_tensor(w_diag[:, par], wts[:].unsqueeze(2).to_broadcast((P, TB, TB)), eye[:],
                                        ALU.mult).then_inc(w_ready, 1)

            def finish(b):
                dve.wait_ge(v_free, V_SLOTS + TB * b + TB)
                dve.wait_ge(resid_landed, 16 * (b + 1))
                nc.vector.tensor_tensor(x_out[:], acc[:], resid[:], ALU.add).then_inc(acc_read, 1)
                dve.wait_ge(sq_done, b + 1)
                nc.vector.tensor_scalar(stat[:, 1:2], stat[:, 0:1], 1.0 / D, EPS, ALU.mult, ALU.add).then_inc(ms_done, 1)
                dve.wait_ge(rt_done, b + 1)
                nc.vector.reciprocal(stat[:, 3:4], stat[:, 2:3]).then_inc(rinv_ready, 1)
                dve.wait_ge(rinv_ready, b + 1)
                nc.vector.scalar_tensor_tensor(out=y_out[:], in0=x_out[:], scalar=stat[:, 3:4], in1=gfin[:],
                                               op0=ALU.mult, op1=ALU.mult).then_inc(y_ready, 1)
                dve.wait_ge(y_ready, b + 1)
                dve.sem_inc(passed, 1)

            dve.sem_inc(acc_read, 1)
            dve.wait_ge(opt_ready, 1)
            nc.vector.tensor_copy(opt[:], opt_i[:])
            for i in range(RSTEPS):
                route(0, i)
            dve.wait_ge(const_ready, 6)
            dve.wait_ge(gfin_landed, 16)
            dve.wait_ge(kept, 1)
            indices_u(0, 0)
            indices_u(1, 1)
            indices_v(0, 0)
            for t in range(TB):
                dot(0, t)
            weigh(0, 0)
            with dve.Fori(0, PT) as tile:
                for j in range(QB):
                    b = QB * tile + j
                    indices_v(b + 1, (j + 1) % 2)
                    for t in range(TB):
                        dot(b + 1, t)
                        route(tile + 1, TB * j + t)
                        if t == TURN:
                            if j == 2:
                                dve.wait_ge(kept, tile + 2)
                                dve.sem_inc(passed, 1)
                            indices_u(b + 2, j % 2)
                    weigh(b + 1, (j + 1) % 2)
                    finish(b)
            finish(NB - 1)


class Consts:
    OLD = (PAST - HALF) // 16
    SK = HALF + DT * OLD


def program(nc, a):
    c = Consts()
    with ExitStack() as ctx:
        s = Shop(nc, ctx, "program")
        c.ident, c.ones = s.sb("ident", [P, P]), s.sb("ones", [P, P])
        c.par, c.coef = s.sb("par", [P, CC, N_ROWS]), s.sb("coef", [P, 2, CC])
        c.g_mix, c.g_ffn = s.sb("g_mix_T", [P, KC]), s.sb("g_ffn_T", [P, KC])
        x_res = nc.dram_tensor("x_res", (NTOK, D), F32, kind="Internal").ap()
        x_parts = nc.dram_tensor("x_parts", (3, NTOK, D), BF16, kind="Internal").ap()
        x_turned = nc.dram_tensor("x_turned", (PT + 1, P, KC, P), F32, kind="Internal").ap()
        with ExitStack() as ctx2:
            s2 = Shop(nc, ctx2, "program")
            xT = s2.sb("xT", [P, KC, NTOK])
            c.mult, c.bias = s2.sb("mult", [P, SEQ]), s2.sb("bias", [P, SEQ])
            c.s_mult, c.s_bias = s2.sb("s_mult", [NS, 2, c.SK + NS]), s2.sb("s_bias", [NS, 2, c.SK + NS])
            c.n_mult, c.n_bias = s2.sb("n_mult", [NS, DB, NS]), s2.sb("n_bias", [NS, DB, NS])
            zT, v_tok = s2.sb("zT", [P, 4 * CC, NTOK]), s2.sb("v_tok", [P, PT + 1, DR])
            with ExitStack() as ctx3:
                s3 = Shop(nc, ctx3, "program")
                c.wgate = s3.sb("wgate", [P, 2, CC, P])
                c.w1, c.w2, c.w3 = (s3.sb(x, [P, CC]) for x in ("w1", "w2", "w3"))
                constants(nc, a, c)
                normed_T(nc, a, c, xT)
                project(nc, a, c, xT, zT, v_tok)
            yaT = s2.sb("yaT", [P, CC, NTOK])
            attend_prompt(nc, a, c, zT, v_tok, yaT)
            w_early = v_tok[:, 0:PT, :].rearrange("p (j two) e -> p j (two e)", j=CC)
            early_landed = s2.sem("early_landed")
            attend_sample(nc, a, c, zT, v_tok, yaT, xT, w_early, early_landed)
            merge(nc, a, c, zT, yaT, xT, w_early, early_landed, x_res, x_parts, x_turned)
        expert_stage(nc, a, c, x_parts, x_res, x_turned)


_OUTS = [((1, SEQ, D), 'y_prompt'), ((DB, DT, D), 'y_sample'),
         ((1, 1, SEQ, HEADS, HD), 'k_prompt'), ((1, 1, SEQ, HEADS, HD), 'v_prompt'),
         ((1, DB, DT, HEADS, HD), 'k_sample'), ((1, DB, DT, HEADS, HD), 'v_sample'),
         ((1, 1, CW - 1, DR), 'conv_prompt'), ((1, DB, CW - 1, DR), 'conv_sample'),
         ((1, 1, DR), 'h_prompt'), ((1, DB, DR), 'h_sample')]


def rows_of(ap):
    n = len(ap.shape)
    if n == 5:
        return ap.rearrange("a b t h e -> (a b t) (h e)")
    if n == 4:
        return ap.rearrange("a b t e -> (a b t) e")
    return ap.rearrange("a b e -> (a b) e")


def kernel(**inputs):
    import numpy as _np
    import concourse.bacc as _bacc
    from concourse.bass_utils import run_bass_kernel_spmd as _run

    nc = _bacc.Bacc("TRN2", target_bir_lowering=False, num_devices=1)
    arrays, a = {}, {}
    for name, x in inputs.items():
        arrays[name] = _np.ascontiguousarray(x)
        a[name] = nc.dram_tensor(name, arrays[name].shape, mybir.dt.from_np(arrays[name].dtype), kind="ExternalInput").ap()
    for shape, name in _OUTS:
        a[name] = rows_of(nc.dram_tensor("out_" + name, shape, F32, kind="ExternalOutput").ap())
    program(nc, a)
    r = _run(nc, [arrays], core_ids=[0])
    return tuple(r.results[0]["out_" + name] for _, name in _OUTS)
```
